# Optimizing a Trainium2 kernel written in Bass

```python
import math
import jax, jax.numpy as jnp
from jax import lax
import numpy as np

D_MODEL = 2048
BATCH = 1
SEQ = 256
DEPTH = 1
DEC_BATCH = 8
DEC_SEQ = 8
PAST_LEN = 1024
PAGE_SIZE = 128

N_HEADS = 16
HEAD_DIM = 64
KV_HEADS = 4
NSA_WIDTH = N_HEADS * HEAD_DIM
KV_WIDTH = KV_HEADS * HEAD_DIM
ROT_DIM = HEAD_DIM // 4
ROPE_THETA = 500000.0
L_CMP = 32
STRIDE = 16
CMP_R = L_CMP // STRIDE
CMP_HIDDEN = 128
L_SEL = 64
SEL_RATIO = L_SEL // STRIDE
SEL_INNER = (L_SEL - L_CMP) // STRIDE + 1
TOP_N = 16
WINDOW = 512
WIN_QB = 128
SEL_QB = 32
SGU_WIDTH = D_MODEL // 2
SGU_GROUPS = 8
SGU_GROUP_DIM = SGU_WIDTH // SGU_GROUPS
CHUNK = 128
MIX_WIDTH = NSA_WIDTH + SGU_WIDTH
IN_COLS = NSA_WIDTH + 6 * KV_WIDTH + 3 * N_HEADS + 2 * SGU_WIDTH
N_MEM = 256
MEM_HEADS = 4
MEM_HEAD_DIM = 128
MEM_WIDTH = MEM_HEADS * MEM_HEAD_DIM
N_GROUPS = 4
EXPERTS_PER_GROUP = 4
N_EXPERTS = N_GROUPS * EXPERTS_PER_GROUP
TOP_K_IN_GROUP = 2
EXPERT_FF = 512
EPS = 1e-6
NEG_INF = -1e30
BIG = 1e9
STATE_NAMES = ('cmp_k_p', 'cmp_v_p', 'sel_k_p', 'sel_v_p', 'win_k_p', 'win_v_p', 'mem_k_p', 'mem_v_p', 'cmp_k_s', 'cmp_v_s', 'sel_k_s', 'sel_v_s', 'win_k_s', 'win_v_s', 'sgu_v_s')

kernel_name = 'nsa_gmlp_hybrid_step'

def rmsnorm(x, g):
    xf = x.astype(jnp.float32)
    y = xf * lax.rsqrt(jnp.mean(xf * xf, axis=-1, keepdims=True) + EPS)
    return (y * g.astype(jnp.float32)).astype(x.dtype)

def partial_rope(x, pos):
    half = ROT_DIM // 2
    freqs = ROPE_THETA ** (-jnp.arange(half, dtype=jnp.float32) / half)
    ang = pos.astype(jnp.float32)[:, None] * freqs[None, :]
    cos = jnp.cos(ang)[None, :, None, :]
    sin = jnp.sin(ang)[None, :, None, :]
    xf = x.astype(jnp.float32)
    x1, x2 = xf[..., :half], xf[..., half:ROT_DIM]
    rot = jnp.concatenate([x1 * cos - x2 * sin, x2 * cos + x1 * sin], axis=-1).astype(x.dtype)
    return jnp.concatenate([rot, x[..., ROT_DIM:]], axis=-1)

def masked_softmax(s, mask):
    s = jnp.where(mask, s, NEG_INF)
    m = jnp.max(s, axis=-1, keepdims=True)
    e = jnp.where(mask, jnp.exp(s - m), 0.0)
    return e / jnp.maximum(jnp.sum(e, axis=-1, keepdims=True), 1e-30)

def gqa_attend(q, k, v, mask):
    n, tq, h, d = q.shape
    g = k.shape[2]
    qg = q.reshape(n, tq, g, h // g, d)
    s = jnp.einsum('ntgqd,nkgd->ngqtk', qg, k).astype(jnp.float32) * (d ** -0.5)
    p = masked_softmax(s, mask)
    o = jnp.einsum('ngqtk,nkgd->ntgqd', p.astype(v.dtype), v)
    return o.reshape(n, tq, h, d), p

def compress(raw, pe, w1, w2):
    b, t, g, d = raw.shape
    n_sub = t // STRIDE
    nc = n_sub - CMP_R + 1
    sub = raw[:, :n_sub * STRIDE].reshape(b, n_sub, STRIDE, g, d)
    w1r = w1.reshape(CMP_R, STRIDE, d, CMP_HIDDEN)
    part = jnp.einsum('bnsgd,rsdh->brngh', sub, w1r)
    part = part + jnp.einsum('rsd,rsdh->rh', pe.reshape(CMP_R, STRIDE, d), w1r)[None, :, None, None, :]
    hsum = part[:, 0, 0:nc]
    for r in range(1, CMP_R):
        hsum = hsum + part[:, r, r:r + nc]
    return jax.nn.silu(hsum) @ w2

def cmp_branch(q, kc, vc, q_pos):
    nc = kc.shape[1]
    end = jnp.arange(nc) * STRIDE + (L_CMP - 1)
    mask = (end[None, :] <= q_pos[:, None])[None, None, None]
    return gqa_attend(q, kc, vc, mask)

def select_blocks(p, q_pos, n_keys):
    b, g, qg, tq, nc = p.shape
    ns = -(-n_keys // L_SEL)
    pg = jnp.sum(p, axis=2)
    pg = jnp.pad(pg, ((0, 0), (0, 0), (0, 0), (0, ns * SEL_RATIO - nc)))
    ps = pg.reshape(b, g, tq, ns, SEL_RATIO)[..., :SEL_INNER].sum(-1)
    blk = jnp.arange(ns)[None, :]
    cur = (q_pos // L_SEL)[:, None]
    forced = (blk == 0) | (blk == cur) | (blk == cur - 1)
    future = blk * L_SEL > q_pos[:, None]
    score = jnp.where(forced, BIG, jnp.where(future, -BIG, ps))
    _, idx = lax.top_k(score, min(TOP_N, ns))
    return idx

def to_blocks(k, ns):
    b, t, g, d = k.shape
    k = jnp.pad(k, ((0, 0), (0, ns * L_SEL - t), (0, 0), (0, 0)))
    return k.reshape(b, ns, L_SEL, g, d).transpose(0, 3, 1, 2, 4)

def sel_branch(q_rot, kb, vb, idx, q_pos):
    b, tq, h, d = q_rot.shape
    g = kb.shape[1]
    n = idx.shape[-1]
    bi = jnp.arange(b)[:, None, None, None]
    gi = jnp.arange(g)[None, :, None, None]
    ksel = kb[bi, gi, idx].reshape(b, g, tq, n * L_SEL, d)
    vsel = vb[bi, gi, idx].reshape(b, g, tq, n * L_SEL, d)
    kpos = (idx[..., None] * L_SEL + jnp.arange(L_SEL)).reshape(b, g, tq, n * L_SEL)
    mask = (kpos <= q_pos[None, None, :, None])[:, :, None]
    qg = q_rot.reshape(b, tq, g, h // g, d)
    s = jnp.einsum('btgqd,bgtkd->bgqtk', qg, ksel).astype(jnp.float32) * (d ** -0.5)
    p = masked_softmax(s, mask)
    o = jnp.einsum('bgqtk,bgtkd->btgqd', p.astype(vsel.dtype), vsel)
    return o.reshape(b, tq, h, d)

def sel_attend_blocked(q_rot, kb, vb, idx, q_pos):
    b, tq, h, d = q_rot.shape
    g, n = idx.shape[1], idx.shape[-1]
    qb = SEL_QB if (tq > SEL_QB and tq % SEL_QB == 0) else tq
    nq = tq // qb
    qs = q_rot.reshape(b, nq, qb, h, d).transpose(1, 0, 2, 3, 4)
    ids = idx.reshape(b, g, nq, qb, n).transpose(2, 0, 1, 3, 4)
    pss = q_pos.reshape(nq, qb)
    o = lax.map(lambda a: sel_branch(a[0], kb, vb, a[1], a[2]), (qs, ids, pss))
    return o.transpose(1, 0, 2, 3, 4).reshape(b, tq, h, d)

def window_mask(q_pos, k_pos):
    qp = q_pos[..., :, None]
    kp = k_pos[..., None, :]
    return (kp <= qp) & (kp > qp - WINDOW) & (kp >= 0)

def win_banded(q_rot, kw, vw):
    b, t, h, d = q_rot.shape
    g = kw.shape[2]
    qb = min(WIN_QB, t)
    nb = t // qb
    wk = WINDOW + qb
    pad = ((0, 0), (WINDOW, 0), (0, 0), (0, 0))
    idx = jnp.arange(nb)[:, None] * qb + jnp.arange(wk)[None, :]
    kblk = jnp.pad(kw, pad)[:, idx].reshape(b * nb, wk, g, d)
    vblk = jnp.pad(vw, pad)[:, idx].reshape(b * nb, wk, g, d)
    mask = window_mask(jnp.arange(t).reshape(nb, qb), idx - WINDOW)
    mask = jnp.broadcast_to(mask[None], (b, nb, qb, wk)).reshape(b * nb, 1, 1, qb, wk)
    o, _ = gqa_attend(q_rot.reshape(b * nb, qb, h, d), kblk, vblk, mask)
    return o.reshape(b, t, h, d)

def win_cached(q_rot, buf_k, buf_v, kw, vw, q_pos, past_len):
    wb = buf_k.shape[1]
    k_all = jnp.concatenate([buf_k, kw], axis=1)
    v_all = jnp.concatenate([buf_v, vw], axis=1)
    k_pos = past_len - wb + jnp.arange(wb + kw.shape[1])
    mask = window_mask(q_pos, k_pos)[None, None, None]
    o, _ = gqa_attend(q_rot, k_all, v_all, mask)
    return o

def gather_pages(pool, page_table):
    b, n = page_table.shape
    rows = pool[page_table]
    return rows.reshape(b, n * pool.shape[1], pool.shape[2], pool.shape[3])

def sgu(u, v, w_s, b_s):
    b, t, _ = u.shape
    c = min(t, CHUNK)
    n = t // c
    tri = jnp.tril(jnp.ones((c, c), dtype=w_s.dtype))
    ws = w_s[:, :c, :c] * tri[None]
    vr = v.reshape(b, n, c, SGU_GROUPS, SGU_GROUP_DIM)
    mixed = jnp.einsum('gts,bnsgd->bntgd', ws, vr) + b_s[:, :c].T[None, None, :, :, None]
    return u * mixed.reshape(b, t, SGU_WIDTH)

def project(h, lw, q_pos):
    b, t, _ = h.shape
    z = h @ lw['w_in']
    sizes = (NSA_WIDTH, KV_WIDTH, KV_WIDTH, KV_WIDTH, KV_WIDTH, KV_WIDTH, KV_WIDTH, 3 * N_HEADS, SGU_WIDTH, SGU_WIDTH)
    parts = []
    off = 0
    for s in sizes:
        parts.append(z[..., off:off + s])
        off += s
    q, kc, vc, ks, vs, kw, vw, gt, u, v = parts
    heads = lambda a, nh: a.reshape(b, t, nh, HEAD_DIM)
    q = heads(q, N_HEADS)
    kc, vc, vs, vw = heads(kc, KV_HEADS), heads(vc, KV_HEADS), heads(vs, KV_HEADS), heads(vw, KV_HEADS)
    q_rot = partial_rope(q, q_pos)
    ks = partial_rope(heads(ks, KV_HEADS), q_pos)
    kw = partial_rope(heads(kw, KV_HEADS), q_pos)
    gates = jax.nn.sigmoid(gt.astype(jnp.float32)).reshape(b, t, N_HEADS, 3).astype(h.dtype)
    u = jax.nn.gelu(u)
    v = rmsnorm(jax.nn.gelu(v), lw['g_sgu_v'])
    return q, q_rot, kc, vc, ks, vs, kw, vw, gates, u, v

def nsa_cmp_sel(q, q_rot, kc_all, vc_all, ks_all, vs_all, q_pos, lw):
    kc = compress(kc_all, lw['pe_cmp_k'], lw['w_cmp_k1'], lw['w_cmp_k2'])
    vc = compress(vc_all, lw['pe_cmp_v'], lw['w_cmp_v1'], lw['w_cmp_v2'])
    o_cmp, p_cmp = cmp_branch(q, kc, vc, q_pos)
    n_keys = ks_all.shape[1]
    ns = -(-n_keys // L_SEL)
    idx = select_blocks(p_cmp, q_pos, n_keys)
    o_sel = sel_attend_blocked(q_rot, to_blocks(ks_all, ns), to_blocks(vs_all, ns), idx, q_pos)
    return o_cmp, o_sel

def memory_kv(mem, lw):
    b, m, _ = mem.shape
    mn = rmsnorm(mem, lw['g_mem_src'])
    mk = (mn @ lw['w_mem_k']).reshape(b, m, MEM_HEADS, MEM_HEAD_DIM)
    mv = (mn @ lw['w_mem_v']).reshape(b, m, MEM_HEADS, MEM_HEAD_DIM)
    return mk, mv

def hier_moe(h, w_rg, w_re, w_gate, w_up, w_down):
    b, t, dm = h.shape
    xf = h.reshape(b * t, dm)
    pg = jax.nn.softmax((xf @ w_rg).astype(jnp.float32), axis=-1)
    g_top = jnp.argmax(pg, axis=-1)
    pg_top = jnp.max(pg, axis=-1)
    fl = (xf @ w_re).astype(jnp.float32).reshape(-1, N_GROUPS, EXPERTS_PER_GROUP)
    fl = jnp.take_along_axis(fl, g_top[:, None, None], axis=1)[:, 0]
    pf = jax.nn.softmax(fl, axis=-1)
    top_p, top_i = lax.top_k(pf, TOP_K_IN_GROUP)
    wts = top_p / jnp.sum(top_p, axis=-1, keepdims=True) * pg_top[:, None]
    eid = g_top[:, None] * EXPERTS_PER_GROUP + top_i
    comb = jnp.sum(jax.nn.one_hot(eid, N_EXPERTS, dtype=jnp.float32) * wts[..., None], axis=1)
    act = jax.nn.silu(jnp.einsum('nd,edf->nef', xf, w_gate)) * jnp.einsum('nd,edf->nef', xf, w_up)
    act = act * comb.astype(act.dtype)[..., None]
    return jnp.einsum('nef,efd->nd', act, w_down).reshape(b, t, dm)

def finish_layer(x, o_cmp, o_sel, o_win, gates, u, v, mem_k, mem_v, lw):
    b, t, _ = x.shape
    o_nsa = gates[..., 0:1] * o_cmp + gates[..., 1:2] * o_sel + gates[..., 2:3] * o_win
    o_nsa = rmsnorm(o_nsa.reshape(b, t, NSA_WIDTH), lw['g_nsa_out'])
    o_sgu = rmsnorm(sgu(u, v, lw['w_sgu'], lw['b_sgu']), lw['g_sgu_out'])
    x = x + jnp.concatenate([o_nsa, o_sgu], axis=-1) @ lw['w_out']
    hq = (rmsnorm(x, lw['g_mem_norm']) @ lw['w_mem_q']).reshape(b, t, MEM_HEADS, MEM_HEAD_DIM)
    o_m, _ = gqa_attend(hq, mem_k, mem_v, jnp.ones((1, 1, 1, 1, 1), dtype=bool))
    x = x + o_m.reshape(b, t, MEM_WIDTH) @ lw['w_mem_o']
    x = x + hier_moe(rmsnorm(x, lw['g_moe_norm']), lw['w_router_group'], lw['w_router_expert'], lw['w_exp_gate'], lw['w_exp_up'], lw['w_exp_down'])
    return x

def setup_inputs(seed: int = 0) -> dict:
    key = jax.random.key(seed)
    keys = iter(jax.random.split(key, 64))

    def nrm(shape, scale):
        return scale * jax.random.normal(next(keys), shape, jnp.float32)

    def gain(shape):
        return 1.0 + nrm(shape, 0.02)

    n_pages = PAST_LEN // PAGE_SIZE
    n_used = DEC_BATCH * n_pages
    n_pool = n_used + max(1, n_used // 4)
    wb = min(WINDOW, PAST_LEN)
    pool = (DEPTH, n_pool, PAGE_SIZE, KV_HEADS, HEAD_DIM)
    win = (DEPTH, DEC_BATCH, wb, KV_HEADS, HEAD_DIM)
    memc = (DEPTH, DEC_BATCH, N_MEM, MEM_HEADS, MEM_HEAD_DIM)
    page_table = jax.random.permutation(next(keys), n_pool)[:n_used].reshape(DEC_BATCH, n_pages).astype(jnp.int32)
    return {
        'x_prompt': nrm((BATCH, SEQ, D_MODEL), 1.0),
        'x_sample': nrm((DEC_BATCH, DEC_SEQ, D_MODEL), 1.0),
        'cache_cmp_k': nrm(pool, 1.0),
        'cache_cmp_v': nrm(pool, 1.0),
        'cache_sel_k': nrm(pool, 1.0),
        'cache_sel_v': nrm(pool, 1.0),
        'cache_win_k': nrm(win, 1.0),
        'cache_win_v': nrm(win, 1.0),
        'cache_mem_k': nrm(memc, 1.0),
        'cache_mem_v': nrm(memc, 1.0),
        'page_table': page_table,
        'mem_prompt': nrm((BATCH, N_MEM, D_MODEL), 1.0),
        'w_in': nrm((DEPTH, D_MODEL, IN_COLS), D_MODEL ** -0.5),
        'g_attn_norm': gain((DEPTH, D_MODEL)),
        'pe_cmp_k': nrm((DEPTH, L_CMP, HEAD_DIM), 0.1),
        'w_cmp_k1': nrm((DEPTH, L_CMP * HEAD_DIM, CMP_HIDDEN), (L_CMP * HEAD_DIM) ** -0.5),
        'w_cmp_k2': nrm((DEPTH, CMP_HIDDEN, HEAD_DIM), CMP_HIDDEN ** -0.5),
        'pe_cmp_v': nrm((DEPTH, L_CMP, HEAD_DIM), 0.1),
        'w_cmp_v1': nrm((DEPTH, L_CMP * HEAD_DIM, CMP_HIDDEN), (L_CMP * HEAD_DIM) ** -0.5),
        'w_cmp_v2': nrm((DEPTH, CMP_HIDDEN, HEAD_DIM), CMP_HIDDEN ** -0.5),
        'g_sgu_v': gain((DEPTH, SGU_WIDTH)),
        'w_sgu': nrm((DEPTH, SGU_GROUPS, CHUNK, CHUNK), CHUNK ** -0.5),
        'b_sgu': gain((DEPTH, SGU_GROUPS, CHUNK)),
        'g_nsa_out': gain((DEPTH, NSA_WIDTH)),
        'g_sgu_out': gain((DEPTH, SGU_WIDTH)),
        'w_out': nrm((DEPTH, MIX_WIDTH, D_MODEL), MIX_WIDTH ** -0.5),
        'g_mem_norm': gain((DEPTH, D_MODEL)),
        'g_mem_src': gain((DEPTH, D_MODEL)),
        'w_mem_q': nrm((DEPTH, D_MODEL, MEM_WIDTH), D_MODEL ** -0.5),
        'w_mem_k': nrm((DEPTH, D_MODEL, MEM_WIDTH), D_MODEL ** -0.5),
        'w_mem_v': nrm((DEPTH, D_MODEL, MEM_WIDTH), D_MODEL ** -0.5),
        'w_mem_o': nrm((DEPTH, MEM_WIDTH, D_MODEL), MEM_WIDTH ** -0.5),
        'g_moe_norm': gain((DEPTH, D_MODEL)),
        'w_router_group': nrm((DEPTH, D_MODEL, N_GROUPS), D_MODEL ** -0.5),
        'w_router_expert': nrm((DEPTH, D_MODEL, N_EXPERTS), D_MODEL ** -0.5),
        'w_exp_gate': nrm((DEPTH, N_EXPERTS, D_MODEL, EXPERT_FF), D_MODEL ** -0.5),
        'w_exp_up': nrm((DEPTH, N_EXPERTS, D_MODEL, EXPERT_FF), D_MODEL ** -0.5),
        'w_exp_down': nrm((DEPTH, N_EXPERTS, EXPERT_FF, D_MODEL), EXPERT_FF ** -0.5),
        'g_final': gain((D_MODEL,)),
    }

def reference(x_prompt, x_sample, cache_cmp_k, cache_cmp_v, cache_sel_k, cache_sel_v, cache_win_k, cache_win_v, cache_mem_k, cache_mem_v, page_table, mem_prompt, w_in, g_attn_norm, pe_cmp_k, w_cmp_k1, w_cmp_k2, pe_cmp_v, w_cmp_v1, w_cmp_v2, g_sgu_v, w_sgu, b_sgu, g_nsa_out, g_sgu_out, w_out, g_mem_norm, g_mem_src, w_mem_q, w_mem_k, w_mem_v, w_mem_o, g_moe_norm, w_router_group, w_router_expert, w_exp_gate, w_exp_up, w_exp_down, g_final):
    past_len = page_table.shape[1] * PAGE_SIZE
    pos_p = jnp.arange(x_prompt.shape[1], dtype=jnp.int32)
    pos_s = past_len + jnp.arange(x_sample.shape[1], dtype=jnp.int32)
    xp, xs = x_prompt, x_sample
    out = {name: [] for name in STATE_NAMES}
    for l in range(DEPTH):
        lw = {
            'w_in': w_in[l], 'g_attn_norm': g_attn_norm[l],
            'pe_cmp_k': pe_cmp_k[l], 'w_cmp_k1': w_cmp_k1[l], 'w_cmp_k2': w_cmp_k2[l],
            'pe_cmp_v': pe_cmp_v[l], 'w_cmp_v1': w_cmp_v1[l], 'w_cmp_v2': w_cmp_v2[l],
            'g_sgu_v': g_sgu_v[l], 'w_sgu': w_sgu[l], 'b_sgu': b_sgu[l],
            'g_nsa_out': g_nsa_out[l], 'g_sgu_out': g_sgu_out[l], 'w_out': w_out[l],
            'g_mem_norm': g_mem_norm[l], 'g_mem_src': g_mem_src[l],
            'w_mem_q': w_mem_q[l], 'w_mem_k': w_mem_k[l], 'w_mem_v': w_mem_v[l], 'w_mem_o': w_mem_o[l],
            'g_moe_norm': g_moe_norm[l], 'w_router_group': w_router_group[l], 'w_router_expert': w_router_expert[l],
            'w_exp_gate': w_exp_gate[l], 'w_exp_up': w_exp_up[l], 'w_exp_down': w_exp_down[l],
        }
        hp = rmsnorm(xp, lw['g_attn_norm'])
        q, q_rot, kc, vc, ks, vs, kw, vw, gates, u, v = project(hp, lw, pos_p)
        o_cmp, o_sel = nsa_cmp_sel(q, q_rot, kc, vc, ks, vs, pos_p, lw)
        o_win = win_banded(q_rot, kw, vw)
        mk, mv = memory_kv(mem_prompt, lw)
        xp = finish_layer(xp, o_cmp, o_sel, o_win, gates, u, v, mk, mv, lw)
        wbp = min(WINDOW, xp.shape[1])
        out['cmp_k_p'].append(kc)
        out['cmp_v_p'].append(vc)
        out['sel_k_p'].append(ks)
        out['sel_v_p'].append(vs)
        out['win_k_p'].append(kw[:, -wbp:])
        out['win_v_p'].append(vw[:, -wbp:])
        out['mem_k_p'].append(mk)
        out['mem_v_p'].append(mv)
        hs = rmsnorm(xs, lw['g_attn_norm'])
        q, q_rot, kc, vc, ks, vs, kw, vw, gates, u, v = project(hs, lw, pos_s)
        kc_all = jnp.concatenate([gather_pages(cache_cmp_k[l], page_table), kc], axis=1)
        vc_all = jnp.concatenate([gather_pages(cache_cmp_v[l], page_table), vc], axis=1)
        ks_all = jnp.concatenate([gather_pages(cache_sel_k[l], page_table), ks], axis=1)
        vs_all = jnp.concatenate([gather_pages(cache_sel_v[l], page_table), vs], axis=1)
        o_cmp, o_sel = nsa_cmp_sel(q, q_rot, kc_all, vc_all, ks_all, vs_all, pos_s, lw)
        o_win = win_cached(q_rot, cache_win_k[l], cache_win_v[l], kw, vw, pos_s, past_len)
        xs = finish_layer(xs, o_cmp, o_sel, o_win, gates, u, v, cache_mem_k[l], cache_mem_v[l], lw)
        wb = cache_win_k.shape[2]
        out['cmp_k_s'].append(kc)
        out['cmp_v_s'].append(vc)
        out['sel_k_s'].append(ks)
        out['sel_v_s'].append(vs)
        out['win_k_s'].append(jnp.concatenate([cache_win_k[l], kw], axis=1)[:, -wb:])
        out['win_v_s'].append(jnp.concatenate([cache_win_v[l], vw], axis=1)[:, -wb:])
        out['sgu_v_s'].append(v)
    y_prompt = rmsnorm(xp, g_final)
    y_sample = rmsnorm(xs, g_final)
    return (y_prompt, y_sample, jnp.stack(out['cmp_k_p']), jnp.stack(out['cmp_v_p']), jnp.stack(out['sel_k_p']), jnp.stack(out['sel_v_p']), jnp.stack(out['win_k_p']), jnp.stack(out['win_v_p']), jnp.stack(out['mem_k_p']), jnp.stack(out['mem_v_p']), jnp.stack(out['cmp_k_s']), jnp.stack(out['cmp_v_s']), jnp.stack(out['sel_k_s']), jnp.stack(out['sel_v_s']), jnp.stack(out['win_k_s']), jnp.stack(out['win_v_s']), jnp.stack(out['sgu_v_s']))


_drawn_inputs = setup_inputs


def setup_inputs(seed=0):
    import zlib

    import numpy as np

    out = dict(_drawn_inputs(seed))
    spreads = {}
    factors = {'pe_cmp_k': 4.355,
     'g_sgu_v': 2.952,
     'b_sgu': 3.073,
     'g_nsa_out': 3.124,
     'g_sgu_out': 3.516,
     'g_mem_norm': 8.0,
     'g_mem_src': 2.824,
     'g_moe_norm': 2.671,
     'g_final': 2.834}
    for name, (base, spread) in spreads.items():
        noise = np.random.default_rng([zlib.crc32(name.encode()), seed]).standard_normal(out[name].shape)
        drawn = base * np.exp(spread * noise) if base else spread * noise
        out[name] = __import__('jax').numpy.asarray(drawn.astype(out[name].dtype))
    for name, factor in factors.items():
        out[name] = (out[name] * factor).astype(out[name].dtype)
    return out
```

```python
from contextlib import ExitStack, contextmanager

import concourse.bass as bass
import numpy as np
from concourse import mybir

F32 = mybir.dt.float32
I32 = mybir.dt.int32
ALU = mybir.AluOpType
ACT = mybir.ActivationFunctionType
AX = mybir.AxisListType.X

D = 2048
P = 128
KC = D // P
SEQ = 256
NB = 8
NT = 8
NS = NB * NT
PAST = 1024
PAGE = 128
NPG = PAST // PAGE
NH = 16
HD = 64
NG = 4
NJ = NH // NG
KVW = NG * HD
ROT = 16
STRIDE = 16
CH = 128
NSUB = PAST // STRIDE
NCS = NSUB - 1
NSUBP = SEQ // STRIDE
NCP = NSUBP - 1
LSEL = 64
NBLK = PAST // LSEL
WIN = 512
SW = 1024
SG = 8
IN_COLS = 4656
NMEM = 256
MH = 4
MD = 128
MW = MH * MD
NE = 16
FF = 512
EPS = 1e-6
NEG = -1e30
SCALE = HD ** -0.5
MSCALE = MD ** -0.5
C_Q, C_KC, C_VC, C_KS, C_VS, C_KW, C_VW, C_G, C_U, C_V = 0, 1024, 1280, 1536, 1792, 2048, 2304, 2560, 2608, 3632
TILES = 3


def shape_constants():
    p = np.arange(P)
    rows = np.zeros((TILES, P))
    rows[0], rows[1] = p, P + p
    rows[2] = PAST + p % NT
    freqs = np.float32(500000.0) ** (-np.arange(ROT // 2, dtype=np.float32) / np.float32(ROT // 2))
    ang = rows.astype(np.float32)[:, :, None] * freqs[None, None, :].astype(np.float32)
    cos, sin = np.cos(ang), np.sin(ang)
    t = p % NT
    key = np.arange(SEQ)
    end = np.arange(16) * STRIDE + 31
    q = np.stack([p, P + p], 1)
    bt = np.arange(NS)
    parts = {
        "ident": np.eye(P),
        "causal": np.where(key[None, None, :] <= q[:, :, None], 0.0, NEG),
        "cmp_add": np.where(end[None, None, :NCP] <= q[:, :, None], 0.0, NEG),
        "cmp_mul": np.where(end[None, None, :NCP] <= q[:, :, None], 1.0, 0.0),
        "win_add": np.where(np.arange(WIN)[None, :] > t[:, None], 0.0, NEG),
        "new_add": np.where((bt[None, None, :] // NT == np.arange(NB)[None, :, None])
                            & (bt[None, None, :] % NT <= t[:, None, None]), 0.0, NEG),
        "group": np.where((p[:, None] // 32 == p[None, :] // 32) & (p[:, None] % NT == p[None, :] % NT), 1.0, 0.0),
        "block_id": np.tile(np.arange(NBLK), (P, 1)),
        "cos2": np.concatenate([cos, cos], -1).transpose(1, 0, 2),
        "sin2": np.concatenate([-sin, sin], -1).transpose(1, 0, 2),
        "tri": np.where(p[:, None] <= p[None, :], 1.0, 0.0),
        "tri_strict": np.where(p[:, None] < p[None, :], 1.0, 0.0),
        "ones": np.ones((P, P)),
        "rep": np.where(p[:, None] == bt[None, :] % NT, 1.0, 0.0),
        "same_b": np.where((p[:, None, None] // NT == np.arange(NB)[None, :, None])
                           & (p[:, None, None] % NT <= np.arange(NT)[None, None, :]), 1.0, 0.0),
        "valid": np.stack([np.ones(P), np.ones(P), (p < NS) * 1.0], 1),
        "token": np.stack([p, P + p, 2 * P + p], 1),
        "first": np.tile(4.0 - np.arange(4), (P, 1)),
        "slot0": np.tile(np.arange(NE) * float(P), (P, 1)),
    }
    at, off = {}, 0
    for k, v in parts.items():
        v = v.reshape(P, -1)
        at[k] = (off, v.shape[1])
        off += v.shape[1]
    return np.concatenate([v.reshape(P, -1) for v in parts.values()], 1).astype(np.float32), at


class Steps:

    def __init__(self, sem):
        self.sem, self.n, self.turn, self.eng = sem, 0, 0, None

    def on(self, eng):
        self.eng = eng
        return self

    def link(self, ins):
        self.n += 1
        ins.then_inc(self.sem, 1)
        self.eng.wait_ge(self.sem, self.turn + self.n)

    @contextmanager
    def loop(self, i, turns, per):
        start, self.turn = self.n, i * per
        yield
        assert self.n - start == per, self.n - start
        self.n, self.turn = start + turns * per, 0


def trunk(nc, A, out, scratch, const_at):
    top = ExitStack()
    with top:
        def sb(scope, name, shape, dt=F32):
            return scope.enter_context(nc.sbuf_tensor(name, shape, dt))

        kept_sems, phase_sems = [], []

        def sem(name, keep=False):
            handle = nc.alloc_semaphore(name=name)
            (kept_sems if keep else phase_sems).append(handle)
            return handle

        def end_of_era():
            nc.clear_and_free_semaphores(list(phase_sems))
            phase_sems.clear()
            nc.all_engine_barrier()

        bank2 = [top.enter_context(nc.psum_tensor(f"bank2_{i}", [P, 1024], F32)) for i in range(4)]
        bank = [bank2[i // 2][:, 512 * (i % 2):512 * (i % 2) + 512] for i in range(8)]
        dve_steps, act_steps, pool_steps = Steps(sem("dve_step", True)), Steps(sem("act_step", True)), Steps(sem("pool_step", True))

        pool_passed = sem("pool_passed", True)

        n_const = sum(n for _, n in const_at.values())
        const = sb(top, "const", [P, n_const])

        def cst(name, **dims):
            a, n = const_at[name]
            v = const[:, a:a + n]
            return v.rearrange(dims.pop("to"), **dims) if dims else v

        ident = cst("ident")
        gain_attn = sb(top, "gain_attn", [P, KC])
        gain_src = sb(top, "gain_src", [P, KC])
        gain_mem = sb(top, "gain_mem", [P, KC])
        gain_moe = sb(top, "gain_moe", [P, KC])
        gain_mix = sb(top, "gain_mix", [P, KC])
        mem_kT = sb(top, "mem_kT", [P, MH, NMEM])
        mem_kv = sb(top, "mem_kv", [P, 2, 2 * MW])

        window_out = sem("window_out", True)
        const_loaded = sem("const_loaded")
        with nc.Block() as block:
            @block.sync
            def _(sp):
                sp.dma_start(const[:, :], A["const"]).then_inc(const_loaded, 16)
                for dst, src in ((gain_attn, "g_attn_norm"), (gain_src, "g_mem_src"), (gain_mem, "g_mem_norm"),
                                 (gain_moe, "g_moe_norm")):
                    sp.dma_start(dst[:, :], A[src][0].rearrange("(p c) -> p c", c=KC)).then_inc(const_loaded, 16)
                sp.dma_start(gain_mix[0:64, :], A["g_nsa_out"][0].rearrange("(p c) -> p c", c=KC)).then_inc(const_loaded, 16)
                sp.dma_start(gain_mix[64:128, :], A["g_sgu_out"][0].rearrange("(p c) -> p c", c=KC)).then_inc(const_loaded, 16)
                sp.wait_ge(const_loaded, 16 * 7)

            @block.gpsimd
            def _(pool):
                for cache, dst in (("cache_win_k", "win_k_s"), ("cache_win_v", "win_v_s")):
                    pool.dma_start(out[dst][0, :, 0:WIN - NT].rearrange("b (s t) g d -> b s (t g d)", s=NT),
                                   A[cache][0, :, NT:WIN].rearrange("b (s t) g d -> b s (t g d)", s=NT)).then_inc(window_out, 16)

        def norm_transpose(tag, tiles, segs, stores=()):
            n, ns, width = len(tiles), len(segs), segs[0][1] - segs[0][0]
            squared, scaled, rooted = sem(tag + "_squared"), sem(tag + "_scaled"), sem(tag + "_rooted")
            normed, turned, drained = (sem(tag + x) for x in ("_normed", "_turned", "_drained"))
            stored = [sem(tag + f"_stored{v}") for v in range(2)] if stores else []
            with ExitStack() as scope:
                junk = sb(scope, tag + "_junk", [P, width])
                hn = sb(scope, tag + "_hn", [P, 2, D])
                ms = sb(scope, tag + "_ms", [P, n * ns])
                block = scope.enter_context(nc.Block())

                @block.scalar
                def _(act):
                    for i, (src, _, _, loaded) in enumerate(tiles):
                        if loaded:
                            act.wait_ge(*loaded)
                        for j, (a, b) in enumerate(segs):
                            k = i * ns + j
                            if k:
                                act.wait_ge(squared, k)
                            act.activation(junk[:, :], src[:, a:b], ACT.Square,
                                           accum_out=ms[:, k:k + 1]).then_inc(squared, 1)
                    act.wait_ge(scaled, 1)
                    act.activation(ms[:, :], ms[:, :], ACT.Sqrt).then_inc(rooted, 1)

                @block.vector
                def _(dve):
                    own = dve_steps.on(dve)
                    dve.wait_ge(squared, n * ns)
                    dve.tensor_scalar(ms[:, :], ms[:, :], 1.0 / width, EPS, ALU.mult, ALU.add).then_inc(scaled, 1)
                    dve.wait_ge(rooted, 1)
                    own.link(dve.reciprocal(ms[:, :], ms[:, :]))

                    def normalise(i):
                        if i >= 2:
                            dve.wait_ge(turned, 4 * (i - 1))
                            if stores:
                                dve.wait_ge(stored[i % 2], 16 * (i // 2))
                        for j, (a, b) in enumerate(segs):
                            k = i * ns + j
                            dve.tensor_scalar(hn[:, i % 2, a:b], tiles[i][0][:, a:b], ms[:, k:k + 1], None,
                                              ALU.mult).then_inc(normed, 1)

                    def drain(i):
                        for j in range(4):
                            dve.wait_ge(turned, 4 * i + j + 1)
                            dve.tensor_tensor(tiles[i][2][:, 4 * j:4 * j + 4, :],
                                              bank[(i % 2) * 4 + j].rearrange("p (c r) -> p c r", c=4),
                                              tiles[i][1][:, 4 * j:4 * j + 4].unsqueeze(2).to_broadcast([P, 4, P]),
                                              ALU.mult).then_inc(drained, 1)

                    for i in range(n + 1):
                        if i < n:
                            normalise(i)
                        if i >= 1:
                            drain(i - 1)

                @block.tensor
                def _(pe):
                    for i in range(n):
                        pe.wait_ge(normed, ns * (i + 1))
                        if i >= 2:
                            pe.wait_ge(drained, 4 * (i - 1))
                        for c in range(KC):
                            mm = pe.transpose(bank[(i % 2) * 4 + c // 4][:, (c % 4) * P:(c % 4) * P + P],
                                              hn[:, i % 2, c:D:KC], ident)
                            if c % 4 == 3:
                                mm.then_inc(turned, 1)

                if stores:
                    @block.sync
                    def _(sp):
                        for i, (dst, rows) in enumerate(stores):
                            sp.wait_ge(normed, ns * (i + 1))
                            sp.dma_start(dst, hn[0:rows, i % 2, :]).then_inc(stored[i % 2], 16)
                        for v in range(2):
                            sp.wait_ge(stored[v], 16 * ((len(stores) + 1 - v) // 2))

        def transpose_jobs(tag, jobs, loads=()):
            turned = [sem(tag + f"_turned{v}") for v in range(2)]
            copied = [sem(tag + f"_copied{v}") for v in range(2)]
            loaded = sem(tag + "_loaded")
            with nc.Block() as block:
                @block.sync
                def _(sp):
                    for dst, src in loads:
                        sp.dma_start(dst, src).then_inc(loaded, 16)

                @block.tensor
                def _(pe):
                    if loads:
                        pe.wait_ge(loaded, 16 * len(loads))
                    for n, (blocks, _) in enumerate(jobs):
                        b = n % 4
                        if n >= 4:
                            pe.wait_ge(copied[n % 2], n // 2 - 1)
                        for rows, cols, off, src in blocks:
                            mm = pe.transpose(bank[b][0:cols, off:off + rows], src, ident[0:rows, 0:rows])
                        mm.then_inc(turned[n % 2], 1)

                def copies(eng, copy, v):
                    for n, (_, pairs) in enumerate(jobs):
                        if n % 2 != v:
                            continue
                        eng.wait_ge(turned[v], n // 2 + 1)
                        for dst, view in pairs:
                            ins = copy(dst, view(bank[n % 4]))
                        ins.then_inc(copied[v], 1)

                @block.scalar
                def _(act):
                    copies(act, act.copy, 0)

                @block.vector
                def _(dve):
                    copies(dve, dve.tensor_copy, 1)

        def project(tag, hT, toks, plan, wbuf, residual=False, chunks=KC):
            loaded = [sem(tag + f"_w_loaded{u}") for u in range(2)]
            ready = [sem(tag + f"_ready{u}") for u in range(2)]
            copied = [sem(tag + f"_copied{u}") for u in range(2)]
            pairs, tile_of, peeled = plan

            def tiles(eng, body):
                if pairs:
                    with eng.Fori(0, pairs) as i:
                        for u in range(2):
                            body(u, i, *tile_of(i, u))
                for n, tile in enumerate(peeled):
                    body(n % 2, pairs + n // 2, *tile)

            with nc.Block() as block:
                @block.sync
                def _(sp):
                    def load(u, i, w, width, dst):
                        sp.wait_ge(ready[u], i * toks)
                        sp.dma_start(wbuf[:, u, 0:chunks, 0:width], w).then_inc(loaded[u], 16)
                    tiles(sp, load)

                @block.tensor
                def _(pe):
                    def multiply(u, i, w, width, dst):
                        pe.wait_ge(loaded[u], i * 16 + 16)
                        pe.wait_ge(copied[u], i * toks)
                        for r in range(toks):
                            for c in range(chunks):
                                mm = pe.matmul(bank[4 * u + r][:, 0:width], hT[:, c, r * P:(r + 1) * P],
                                               wbuf[:, u, c, 0:width], start=(c == 0), stop=(c == chunks - 1))
                            mm.then_inc(ready[u], 1)
                    tiles(pe, multiply)

                @block.scalar
                def _(act):
                    if residual:
                        return

                    def take(u, i, w, width, dst):
                        for r in range(0, toks, 2):
                            act.wait_ge(ready[u], i * toks + r + 1)
                            act.copy(dst(r), bank[4 * u + r][:, 0:width]).then_inc(copied[u], 1)
                    tiles(act, take)

                @block.vector
                def _(dve):
                    def take(u, i, w, width, dst):
                        for r in range(0, toks) if residual else range(1, toks, 2):
                            dve.wait_ge(ready[u], i * toks + r + 1)
                            if residual:
                                dve.tensor_tensor(dst(r), bank[4 * u + r][:, 0:width], dst(r), ALU.add).then_inc(copied[u], 1)
                                continue
                            dve.tensor_copy(dst(r), bank[4 * u + r][:, 0:width]).then_inc(copied[u], 1)
                    tiles(dve, take)

        w_view = lambda name: A[name][0].rearrange("(p c) n -> p c n", c=KC)

        with ExitStack() as scope:
            hmT = sb(scope, "hmT", [P, KC, NMEM])
            with ExitStack() as inner:
                mem_x = sb(inner, "mem_x", [P, 2, D])
                mem_loaded = sem("mem_loaded")
                with nc.Block() as block:
                    @block.sync
                    def _(sp):
                        sp.dma_start(mem_x[:, :, :], A["mem_prompt"][0].rearrange("(r p) n -> p r n", p=P)).then_inc(mem_loaded, 16)
                norm_transpose("mem_src", [(mem_x[:, r, :], gain_src, hmT[:, :, r * P:(r + 1) * P], (mem_loaded, 16))
                                           for r in range(2)], [(0, D)])
            wbuf = sb(scope, "w_mem", [P, 2, KC, 512])
            project("mem_kv", hmT, 2, (0, None, [
                (w_view("w_mem_k"), 512, lambda r: mem_kv[:, r, 0:512]),
                (w_view("w_mem_v"), 512, lambda r: mem_kv[:, r, 512:1024])]), wbuf)

        attn = top.enter_context(ExitStack())
        Z = sb(attn, "Z", [P, TILES, IN_COLS])
        with ExitStack() as scope:
            hT = sb(scope, "hT", [P, KC, TILES * P])
            with ExitStack() as inner:
                x0 = sb(inner, "x0", [P, TILES, D])
                x_loaded = sem("x_loaded")
                with nc.Block() as block:
                    @block.sync
                    def _(sp):
                        sp.dma_start(x0[0:NS, 2, :], A["x_sample"].rearrange("b t n -> (b t) n")).then_inc(x_loaded, 16)
                        for r in range(2):
                            sp.dma_start(x0[:, r, :], A["x_prompt"][0, r * P:(r + 1) * P, :]).then_inc(x_loaded, 16)

                    @block.vector
                    def _(dve):
                        dve.memset(x0[NS:P, 2, :], 0.0)
                norm_transpose("attn", [(x0[:, r, :], gain_attn, hT[:, :, r * P:(r + 1) * P], (x_loaded, 48))
                                        for r in range(TILES)], [(0, D)])
            wbuf = sb(scope, "w_in_buf", [P, 2, KC, 512])
            w_in = w_view("w_in")
            project("w_in", hT, TILES, (4, lambda i, u: (w_in[:, :, bass.ds(i * 1024 + u * 512, 512)], 512,
                                                       lambda r: Z[:, r, bass.ds(i * 1024 + u * 512, 512)]), [
                (w_in[:, :, 4096:4608], 512, lambda r: Z[:, r, 4096:4608]),
                (w_in[:, :, 4608:IN_COLS], 48, lambda r: Z[:, r, 4608:IN_COLS])]), wbuf)

        qT = sb(attn, "qT", [P, 8, TILES * P])
        qrT = sb(attn, "qrT", [P, 8, TILES * P])
        kT = sb(attn, "kT", [P, 4, TILES * P])
        state_out = sem("state_out")
        with ExitStack() as scope:
            QQ = sb(scope, "QQ", [P, TILES, 1024])
            QR = sb(scope, "QR", [P, TILES, 1024])
            vgain = sb(scope, "vgain", [P, SW])
            with ExitStack() as inner:
                ta = sb(inner, "rope_a", [P, 256])
                tb = sb(inner, "rope_b", [P, 256])
                vjunk = sb(inner, "vjunk", [P, SW])
                vms = sb(inner, "vms", [P, TILES])
                q_copied, v_squared, v_scaled, v_rooted = (sem(x) for x in ("q_copied", "v_squared", "v_scaled", "v_rooted"))
                roped, gated, v_ready, vgain_loaded = (sem(x) for x in ("roped", "gated", "v_ready", "vgain_loaded"))
                block = inner.enter_context(nc.Block())

                @block.scalar
                def _(act):
                    own = act_steps.on(act)
                    for r in range(TILES):
                        for c in range(2):
                            a = C_Q + 512 * c
                            for dst in (QR, QQ):
                                act.copy(dst[:, r, 512 * c:512 * c + 512].rearrange("p (j g d) -> p g j d", j=NJ, g=2),
                                         Z[:, r, a:a + 512].rearrange("p (g j d) -> p g j d", j=NJ, g=2)).then_inc(q_copied, 1)
                    own.link(act.activation(Z[:, :, C_U:IN_COLS], Z[:, :, C_U:IN_COLS], ACT.Gelu_apprx_tanh))
                    for r in range(TILES):
                        if r:
                            act.wait_ge(v_squared, r)
                        act.activation(vjunk[:, :], Z[:, r, C_V:C_V + SW], ACT.Square,
                                       accum_out=vms[:, r:r + 1]).then_inc(v_squared, 1)
                    act.activation(Z[:, :, C_G:C_G + 48], Z[:, :, C_G:C_G + 48], ACT.Sigmoid).then_inc(gated, 1)
                    act.wait_ge(v_scaled, 1)
                    act.activation(vms[:, :], vms[:, :], ACT.Sqrt).then_inc(v_rooted, 1)

                @block.vector
                def _(dve):
                    own = dve_steps.on(dve)
                    cos2 = cst("cos2", to="p (r n) -> p r n", r=TILES)
                    sin2 = cst("sin2", to="p (r n) -> p r n", r=TILES)

                    def rope(x, r, n, like):
                        def over(v):
                            while len(v.shape) < len(x.shape):
                                v = v.unsqueeze(1)
                            return v.to_broadcast(list(x.shape[:-1]) + [v.shape[-1]])
                        a, b = like(ta[:, 0:n * ROT]), like(tb[:, 0:n * ROT])
                        dve.tensor_tensor(a, x, over(cos2[:, r, :]), ALU.mult)
                        ix = tuple([slice(None)] * (len(x.shape) - 1))
                        dve.tensor_tensor(b[ix + (slice(0, 8),)], x[ix + (slice(8, 16),)], over(sin2[:, r, 0:8]), ALU.mult)
                        own.link(dve.tensor_tensor(b[ix + (slice(8, 16),)], x[ix + (slice(0, 8),)], over(sin2[:, r, 8:16]), ALU.mult))
                        own.link(dve.tensor_tensor(x, a, b, ALU.add))

                    dve.wait_ge(q_copied, 4 * TILES)
                    for r in range(TILES):
                        rope(QR[:, r, :].rearrange("p (h d) -> p h d", d=HD)[:, :, 0:ROT], r, NH,
                             lambda v: v.rearrange("p (h d) -> p h d", d=ROT))
                        rope(Z[:, r, C_KS:C_KS + 1024].rearrange("p (k h d) -> p k h d", k=2, d=HD)[:, :, 0:NG, 0:ROT], r, 2 * NG,
                             lambda v: v.rearrange("p (k h d) -> p k h d", k=2, d=ROT))
                    dve.sem_inc(roped, 1)
                    dve.wait_ge(v_squared, TILES)
                    dve.tensor_scalar(vms[:, :], vms[:, :], 1.0 / SW, EPS, ALU.mult, ALU.add).then_inc(v_scaled, 1)
                    dve.wait_ge(v_rooted, 1)
                    own.link(dve.reciprocal(vms[:, :], vms[:, :]))
                    dve.wait_ge(vgain_loaded, 16)
                    for r in range(TILES):
                        v = Z[:, r, C_V:C_V + SW]
                        dve.scalar_tensor_tensor(out=v, in0=v, scalar=vms[:, r:r + 1], in1=vgain[:, :],
                                                 op0=ALU.mult, op1=ALU.mult).then_inc(v_ready, 1)

                @block.sync
                def _(sp):
                    stored = [0]

                    def store(dst, src):
                        stored[0] += 1
                        sp.dma_start(dst, src).then_inc(state_out, 16)

                    sp.dma_start(vgain[:, :], A["g_sgu_v"][0].partition_broadcast(P)).then_inc(vgain_loaded, 16)

                    def state(kind, col):
                        for r in range(2):
                            store(out[kind + "_p"][0, 0, r * P:(r + 1) * P].rearrange("r g d -> r (g d)"),
                                         Z[:, r, col:col + KVW])

                    def state_s(kind, col):
                        store(out[kind + "_s"][0].rearrange("b t g d -> (b t) (g d)"),
                                     Z[0:NS, 2, col:col + KVW])
                    for kind, col in (("cmp_k", C_KC), ("cmp_v", C_VC), ("sel_v", C_VS)):
                        state(kind, col)
                        state_s(kind, col)
                    state("win_v", C_VW)
                    for n, kind in enumerate(("mem_k_p", "mem_v_p")):
                        for r in range(2):
                            store(out[kind][0, 0, r * P:(r + 1) * P].rearrange("r h d -> r (h d)"),
                                         mem_kv[:, r, n * MW:(n + 1) * MW])
                    sp.wait_ge(roped, 1)
                    state("sel_k", C_KS)
                    state_s("sel_k", C_KS)
                    state("win_k", C_KW)
                    for kind, col in (("win_k_s", C_KW), ("win_v_s", C_VW)):
                        for b in range(NB):
                            store(out[kind][0, b, WIN - NT:WIN].rearrange("t g d -> t (g d)"),
                                         Z[b * NT:(b + 1) * NT, 2, col:col + KVW])
                    sp.wait_ge(gated, 1)
                    store(scratch["gates"], Z[0:NS, 2, C_G:C_G + 48])
                    sp.wait_ge(v_ready, TILES)
                    store(out["sgu_v_s"][0].rearrange("b t n -> (b t) n"), Z[0:NS, 2, C_V:C_V + SW])
                    sp.wait_ge(state_out, 16 * stored[0])


            def bank_view(n):
                return lambda b: b[:, 0:n * P].rearrange("p (c r) -> p c r", c=n)

            jobs = []
            for r in range(TILES):
                rows = slice(r * P, (r + 1) * P)
                for src, dst in ((QQ, qT), (QR, qrT)):
                    for c in range(2):
                        jobs.append(([(P, P, j * P, src[:, r, (4 * c + j) * P:(4 * c + j + 1) * P]) for j in range(NJ)],
                                     [(dst[:, 4 * c:4 * c + 4, rows], bank_view(4))]))
                jobs.append(([(P, P, n * P, Z[:, r, col:col + P]) for n, col in enumerate((C_KS, C_KS + P, C_KW, C_KW + P))],
                             [(kT[:, :, rows], bank_view(4))]))
            for r in range(2):
                jobs.append(([(P, P, h * P, mem_kv[:, r, h * MD:(h + 1) * MD]) for h in range(MH)],
                             [(mem_kT[:, :, r * P:(r + 1) * P], bank_view(4))]))
            transpose_jobs("qk", jobs)
        end_of_era()
        kcT = sb(attn, "kcT", [P, 2, NB * NCS])
        kcT_p = sb(attn, "kcT_p", [P, 2, NCP])
        vc = sb(attn, "vc", [NCS, NB, KVW])
        vc_p = sb(attn, "vc_p", [NCP, KVW])
        pages = sb(attn, "pages", [1, NB * NPG], I32)
        pages_loaded = sem("pages_loaded")
        with ExitStack() as scope:
            raw = sb(scope, "raw", [P, 2, STRIDE * KVW // 2])
            rawg = sb(scope, "rawg", [P, 2, STRIDE * KVW // 2])
            subT = sb(scope, "subT", [P, 8, 512])
            w1 = sb(scope, "w1", [P, 2, KC, CH])
            w2k = sb(scope, "w2k", [P, P])
            w2v = sb(scope, "w2v", [P, HD])
            pe_rows = sb(scope, "pe_rows", [KC, 2, P])
            peT = sb(scope, "peT", [P, 2, KC])
            pe_bias = sb(scope, "pe_bias", [P, 2])
            hid = sb(scope, "hid", [P, 504])
            cw_loaded, pe_turned, pe_copied, pe_summed, pe_ready = (sem(x) for x in (
                "cw_loaded", "pe_turned", "pe_copied", "pe_summed", "pe_ready"))
            raw_loaded = [sem(f"raw_loaded{v}") for v in range(2)]
            regrouped = [sem(f"regrouped{v}") for v in range(2)]
            sub_turned = [[sem(f"sub_turned{e}{v}") for v in range(2)] for e in range(2)]
            sub_copied = [sem(f"sub_copied{v}") for v in range(2)]
            hid_summed, hid_ready, kv_made, kv_kept = (sem(x) for x in ("hid_summed", "hid_ready", "kv_made", "kv_kept"))

            TURNS = NB // 2

            def turns(eng, body):
                with eng.Fori(0, TURNS) as i:
                    for u in range(2):
                        body(i * 2 + u, u, i, False)
                for u in range(2):
                    body(2 * TURNS + u, u, None, True)

            with nc.Block() as block:
                @block.sync
                def _(sp):
                    sp.dma_start(pages[:, :], A["page_table"].rearrange("b n -> (b n)").unsqueeze(0)).then_inc(pages_loaded, 16)
                    for u, kind in enumerate("kv"):
                        sp.dma_start(w1[:, u, :, :], A[f"w_cmp_{kind}1"][0].rearrange("(m p) h -> p m h", p=P)).then_inc(cw_loaded, 16)
                        sp.dma_start(pe_rows[:, u, :], A[f"pe_cmp_{kind}"][0].rearrange("(m l) d -> m (l d)", m=KC)).then_inc(cw_loaded, 16)
                    for n in range(2):
                        sp.dma_start(w2k[:, HD * n:HD * n + HD], A["w_cmp_k2"][0]).then_inc(cw_loaded, 16)
                    sp.dma_start(w2v[:, :], A["w_cmp_v2"][0]).then_inc(cw_loaded, 16)
                    sp.wait_ge(pages_loaded, 16)

                    def load(turn, u, i, prompt):
                        name = ("cache_cmp_k", "cache_cmp_v")[u]
                        half = STRIDE * KVW // 2
                        if prompt:
                            src = out[("cmp_k_p", "cmp_v_p")[u]][0, 0].rearrange("(n s) g d -> n (s g d)", s=STRIDE)
                            for v in range(2):
                                sp.wait_ge(regrouped[v], turn)
                                for n in range(NSUBP):
                                    sp.dma_start(raw[n:n + 1, v, :], src[n:n + 1, half * v:half * v + half]).then_inc(raw_loaded[v], 16)
                            return
                        ids = []
                        for j in range(2 * NPG):
                            ids.append(sp.value_load(pages[0:1, bass.ds(i * 2 * NPG + j, 1)], min_val=0, max_val=A[name].shape[1] - 1))
                        for v in range(2):
                            sp.wait_ge(regrouped[v], turn)
                            for j in range(2 * NPG):
                                src = A[name][0, bass.ds(ids[j], 1)].rearrange("o (n s) g d -> (o n) (s g d)", s=STRIDE)
                                sp.dma_start(raw[8 * j:8 * j + 8, v, :], src[:, half * v:half * v + half]).then_inc(raw_loaded[v], 16)
                    turns(sp, load)

                @block.gpsimd
                def _(pool):
                    def regroup(turn, u, i, prompt):
                        n = NSUBP if prompt else P
                        for v in range(2):
                            pool.wait_ge(raw_loaded[v], turn * 256 + 256)
                            pool.wait_ge(sub_turned[1][v], turn * 2)
                            pool.sem_inc(pool_passed, 1)
                            pool.tensor_copy(rawg[0:n, v, :].rearrange("p (g s d) -> p g s d", g=NG, d=HD),
                                             raw[0:n, v, :].rearrange("p (s g d) -> p g s d", g=NG, d=HD)).then_inc(regrouped[v], 1)
                    turns(pool, regroup)

                @block.tensor
                def _(pe):
                    pe.wait_ge(cw_loaded, 16 * 7)
                    for u in range(2):
                        mm = pe.transpose(bank[0][:, 16 * u:16 * u + KC], pe_rows[:, u, :], ident[0:KC, 0:KC])
                    mm.then_inc(pe_turned, 1)
                    pe.wait_ge(pe_copied, 1)
                    for u in range(2):
                        for m in range(KC):
                            mm = pe.matmul(bank[1][:, u:u + 1], w1[:, u, m, :], peT[:, u, m:m + 1],
                                           start=(m == 0), stop=(m == KC - 1))
                    mm.then_inc(pe_summed, 1)
                    pe.wait_ge(pe_ready, 1)

                    def step(turn, u, i, prompt):
                        n = NSUBP if prompt else P
                        nk = NCP if prompt else NCS
                        groups = NG if prompt else 2 * NG
                        wide = 4 * n
                        for q in range(8):
                            v = q // 4
                            if q % 4 == 0:
                                pe.wait_ge(regrouped[v], turn + 1)
                            if q >= 4:
                                pe.wait_ge(sub_copied[q % 2], turn * 4 + q // 2 - 1)
                            for g in range(NG):
                                a = g * 512 + (q % 4) * P
                                mm = pe.transpose(bank[q % 4][:, g * n:g * n + n], rawg[0:n, v, a:a + P], ident[0:n, 0:n])
                            mm.then_inc(sub_turned[q % 2][v], 1)
                        for v in range(2):
                            pe.wait_ge(sub_copied[v], turn * 4 + 4)
                        for q in range(8):
                            x = subT[:, q, 0:wide].rearrange("p (k n) -> p k n", k=groups)
                            for r in range(2):
                                mm = pe.matmul(bank[4][:, 0:groups * nk], w1[:, u, 8 * r + q, :], x[:, :, r:r + nk],
                                               start=(q == 0 and r == 0), stop=(q == 7 and r == 1))
                        mm.then_inc(hid_summed, 1)
                        pe.wait_ge(hid_ready, turn + 1)
                        pe.wait_ge(kv_kept, turn)
                        if u == 0:
                            mm = pe.matmul(bank[5][:, 0:groups * nk], w2k[:, :], hid[:, 0:groups * nk], start=True, stop=True)
                        else:
                            for k in range(groups):
                                mm = pe.matmul(bank[6][0:nk, HD * k:HD * k + HD], hid[:, nk * k:nk * k + nk], w2v[:, :],
                                               start=True, stop=True)
                        mm.then_inc(kv_made, 1)
                    turns(pe, step)

                def copy_blocks(eng, copy, v, turn, prompt):
                    wide = 4 * (NSUBP if prompt else P)
                    for k in range(4):
                        q = 2 * k + v
                        eng.wait_ge(sub_turned[v][k // 2], turn * 2 + k % 2 + 1)
                        copy(subT[:, q, 0:wide], bank[q % 4][:, 0:wide]).then_inc(sub_copied[v], 1)

                @block.scalar
                def _(act):
                    def step(turn, u, i, prompt):
                        cols = NG * NCP if prompt else 2 * NG * NCS
                        copy_blocks(act, act.copy, 0, turn, prompt)
                        act.wait_ge(hid_summed, turn + 1)
                        act.wait_ge(kv_made, turn)
                        act.activation(hid[:, 0:cols], bank[4][:, 0:cols], ACT.Silu, bias=pe_bias[:, u:u + 1]).then_inc(hid_ready, 1)
                    act.wait_ge(pe_ready, 1)
                    turns(act, step)

                @block.vector
                def _(dve):
                    dve.wait_ge(pe_turned, 1)
                    dve.tensor_copy(peT[:, :, :], bank[0][:, 0:32].rearrange("p (u m) -> p u m", u=2)).then_inc(pe_copied, 1)
                    dve.wait_ge(pe_summed, 1)
                    dve.tensor_copy(pe_bias[:, :], bank[1][:, 0:2]).then_inc(pe_ready, 1)

                    def step(turn, u, i, prompt):
                        copy_blocks(dve, dve.tensor_copy, 1, turn, prompt)
                        dve.wait_ge(kv_made, turn + 1)
                        if u == 0:
                            n = NCP if prompt else 2 * NCS
                            for h in range(2):
                                rows = slice(64 * h, 64 * h + 64)
                                src = bank[5][rows, 0:NG * n].rearrange("p (c g n) -> p c g n", c=2, g=2)[:, :, h, :]
                                dst = kcT_p[rows, :, :] if prompt else kcT[rows, :, bass.ds(i * n, n)]
                                ins = dve.tensor_copy(dst, src)
                        elif prompt:
                            ins = dve.tensor_copy(vc_p[:, :], bank[6][0:NCP, 0:KVW])
                        else:
                            ins = dve.tensor_copy(vc[:, bass.ds(i * 2, 2), :].rearrange("p b (g d) -> p g b d", g=NG),
                                                  bank[6][0:NCS, :].rearrange("p (g b d) -> p g b d", g=NG, b=2))
                        ins.then_inc(kv_kept, 1)
                    turns(dve, step)

        end_of_era()
        gates_ht = sb(attn, "gates_ht", [P, NB, 3])
        qr_bd = sb(attn, "qr_bd", [P, 2, NB, P])
        cmp_pT = sb(attn, "cmp_pT", [NCS, NB, P])
        drop_add = sb(attn, "drop_add", [P, NB, NBLK])
        oT_s = sb(attn, "oT_s", [P, 8, NS])
        with ExitStack() as scope:
            q_bd = sb(scope, "q_bd", [P, 2, NB, P])
            sc = sb(scope, "cmp_s", [P, NB, NCS])
            pc = sb(scope, "cmp_p", [P, NB, NCS])
            pg = sb(scope, "cmp_pg", [P, NB, NCS])
            st = sb(scope, "cmp_stat", [P, 4, NB])
            ps = sb(scope, "cmp_ps", [P, 3, NB, NBLK - 2])
            gates_loaded, bd_ready, cmp_scored, cmp_centred, cmp_exp, cmp_prob, cmp_grouped, cmp_turned, cmp_gated = (
                sem("c_" + x) for x in ("gates_loaded", "bd_ready", "scored", "centred", "exp", "prob", "grouped", "turned", "gated"))
            with nc.Block() as block:
                @block.sync
                def _(sp):
                    for h in range(NH):
                        sp.dma_start(gates_ht[h * NT:(h + 1) * NT, :, :],
                                     scratch["gates"][:, 3 * h:3 * h + 3].rearrange("(b t) c -> t b c", b=NB)).then_inc(gates_loaded, 16)

                @block.vector
                def _(dve):
                    own = dve_steps.on(dve)
                    dve.memset(q_bd[:, :, :, :], 0.0)
                    own.link(dve.memset(qr_bd[:, :, :, :], 0.0))
                    for src, dst in ((qT, q_bd), (qrT, qr_bd)):
                        for c in range(2):
                            for h in range(2):
                                rows = slice(64 * h, 64 * h + 64)
                                a = (2 * c + h) * 32
                                dve.tensor_copy(dst[rows, c, :, a:a + 32].rearrange("p b (j t) -> p j b t", j=NJ),
                                                src[rows, 4 * c:4 * c + 4, 256:256 + NS].rearrange("p j (b t) -> p j b t", b=NB)).then_inc(bd_ready, 1)
                    dve.wait_ge(cmp_scored, 1)
                    own.link(dve.tensor_scalar(sc[:, :, :], bank[0][:, 0:NB * NCS].rearrange("p (b n) -> p b n", b=NB), SCALE, None, ALU.mult))
                    own.link(dve.reduce_max(st[:, 0, :], sc[:, :, :], AX))
                    dve.tensor_tensor(sc[:, :, :], sc[:, :, :], st[:, 0, :].unsqueeze(2).to_broadcast([P, NB, NCS]), ALU.subtract).then_inc(cmp_centred, 1)
                    dve.wait_ge(cmp_exp, 1)
                    own.link(dve.reduce_sum(st[:, 1, :], pc[:, :, :], AX))
                    own.link(dve.reciprocal(st[:, 1, :], st[:, 1, :]))
                    dve.tensor_tensor(pc[:, :, :], pc[:, :, :], st[:, 1, :].unsqueeze(2).to_broadcast([P, NB, NCS]), ALU.mult).then_inc(cmp_prob, 1)
                    dve.wait_ge(cmp_grouped, 1)
                    own.link(dve.tensor_copy(pg[:, :, :], bank[1][:, 0:NB * NCS].rearrange("p (b n) -> p b n", b=NB)))
                    inner = pg[:, :, 4:4 * (NBLK - 1)].rearrange("p b (k r) -> p b k r", r=4)
                    own.link(dve.tensor_tensor(ps[:, 0], inner[:, :, :, 0], inner[:, :, :, 1], ALU.add))
                    own.link(dve.tensor_tensor(ps[:, 1], ps[:, 0], inner[:, :, :, 2], ALU.add))
                    own.link(dve.tensor_reduce(st[:, 2, :], ps[:, 1], AX, ALU.min))
                    own.link(dve.tensor_tensor(ps[:, 2], ps[:, 1], st[:, 2, :].unsqueeze(2).to_broadcast([P, NB, NBLK - 2]), ALU.is_equal))
                    own.link(dve.tensor_tensor(ps[:, 0], ps[:, 2], cst("block_id")[:, 1:NBLK - 1].unsqueeze(1).to_broadcast([P, NB, NBLK - 2]), ALU.mult))
                    own.link(dve.reduce_max(st[:, 3, :], ps[:, 0], AX))
                    own.link(dve.tensor_tensor(drop_add[:, :, :], cst("block_id").unsqueeze(1).to_broadcast([P, NB, NBLK]),
                                               st[:, 3, :].unsqueeze(2).to_broadcast([P, NB, NBLK]), ALU.is_equal))
                    own.link(dve.tensor_scalar(drop_add[:, :, :], drop_add[:, :, :], NEG, None, ALU.mult))
                    dve.wait_ge(gates_loaded, 16 * NH)
                    dve.tensor_tensor(sc[:, :, :], pc[:, :, :], gates_ht[:, :, 0:1].to_broadcast([P, NB, NCS]), ALU.mult).then_inc(cmp_gated, 1)
                    dve.wait_ge(cmp_turned, 1)
                    for n in range(2):
                        dve.tensor_copy(cmp_pT[:, 4 * n:4 * n + 4, :], bank[2 + n][0:NCS, :].rearrange("p (b r) -> p b r", b=4))

                @block.scalar
                def _(act):
                    act.wait_ge(cmp_centred, 1)
                    act.activation(pc[:, :, :], sc[:, :, :], ACT.Exp).then_inc(cmp_exp, 1)

                @block.tensor
                def _(pe):
                    pe.wait_ge(bd_ready, 8)
                    for b in range(NB):
                        for c in range(2):
                            mm = pe.matmul(bank[0][:, NCS * b:NCS * b + NCS], q_bd[:, c, b, :], kcT[:, c, NCS * b:NCS * b + NCS],
                                           start=(c == 0), stop=(c == 1))
                    mm.then_inc(cmp_scored, 1)
                    pe.wait_ge(cmp_prob, 1)
                    pe.matmul(bank[1][:, 0:NB * NCS], cst("group"), pc[:, :, :].rearrange("p b n -> p (b n)"),
                              start=True, stop=True).then_inc(cmp_grouped, 1)
                    pe.wait_ge(cmp_gated, 1)
                    for b in range(NB):
                        mm = pe.transpose(bank[2 + b // 4][0:NCS, (b % 4) * P:(b % 4) * P + P], sc[:, b, :], ident)
                    mm.then_inc(cmp_turned, 1)

        with ExitStack() as scope:
            k_in = sb(scope, "k_in", [P, 12, KVW])
            v_in = sb(scope, "v_in", [P, 2, 12, KVW])
            keyT = sb(scope, "keyT", [P, 2, 12 * P])
            q_now = sb(scope, "q_now", [P, 2, P])
            vc_now = sb(scope, "vc_now", [NCS, KVW])
            s = sb(scope, "s", [P, PAST + NS + WIN + NS])
            S_W = PAST + NS
            s_neg = sb(scope, "s_neg", [P, 2])
            s_sum = sb(scope, "s_sum", [P, 2])
            pT = sb(scope, "pT", [P, 15, P])
            k_loaded, k_turned_all, q_ready, key_scored, max_ready, exp_ready, p_ready, o_made, o_kept, vc_ready = (
                sem("s_" + x) for x in ("k_loaded", "k_turned_all", "q_ready", "key_scored", "max_ready", "exp_ready", "p_ready",
                                        "o_made", "o_kept", "vc_ready"))
            v_loaded = [sem(f"s_v_loaded{v}") for v in range(2)]
            v_used = [sem(f"s_v_used{v}") for v in range(2)]
            k_turned = [sem(f"s_k_turned{v}") for v in range(2)]
            k_copied = [sem(f"s_k_copied{v}") for v in range(2)]
            p_turned = [sem(f"s_p_turned{v}") for v in range(2)]
            p_copied = [sem(f"s_p_copied{v}") for v in range(2)]

            def samples(eng, body):
                with eng.Fori(0, NB // 2) as i:
                    for u in range(2):
                        body(i * 2 + u, u, i)

            with nc.Block() as block:
                @block.sync
                def _(sp):
                    def load(b, u, i):
                        ids = [sp.value_load(pages[0:1, bass.ds(b * NPG + j, 1)], min_val=0, max_val=A["cache_sel_k"].shape[1] - 1)
                               for j in range(NPG)]
                        for kind in "kv":
                            if kind == "k":
                                sp.wait_ge(k_turned_all, b)
                                to, done = k_in[:, :, :], k_loaded
                            else:
                                sp.wait_ge(v_used[u], i)
                                to, done = v_in[:, u, :, :], v_loaded[u]
                            for j in range(NPG):
                                sp.dma_start(to[:, j, :], A["cache_sel_" + kind][0, bass.ds(ids[j], 1)].rearrange("o p g d -> (o p) (g d)")).then_inc(done, 16)
                            sp.dma_start(to[:, NPG:12, :], A["cache_win_" + kind][0, bass.ds(b, 1)].rearrange("o (n p) g d -> p (o n) (g d)", p=P)).then_inc(done, 16)
                    samples(sp, load)

                KBLOCKS = [(c, m) for m in range(3) for c in range(2)]
                PBLOCKS = [[(n, n * P, P) for n in range(0, 4)], [(n, n * P, P) for n in range(4, 8)],
                           [(9 + n, S_W + n * P, P) for n in range(3)] + [(8, PAST, NS)],
                           [(12, S_W + 3 * P, P), (13, S_W + WIN, NS)]]

                @block.tensor
                def _(pe):
                    def step(b, u, i):
                        pe.wait_ge(k_loaded, b * 144 + 144)
                        for n, (c, m) in enumerate(KBLOCKS):
                            if n >= 2:
                                pe.wait_ge(k_copied[n % 2], b * 3 + n // 2)
                            for k in range(4):
                                mm = pe.transpose(bank[4 + n % 2][:, k * P:k * P + P], k_in[:, 4 * m + k, c * P:c * P + P], ident)
                            mm.then_inc(k_turned[n % 2], 1)
                        for v in range(2):
                            pe.wait_ge(k_copied[v], b * 3 + 3)
                        pe.sem_inc(k_turned_all, 1)
                        pe.wait_ge(q_ready, b + 1)
                        for c in range(2):
                            for n in range(3):
                                dst = bank[n]
                                pe.matmul(dst, q_now[:, c, :], keyT[:, c, 512 * n:512 * n + 512], start=(c == 0), stop=(c == 1))
                        for n in range(2):
                            for c in range(2):
                                mm = pe.matmul(bank[3][:, NS * n:NS * n + NS], q_now[:, c, :], kT[:, 2 * n + c, 256:256 + NS],
                                               start=(c == 0), stop=(c == 1))
                        mm.then_inc(key_scored, 1)
                        pe.wait_ge(p_ready, b * 2 + 2)
                        for n, blocks in enumerate(PBLOCKS):
                            if n >= 2:
                                pe.wait_ge(p_copied[n % 2], b * 2 + 1)
                            for k, (slot, off, width) in enumerate(blocks):
                                mm = pe.transpose(bank[6 + n % 2][0:width, k * P:k * P + P], s[:, off:off + width], ident)
                            mm.then_inc(p_turned[n % 2], 1)
                        pe.wait_ge(p_copied[0], b * 2 + 2)
                        pe.wait_ge(p_copied[1], b * 2 + 2)
                        pe.wait_ge(v_loaded[u], i * 144 + 144)
                        pe.wait_ge(vc_ready, b + 1)
                        pe.wait_ge(o_kept, b)
                        for c in range(2):
                            cols = slice(c * P, c * P + P)
                            terms = [(v_in[:, u, n, cols], pT[:, n, :]) for n in range(8)] \
                                + [(Z[0:NS, 2, C_VS + c * P:C_VS + c * P + P], pT[0:NS, 8, :])] \
                                + [(v_in[:, u, 8 + n, cols], pT[:, 9 + n, :]) for n in range(4)] \
                                + [(Z[0:NS, 2, C_VW + c * P:C_VW + c * P + P], pT[0:NS, 13, :])] \
                                + [(vc_now[:, cols], pT[0:NCS, 14, :])]
                            for n, (v, p) in enumerate(terms):
                                mm = pe.matmul(bank[3][:, 256 + 64 * c:320 + 64 * c], v, p[:, 64 * c:64 * c + 64],
                                               start=(n == 0), stop=(n == len(terms) - 1))
                            if c == 1:
                                mm.then_inc(o_made, 1)
                        pe.wait_ge(o_made, b + 1)
                        pe.sem_inc(v_used[u], 1)
                    samples(pe, step)

                def copy_keys(eng, copy, v, b):
                    for n, (c, m) in enumerate(KBLOCKS):
                        if n % 2 == v:
                            eng.wait_ge(k_turned[v], b * 3 + n // 2 + 1)
                            copy(keyT[:, c, 512 * m:512 * m + 512], bank[4 + v]).then_inc(k_copied[v], 1)

                def copy_probs(eng, copy, v, b):
                    for n in (v, v + 2):
                        eng.wait_ge(p_turned[v], b * 2 + n // 2 + 1)
                        blocks = PBLOCKS[n]
                        full = [k for k, x in enumerate(blocks) if x[2] == P]
                        part = [k for k, x in enumerate(blocks) if x[2] < P]
                        for k in part:
                            copy(pT[0:NS, blocks[k][0], :], bank[6 + v][0:NS, k * P:k * P + P])
                        a, z, slot = full[0], full[-1] + 1, blocks[full[0]][0]
                        copy(pT[:, slot:slot + z - a, :], bank[6 + v][:, a * P:z * P].rearrange("p (k r) -> p k r", r=P)).then_inc(p_copied[v], 1)

                @block.scalar
                def _(act):
                    def step(b, u, i):
                        act.wait_ge(o_made, b)
                        act.copy(vc_now[:, :], vc[:, bass.ds(b, 1), :].rearrange("p o n -> p (o n)")).then_inc(vc_ready, 1)
                        copy_keys(act, act.copy, 0, b)
                        act.wait_ge(max_ready, b + 1)
                        for n, (a, z) in enumerate(((0, S_W), (S_W, S_W + WIN + NS))):
                            act.activation(s[:, a:z], s[:, a:z], ACT.Exp, bias=s_neg[:, n:n + 1],
                                           accum_out=s_sum[:, n:n + 1]).then_inc(exp_ready, 1)
                        copy_probs(act, act.copy, 0, b)
                    samples(act, step)

                @block.vector
                def _(dve):
                    own = dve_steps.on(dve)

                    def step(b, u, i):
                        one = lambda v: v.rearrange("p o n -> p (o n)")
                        dve.wait_ge(key_scored, b)
                        dve.tensor_copy(q_now[:, :, :], qr_bd[:, :, bass.ds(b, 1), :].rearrange("p c o r -> p c (o r)")).then_inc(q_ready, 1)
                        copy_keys(dve, dve.tensor_copy, 1, b)
                        dve.wait_ge(key_scored, b + 1)
                        drop = one(drop_add[:, bass.ds(b, 1), :])
                        new = one(cst("new_add", to="p (b n) -> p b n", b=NB)[:, bass.ds(b, 1), :])
                        for a, width, src, mask in (
                                (0, PAST, bank2[0][:, :].rearrange("p (k l) -> p k l", l=LSEL), drop.unsqueeze(2).to_broadcast([P, NBLK, LSEL])),
                                (PAST, NS, bank[3][:, 0:NS], new),
                                (S_W, WIN, bank[2], cst("win_add")),
                                (S_W + WIN, NS, bank[3][:, NS:2 * NS], new)):
                            dst = s[:, a:a + width]
                            if a == 0:
                                dst = dst.rearrange("p (k l) -> p k l", l=LSEL)
                            ins = dve.scalar_tensor_tensor(out=dst, in0=src, scalar=SCALE, in1=mask, op0=ALU.mult, op1=ALU.add)
                        own.link(ins)
                        dve.reduce_max(s_neg[:, 0:1], s[:, 0:S_W], AX, negate=True)
                        own.link(dve.reduce_max(s_neg[:, 1:2], s[:, S_W:], AX, negate=True))
                        dve.sem_inc(max_ready, 1)
                        dve.tensor_copy(pT[0:NCS, 14, :], one_wait(dve, b, cmp_pT))
                        dve.wait_ge(exp_ready, b * 2 + 2)
                        own.link(dve.reciprocal(s_sum[:, :], s_sum[:, :]))
                        own.link(dve.tensor_tensor(s_sum[:, :], s_sum[:, :], one(gates_ht[:, bass.ds(b, 1), 1:3]), ALU.mult))
                        for n, (a, z) in enumerate(((0, S_W), (S_W, S_W + WIN + NS))):
                            dve.tensor_scalar(s[:, a:z], s[:, a:z], s_sum[:, n:n + 1], None, ALU.mult).then_inc(p_ready, 1)
                        copy_probs(dve, dve.tensor_copy, 1, b)
                        dve.wait_ge(o_made, b + 1)
                        for h in range(2):
                            rows = slice(64 * h, 64 * h + 64)
                            own.link(dve.tensor_copy(
                                oT_s[rows, :, bass.ds(b * NT, NT)],
                                bank[3][rows, 256:384].rearrange("p (c g n) -> p c g n", c=2, g=2)[:, :, h, :].rearrange("p c (j t) -> p c j t", t=NT)))
                        dve.sem_inc(o_kept, 1)

                    def one_wait(eng, b, src):
                        eng.wait_ge(o_made, b)
                        return src[:, bass.ds(b, 1), :].rearrange("p o n -> p (o n)")

                    with dve.Fori(0, NB // 2) as i:
                        with own.loop(i, NB // 2, 12):
                            for u in range(2):
                                step(i * 2 + u, u, i)

        end_of_era()
        mix = sb(attn, "mix", [P, TILES, D])
        with ExitStack() as scope:
            s = sb(scope, "ps", [P, 2, NJ, SEQ])
            s_c = sb(scope, "ps_c", [P, NJ, NCP])
            stat = sb(scope, "p_stat", [P, 4, 3, NJ])
            pT = sb(scope, "p_pT", [P, 20, P])
            o_part = sb(scope, "o_part", [P, 3, NJ * HD])
            scored, max_ready, centred, exp_ready, exp_c_ready, c_ready, o_made, o_taken = (sem("p_" + x) for x in (
                "scored", "max_ready", "centred", "exp_ready", "exp_c_ready", "c_ready", "o_made", "o_taken"))
            turned = [sem(f"p_turned{v}") for v in range(2)]
            copied = [sem(f"p_copied{v}") for v in range(2)]
            STEPS = [(r, g) for r in range(2) for g in range(NG)]

            def blocks_of(r):
                todo = [((kind * NJ + j) * (r + 1) + k, s[:, kind, j, k * P:k * P + P], P)
                        for kind in range(2) for j in range(NJ) for k in range(r + 1)]
                todo += [(2 * NJ * (r + 1) + j, s_c[:, j, :], NCP) for j in range(NJ)]
                return [todo[a:a + 4] for a in range(0, len(todo), 4)]

            BEFORE = []
            for r, g in STEPS:
                BEFORE.append(BEFORE[-1] + nblk if BEFORE else 0)
                nblk = len(blocks_of(r))
            half_up = lambda n, v: (n + 1 - v) // 2

            with nc.Block() as block:
                @block.tensor
                def _(pe):
                    for n, (r, g) in enumerate(STEPS):
                        c, half = g // 2, slice(64 * (g % 2), 64 * (g % 2) + 64)
                        keys, rows = (r + 1) * P, slice(r * P, r * P + P)
                        if n:
                            pe.wait_ge(o_taken, n)
                        for kind in range(2):
                            for j in range(NJ):
                                pe.matmul(bank2[kind][:, SEQ * j:SEQ * j + keys], qrT[half, 4 * c + j, rows],
                                          kT[half, 2 * kind + c, 0:keys], start=True, stop=True)
                        for j in range(NJ):
                            mm = pe.matmul(bank[4][:, NCP * j:NCP * j + NCP], qT[half, 4 * c + j, rows], kcT_p[half, c, :],
                                           start=True, stop=True)
                        mm.then_inc(scored, 1)
                        pe.wait_ge(exp_ready, 2 * NJ * (n + 1))
                        pe.wait_ge(c_ready, n + 1)
                        for m, blocks in enumerate(blocks_of(r)):
                            k = BEFORE[n] + m
                            if k >= 2:
                                pe.wait_ge(copied[k % 2], k // 2)
                            for x, (slot, src, width) in enumerate(blocks):
                                mm = pe.transpose(bank[6 + k % 2][0:width, x * P:x * P + P], src, ident)
                            mm.then_inc(turned[k % 2], 1)
                        k = BEFORE[n] + len(blocks_of(r))
                        for v in range(2):
                            pe.wait_ge(copied[v], half_up(k, v))
                        for kind, col in enumerate((C_VS, C_VW)):
                            for j in range(NJ):
                                for kt in range(r + 1):
                                    pe.matmul(bank[5][:, (kind * NJ + j) * HD:(kind * NJ + j) * HD + HD],
                                              pT[:, (kind * NJ + j) * (r + 1) + kt, :], Z[:, kt, col + HD * g:col + HD * g + HD],
                                              start=(kt == 0), stop=(kt == r))
                        for j in range(NJ):
                            mm = pe.matmul(bank[4][:, 64 + HD * j:128 + HD * j], pT[0:NCP, 2 * NJ * (r + 1) + j, :],
                                           vc_p[:, HD * g:HD * g + HD], start=True, stop=True)
                        mm.then_inc(o_made, 1)

                def copy_blocks(eng, copy, v, n, r):
                    for m, blocks in enumerate(blocks_of(r)):
                        k = BEFORE[n] + m
                        if k % 2 != v:
                            continue
                        eng.wait_ge(turned[v], k // 2 + 1)
                        w, slot = blocks[0][2], blocks[0][0]
                        copy(pT[0:w, slot:slot + len(blocks), :],
                             bank[6 + v][0:w, 0:len(blocks) * P].rearrange("p (k r) -> p k r", r=P)).then_inc(copied[v], 1)

                @block.scalar
                def _(act):
                    for n, (r, g) in enumerate(STEPS):
                        keys = (r + 1) * P
                        act.wait_ge(centred, n + 1)
                        act.activation(s_c[:, :, :], s_c[:, :, :], ACT.Exp).then_inc(exp_c_ready, 1)
                        act.wait_ge(max_ready, n + 1)
                        for kind in range(2):
                            for j in range(NJ):
                                act.activation(s[:, kind, j, 0:keys], s[:, kind, j, 0:keys], ACT.Exp, bias=stat[:, 0, kind, j:j + 1],
                                               accum_out=stat[:, 1, kind, j:j + 1]).then_inc(exp_ready, 1)
                        copy_blocks(act, act.copy, 0, n, r)

                @block.vector
                def _(dve):
                    own = dve_steps.on(dve)
                    for n, (r, g) in enumerate(STEPS):
                        keys = (r + 1) * P
                        causal = cst("causal", to="p (r k) -> p r k", r=2)[:, r, 0:keys].unsqueeze(1).to_broadcast([P, NJ, keys])
                        c_add = cst("cmp_add", to="p (r k) -> p r k", r=2)[:, r, :].unsqueeze(1).to_broadcast([P, NJ, NCP])
                        c_mul = cst("cmp_mul", to="p (r k) -> p r k", r=2)[:, r, :].unsqueeze(1).to_broadcast([P, NJ, NCP])
                        dve.wait_ge(scored, n + 1)
                        dve.scalar_tensor_tensor(out=s_c[:, :, :], in0=bank[4][:, 0:NJ * NCP].rearrange("p (j k) -> p j k", j=NJ),
                                                 scalar=SCALE, in1=c_add, op0=ALU.mult, op1=ALU.add)
                        for kind in range(2):
                            ins = dve.scalar_tensor_tensor(out=s[:, kind, :, 0:keys], in0=bank2[kind][:, :].rearrange("p (j k) -> p j k", j=NJ)[:, :, 0:keys],
                                                           scalar=SCALE, in1=causal, op0=ALU.mult, op1=ALU.add)
                        own.link(ins)
                        own.link(dve.reduce_max(stat[:, 0, 2, :], s_c[:, :, :], AX))
                        dve.tensor_tensor(s_c[:, :, :], s_c[:, :, :], stat[:, 0, 2, :].unsqueeze(2).to_broadcast([P, NJ, NCP]),
                                          ALU.subtract).then_inc(centred, 1)
                        dve.reduce_max(stat[:, 0, 0:2, :], s[:, :, :, 0:keys], AX, negate=True).then_inc(max_ready, 1)
                        dve.wait_ge(exp_c_ready, n + 1)
                        dve.tensor_tensor(s_c[:, :, :], s_c[:, :, :], c_mul, ALU.mult).then_inc(c_ready, 1)
                        dve.wait_ge(c_ready, n + 1)
                        own.link(dve.reduce_sum(stat[:, 1, 2, :], s_c[:, :, :], AX))
                        dve.wait_ge(exp_ready, 2 * NJ * (n + 1))
                        copy_blocks(dve, dve.tensor_copy, 1, n, r)
                        own.link(dve.tensor_scalar(stat[:, 2], stat[:, 1], 1e-30, None, ALU.max))
                        own.link(dve.reciprocal(stat[:, 2], stat[:, 2]))
                        gate = Z[:, r, C_G + 12 * g:C_G + 12 * g + 12].rearrange("p (j c) -> p c j", c=3)
                        dve.tensor_tensor(stat[:, 3, 2, :], stat[:, 2, 2, :], gate[:, 0, :], ALU.mult)
                        own.link(dve.tensor_tensor(stat[:, 3, 0:2, :], stat[:, 2, 0:2, :], gate[:, 1:3, :], ALU.mult))
                        dve.wait_ge(o_made, n + 1)
                        for kind, src in enumerate((bank[5][:, 0:256], bank[5][:, 256:512], bank[4][:, 64:320])):
                            ins = dve.tensor_tensor(o_part[:, kind, :].rearrange("p (j d) -> p j d", j=NJ), src.rearrange("p (j d) -> p j d", j=NJ),
                                                    stat[:, 3, kind, :].unsqueeze(2).to_broadcast([P, NJ, HD]), ALU.mult)
                        own.link(ins)
                        dve.sem_inc(o_taken, 1)
                        own.link(dve.tensor_tensor(o_part[:, 0, :], o_part[:, 0, :], o_part[:, 2, :], ALU.add))
                        own.link(dve.tensor_tensor(mix[:, r, 256 * g:256 * g + 256], o_part[:, 0, :], o_part[:, 1, :], ALU.add))

        with ExitStack() as scope:
            w_s = sb(scope, "w_s", [P, SG, P])
            wsT = sb(scope, "wsT", [P, SG, P])
            b_s = sb(scope, "b_s", [SG, P])
            bT = sb(scope, "bT", [P, SG])
            rep = sb(scope, "rep_s", [NS, SG * NT + SG])
            bd = sb(scope, "w_bd", [NS, SG, NB, NT])
            jobs = []
            for c in range(2):
                dst = mix[0:NS, 2, 512 * c:512 * c + 512].rearrange("p (g j d) -> p j g d", g=2, j=NJ)
                jobs.append(([(P, NS, j * P, oT_s[:, 4 * c + j, :]) for j in range(NJ)],
                             [(dst[:, j], (lambda j: lambda b: b[0:NS, j * P:j * P + P].rearrange("p (g d) -> p g d", g=2))(j)) for j in range(NJ)]))
            for m in range(2):
                jobs.append(([(P, P, k * P, w_s[:, 4 * m + k, :]) for k in range(4)],
                             [(wsT[:, 4 * m:4 * m + 4, :], bank_view(4))]))
            jobs.append(([(SG, P, 0, b_s[:, :])], [(bT[:, :], lambda b: b[:, 0:SG])]))
            transpose_jobs("sgu", jobs, loads=[(w_s[:, :, :], A["w_sgu"][0].rearrange("g t s -> t g s")), (b_s[:, :], A["b_sgu"][0])])

            masked, rep_made, bd_ready, mixed = (sem("sgu_" + x) for x in ("masked", "rep_made", "bd_ready", "mixed"))
            with nc.Block() as block:
                @block.gpsimd
                def _(pool):
                    pool.memset(mix[NS:P, 2, :], 0.0)

                @block.vector
                def _(dve):
                    own = dve_steps.on(dve)
                    dve.tensor_tensor(wsT[:, :, :], wsT[:, :, :], cst("tri").unsqueeze(1).to_broadcast([P, SG, P]), ALU.mult).then_inc(masked, 1)
                    dve.wait_ge(rep_made, 1)
                    own.link(dve.tensor_copy(rep[:, :], bank[4][0:NS, 0:SG * NT + SG]))
                    same_b = cst("same_b", to="p (b t) -> p b t", b=NB)
                    for g in range(SG):
                        dve.tensor_tensor(bd[:, g], same_b[0:NS], rep[:, NT * g:NT * g + NT].unsqueeze(1).to_broadcast([NS, NB, NT]),
                                          ALU.mult).then_inc(bd_ready, 1)
                    for r in range(TILES):
                        rows = P if r < 2 else NS
                        dve.wait_ge(mixed, r + 1)
                        for g in range(SG):
                            bias = bT[:, g:g + 1] if r < 2 else rep[:, SG * NT + g:SG * NT + g + 1]
                            b = (0, 2, 5)[r] + g // 4
                            dve.scalar_tensor_tensor(out=mix[0:rows, r, SW + P * g:SW + P * g + P], in0=bank[b][0:rows, P * (g % 4):P * (g % 4) + P],
                                                     scalar=bias, in1=Z[0:rows, r, C_U + P * g:C_U + P * g + P], op0=ALU.add, op1=ALU.mult)

                @block.tensor
                def _(pe):
                    pe.matmul(bank[4][0:NS, SG * NT:SG * NT + SG], cst("rep")[0:NT, :], bT[0:NT, :], start=True, stop=True)
                    pe.wait_ge(masked, 1)
                    for g in range(SG):
                        mm = pe.matmul(bank[4][0:NS, NT * g:NT * g + NT], cst("rep")[0:NT, :], wsT[0:NT, g, 0:NT], start=True, stop=True)
                    mm.then_inc(rep_made, 1)
                    for r in range(TILES):
                        rows = P if r < 2 else NS
                        if r == 2:
                            pe.wait_ge(bd_ready, SG)
                        for g in range(SG):
                            b = (0, 2, 5)[r] + g // 4
                            lhsT = wsT[:, g, :] if r < 2 else bd[:, g].rearrange("p b t -> p (b t)")
                            mm = pe.matmul(bank[b][0:rows, P * (g % 4):P * (g % 4) + P], lhsT,
                                           Z[0:rows, r, C_V + P * g:C_V + P * g + P], start=True, stop=True)
                        mm.then_inc(mixed, 1)

        end_of_era()
        mix_scope = top.enter_context(ExitStack())
        mixT = mix_scope.enter_context(nc.sbuf_tensor("mixT", [P, KC, TILES * P], F32, side="right"))
        norm_transpose("mix", [(mix[:, r, :], gain_mix, mixT[:, :, r * P:(r + 1) * P], None) for r in range(TILES)],
                       [(0, SW), (SW, D)])
        attn.close()
        x = sb(top, "x", [P, TILES, D])
        x_again = sem("x_again")
        with nc.Block() as block:
            @block.sync
            def _(sp):
                sp.dma_start(x[0:NS, 2, :], A["x_sample"].rearrange("b t n -> (b t) n")).then_inc(x_again, 16)
                sp.dma_start(x[:, 0:2, :], A["x_prompt"][0].rearrange("(r p) n -> p r n", p=P)).then_inc(x_again, 16)
                sp.wait_ge(x_again, 32)

            @block.vector
            def _(dve):
                dve.memset(x[NS:P, 2, :], 0.0)
        with ExitStack() as scope:
            wbuf = sb(scope, "w_out_buf", [P, 2, KC, 512])
            w_out = w_view("w_out")
            project("w_out", mixT, TILES, (2, lambda i, u: (w_out[:, :, bass.ds(i * 1024 + u * 512, 512)], 512,
                                                          lambda r: x[:, r, bass.ds(i * 1024 + u * 512, 512)]), []), wbuf, residual=True)

        mix_scope.close()
        with ExitStack() as era:
            o_mT = sb(era, "o_mT", [P, MH, TILES * P])
            with ExitStack() as scope:
                hqT = sb(scope, "hqT", [P, MH, TILES * P])
                with ExitStack() as inner:
                    hT = sb(inner, "hT_mem", [P, KC, TILES * P])
                    w_q = sb(inner, "w_q", [P, KC, MW])
                    norm_transpose("mem", [(x[:, r, :], gain_mem, hT[:, :, r * P:(r + 1) * P], None) for r in range(TILES)], [(0, D)])
                    wq_loaded, hq_made = sem("wq_loaded"), sem("hq_made")
                    with nc.Block() as block:
                        @block.sync
                        def _(sp):
                            sp.dma_start(w_q[:, :, :], w_view("w_mem_q")).then_inc(wq_loaded, 16)

                        @block.tensor
                        def _(pe):
                            pe.wait_ge(wq_loaded, 16)
                            for h in range(MH):
                                for c in range(KC):
                                    mm = pe.matmul(bank[h][:, 0:TILES * P], w_q[:, c, h * MD:(h + 1) * MD], hT[:, c, :],
                                                   start=(c == 0), stop=(c == KC - 1))
                                mm.then_inc(hq_made, 1)

                        @block.vector
                        def _(dve):
                            for h in range(MH):
                                dve.wait_ge(hq_made, h + 1)
                                dve.tensor_copy(hqT[:, h, :], bank[h][:, 0:TILES * P])

                m_keyT = sb(scope, "m_keyT", [P, MH, NB, NMEM])
                m_v = sb(scope, "m_v", [P, NB, 2, MW])
                with ExitStack() as inner:
                    m_k = sb(inner, "m_k", [P, NB, 2, MW])
                    jobs = []
                    for b in range(NB):
                        for k in range(2):
                            jobs.append(([(P, P, h * P, m_k[:, b, k, h * MD:(h + 1) * MD]) for h in range(MH)],
                                         [(m_keyT[:, :, b, k * P:(k + 1) * P], bank_view(4))]))
                    tiled = lambda name, b: A[name][0, b].rearrange("(k p) h d -> p k (h d)", p=P)
                    transpose_jobs("m_keys", jobs, loads=[(m_k[:, b], tiled("cache_mem_k", b)) for b in range(NB)]
                                   + [(m_v[:, b], tiled("cache_mem_v", b)) for b in range(NB)])
                q_bd = sb(scope, "m_q_bd", [P, NB * MH, P])
                s = sb(scope, "m_s", [P, MH, NMEM])
                stat = sb(scope, "m_stat", [P, 2, MH])
                pT = sb(scope, "m_pT", [P, 2 * MH, P])
                bd_ready, scored, max_ready, exp_ready, p_ready, o_made, o_kept = (sem("m_" + n) for n in (
                    "bd_ready", "scored", "max_ready", "exp_ready", "p_ready", "o_made", "o_kept"))
                turned = [sem(f"m_turned{v}") for v in range(2)]
                copied = [sem(f"m_copied{v}") for v in range(2)]
                PARTS = [MH, MH, 1, 1]
                BLOCKS = [[[(2 * j + k, j, k) for j in range(a, min(a + 2, n)) for k in range(2)] for a in range(0, n, 2)] for n in PARTS]
                M_BEFORE = [sum(len(x) for x in BLOCKS[:n]) for n in range(5)]
                E_BEFORE = [sum(PARTS[:n]) for n in range(5)]
                half_up = lambda n, v: (n + 1 - v) // 2
                with nc.Block() as block:
                    @block.tensor
                    def _(pe):
                        for n in range(4):
                            if n < 2:
                                for h in range(MH):
                                    mm = pe.matmul(bank2[0][:, NMEM * h:NMEM * h + NMEM], hqT[:, h, n * P:(n + 1) * P], mem_kT[:, h, :],
                                                   start=True, stop=True)
                            else:
                                pe.wait_ge(bd_ready, MH)
                                for k in range(4 * MH):
                                    b, h = 4 * (n - 2) + k // MH, k % MH
                                    mm = pe.matmul(bank[0][:, 0:NMEM], q_bd[:, b * MH + h, :], m_keyT[:, h, b, :],
                                                   start=(k == 0), stop=(k == 4 * MH - 1))
                            mm.then_inc(scored, 1)
                            pe.wait_ge(p_ready, n + 1)
                            for m, blocks in enumerate(BLOCKS[n]):
                                k = M_BEFORE[n] + m
                                if k >= 2:
                                    pe.wait_ge(copied[k % 2], k // 2)
                                for y, (slot, j, kt) in enumerate(blocks):
                                    mm = pe.transpose(bank[2 + k % 2][:, y * P:y * P + P], s[:, j, kt * P:kt * P + P], ident)
                                mm.then_inc(turned[k % 2], 1)
                            for v in range(2):
                                pe.wait_ge(copied[v], half_up(M_BEFORE[n + 1], v))
                            if n:
                                pe.wait_ge(o_kept, n)
                            if n < 2:
                                for h in range(MH):
                                    for kt in range(2):
                                        mm = pe.matmul(bank[4][:, h * P:h * P + P], mem_kv[:, kt, MW + h * MD:MW + (h + 1) * MD],
                                                       pT[:, 2 * h + kt, :], start=(kt == 0), stop=(kt == 1))
                            else:
                                for k in range(4 * MH):
                                    b, h = k // MH, k % MH
                                    for kt in range(2):
                                        mm = pe.matmul(bank[4][:, 32 * h + NT * b:32 * h + NT * b + NT], m_v[:, 4 * (n - 2) + b, kt, h * MD:(h + 1) * MD],
                                                       pT[:, kt, NT * k:NT * k + NT], start=(kt == 0), stop=(kt == 1))
                            mm.then_inc(o_made, 1)

                    def copy_blocks(eng, copy, v, n):
                        for m, blocks in enumerate(BLOCKS[n]):
                            k = M_BEFORE[n] + m
                            if k % 2 == v:
                                eng.wait_ge(turned[v], k // 2 + 1)
                                copy(pT[:, blocks[0][0]:blocks[-1][0] + 1, :],
                                     bank[2 + v][:, 0:len(blocks) * P].rearrange("p (k r) -> p k r", r=P)).then_inc(copied[v], 1)

                    @block.scalar
                    def _(act):
                        for n in range(4):
                            act.wait_ge(max_ready, n + 1)
                            for j in range(PARTS[n]):
                                act.activation(s[:, j, :], s[:, j, :], ACT.Exp, bias=stat[:, 0, j:j + 1],
                                               accum_out=stat[:, 1, j:j + 1]).then_inc(exp_ready, 1)
                            copy_blocks(act, act.copy, 0, n)

                    @block.vector
                    def _(dve):
                        own = dve_steps.on(dve)
                        own.link(dve.memset(q_bd[:, :, :], 0.0))
                        for h in range(MH):
                            q = q_bd[:, :, :].rearrange("p (m b h) r -> p m b h r", m=2, h=MH)
                            for m in range(2):
                                for b in range(4):
                                    ins = dve.tensor_copy(q[:, m, b, h, 32 * b + NT * h:32 * b + NT * h + NT],
                                                          hqT[:, h, 256 + 32 * m + NT * b:256 + 32 * m + NT * b + NT])
                            ins.then_inc(bd_ready, 1)
                        for n in range(4):
                            parts = PARTS[n]
                            dve.wait_ge(scored, n + 1)
                            src = bank2[0][:, 0:parts * NMEM].rearrange("p (j k) -> p j k", j=parts)
                            own.link(dve.tensor_scalar(s[:, 0:parts, :], src, MSCALE, None, ALU.mult))
                            dve.reduce_max(stat[:, 0, 0:parts], s[:, 0:parts, :], AX, negate=True).then_inc(max_ready, 1)
                            dve.wait_ge(exp_ready, E_BEFORE[n + 1])
                            own.link(dve.reciprocal(stat[:, 1, 0:parts], stat[:, 1, 0:parts]))
                            dve.tensor_tensor(s[:, 0:parts, :], s[:, 0:parts, :], stat[:, 1, 0:parts].unsqueeze(2).to_broadcast([P, parts, NMEM]),
                                              ALU.mult).then_inc(p_ready, 1)
                            copy_blocks(dve, dve.tensor_copy, 1, n)
                            dve.wait_ge(o_made, n + 1)
                            if n < 2:
                                ins = dve.tensor_copy(o_mT[:, :, n * P:(n + 1) * P], bank[4].rearrange("p (h r) -> p h r", h=MH))
                            else:
                                a = 256 + 32 * (n - 2)
                                ins = dve.tensor_copy(o_mT[:, :, a:a + 32], bank[4][:, 0:P].rearrange("p (h r) -> p h r", h=MH))
                            ins.then_inc(o_kept, 1)
                        dve.memset(o_mT[:, :, 256 + NS:], 0.0)
            with ExitStack() as scope:
                wbuf = sb(scope, "w_o_buf", [P, 2, MH, 512])
                w_o = A["w_mem_o"][0].rearrange("(c p) n -> p c n", p=P)
                project("w_mem_o", o_mT, TILES, (2, lambda i, u: (w_o[:, :, bass.ds(i * 1024 + u * 512, 512)], 512,
                                                                lambda r: x[:, r, bass.ds(i * 1024 + u * 512, 512)]), []), wbuf,
                        residual=True, chunks=MH)

        end_of_era()
        pairs = sb(top, "pairs", [1, 1], I32)
        with ExitStack() as scope:
            hT = sb(scope, "hT_moe", [P, KC, TILES * P])
            norm_transpose("moe", [(x[:, r, :], gain_moe, hT[:, :, r * P:(r + 1) * P], None) for r in range(TILES)], [(0, D)],
                           stores=[(scratch["hn"][r * P:r * P + (P if r < 2 else NS)], P if r < 2 else NS) for r in range(TILES)])
            w_r = sb(scope, "w_r", [P, KC, 20])
            lg = sb(scope, "lg", [P, TILES, 20])
            t4 = sb(scope, "t4", [P, TILES, 4, 4])
            eg = sb(scope, "eg", [P, TILES, 4])
            oh = sb(scope, "oh", [P, 3, TILES, 4])
            fl = sb(scope, "fl", [P, 2, TILES, 4])
            m = sb(scope, "m_", [P, 8, TILES])
            sel = sb(scope, "sel", [P, 3, TILES, NE])
            rank = sb(scope, "rank", [P, TILES, NE])
            pos = sb(scope, "pos", [P, 4, TILES])
            t16 = sb(scope, "t16", [P, TILES, NE])
            pos_i = sb(scope, "pos_i", [P, 2, TILES], I32)
            row = sb(scope, "row", [P, TILES, 2, 4])
            blank = sb(scope, "blank", [P, 49, 4])
            cnt = sb(scope, "cnt", [P, 4])
            wr_loaded, logits_made, g_centred, g_exp, e_centred, e_exp, sel_ready, rank_made, rows_ready, blank_ready, blanked, slotted = (
                sem("r_" + n) for n in ("wr_loaded", "logits_made", "g_centred", "g_exp", "e_centred", "e_exp", "sel_ready", "rank_made",
                                        "rows_ready", "blank_ready", "blanked", "slotted"))
            with nc.Block() as block:
                @block.sync
                def _(sp):
                    sp.dma_start(w_r[:, :, 0:4], w_view("w_router_group")).then_inc(wr_loaded, 16)
                    sp.dma_start(w_r[:, :, 4:20], w_view("w_router_expert")).then_inc(wr_loaded, 16)

                @block.tensor
                def _(pe):
                    pe.wait_ge(wr_loaded, 32)
                    for r in range(TILES):
                        for c in range(KC):
                            mm = pe.matmul(bank[0][:, 20 * r:20 * r + 20], hT[:, c, r * P:(r + 1) * P], w_r[:, c, :],
                                           start=(c == 0), stop=(c == KC - 1))
                    mm.then_inc(logits_made, 1)
                    pe.wait_ge(sel_ready, 1)
                    for r in range(TILES):
                        for q in range(r):
                            pe.matmul(bank[1][:, NE * r:NE * r + NE], cst("ones"), sel[:, 2, q, :], start=(q == 0), stop=False)
                        pe.matmul(bank[1][:, NE * r:NE * r + NE], cst("tri_strict"), sel[:, 2, r, :], start=(r == 0), stop=True)
                    for q in range(TILES):
                        mm = pe.matmul(bank[1][:, 3 * NE:4 * NE], cst("ones"), sel[:, 2, q, :], start=(q == 0), stop=(q == TILES - 1))
                    mm.then_inc(rank_made, 1)

                @block.scalar
                def _(act):
                    act.wait_ge(g_centred, 1)
                    act.activation(eg[:, :, :], eg[:, :, :], ACT.Exp).then_inc(g_exp, 1)
                    act.wait_ge(e_centred, 1)
                    act.activation(m[:, 5, :], m[:, 4, :], ACT.Exp).then_inc(e_exp, 1)

                @block.vector
                def _(dve):
                    own = dve_steps.on(dve)
                    L = own.link
                    wide = lambda v, k: v.unsqueeze(2).to_broadcast([P, TILES, k])
                    first = cst("first").unsqueeze(1).to_broadcast([P, TILES, 4])
                    L(dve.memset(blank[:, :, :], 0.0))
                    dve.tensor_scalar(blank[:, :, 2:3].rearrange("p n o -> p (n o)").bitcast(I32),
                                      cst("token")[:, 0:1].to_broadcast([P, 49]), float(2 * TILES * P), None, ALU.add).then_inc(blank_ready, 1)
                    dve.wait_ge(logits_made, 1)
                    L(dve.tensor_copy(lg[:, :, :], bank[0][:, 0:60].rearrange("p (r n) -> p r n", r=TILES)))
                    g = lg[:, :, 0:4]

                    def first_max(values, at_max, dst):
                        L(dve.tensor_tensor(dst, values, wide(at_max, 4), ALU.is_equal))
                        L(dve.tensor_tensor(dst, dst, first, ALU.mult))
                        L(dve.reduce_max(m[:, 7, :], dst, AX))
                        L(dve.tensor_tensor(dst, dst, wide(m[:, 7, :], 4), ALU.is_equal))

                    L(dve.reduce_max(m[:, 0, :], g, AX))
                    dve.tensor_tensor(eg[:, :, :], g, wide(m[:, 0, :], 4), ALU.subtract).then_inc(g_centred, 1)
                    first_max(g, m[:, 0, :], oh[:, 0])
                    dve.wait_ge(g_exp, 1)
                    L(dve.reduce_sum(m[:, 1, :], eg[:, :, :], AX))
                    L(dve.reciprocal(m[:, 1, :], m[:, 1, :]))
                    for r in range(TILES):
                        ins = dve.tensor_tensor(t4[:, r], lg[:, r, 4:20].rearrange("p (g k) -> p k g", g=4),
                                                oh[:, 0, r, :].unsqueeze(1).to_broadcast([P, 4, 4]), ALU.mult)
                    L(ins)
                    L(dve.reduce_sum(fl[:, 0], t4[:, :, :, :], AX))
                    L(dve.reduce_max(m[:, 2, :], fl[:, 0], AX))
                    first_max(fl[:, 0], m[:, 2, :], oh[:, 1])
                    L(dve.scalar_tensor_tensor(out=fl[:, 1], in0=oh[:, 1], scalar=NEG, in1=fl[:, 0], op0=ALU.mult, op1=ALU.add))
                    L(dve.reduce_max(m[:, 3, :], fl[:, 1], AX))
                    first_max(fl[:, 1], m[:, 3, :], oh[:, 2])
                    dve.tensor_tensor(m[:, 4, :], m[:, 3, :], m[:, 2, :], ALU.subtract).then_inc(e_centred, 1)
                    for k in range(2):
                        for r in range(TILES):
                            ins = dve.tensor_tensor(sel[:, k, r].rearrange("p (g j) -> p g j", g=4), oh[:, 0, r, :].unsqueeze(2).to_broadcast([P, 4, 4]),
                                                    oh[:, 1 + k, r, :].unsqueeze(1).to_broadcast([P, 4, 4]), ALU.mult)
                    L(ins)
                    L(dve.tensor_tensor(sel[:, 2], sel[:, 0], sel[:, 1], ALU.add))
                    dve.tensor_tensor(sel[:, 2], sel[:, 2], wide(cst("valid"), NE), ALU.mult).then_inc(sel_ready, 1)
                    dve.wait_ge(e_exp, 1)
                    L(dve.tensor_scalar(m[:, 6, :], m[:, 5, :], 1.0, None, ALU.add))
                    L(dve.reciprocal(m[:, 6, :], m[:, 6, :]))
                    L(dve.tensor_tensor(row[:, :, 0, 1], m[:, 6, :], m[:, 1, :], ALU.mult))
                    L(dve.tensor_tensor(row[:, :, 1, 1], row[:, :, 0, 1], m[:, 5, :], ALU.mult))
                    dve.wait_ge(rank_made, 1)
                    L(dve.tensor_copy(rank[:, :, :], bank[1][:, 0:3 * NE].rearrange("p (r e) -> p r e", r=TILES)))
                    for k in range(2):
                        L(dve.tensor_tensor(t16[:, :, :], rank[:, :, :], sel[:, k], ALU.mult))
                        L(dve.reduce_sum(pos[:, 0, :], t16[:, :, :], AX))
                        L(dve.tensor_tensor(t16[:, :, :], cst("slot0").unsqueeze(1).to_broadcast([P, TILES, NE]), sel[:, k], ALU.mult))
                        L(dve.reduce_sum(pos[:, 1, :], t16[:, :, :], AX))
                        L(dve.tensor_tensor(pos[:, 1, :], pos[:, 1, :], pos[:, 0, :], ALU.add))
                        for n in range(1, TILES):
                            L(dve.tensor_scalar(pos[:, 2, :], pos[:, 0, :], n * P - 0.5, float((NE - 1) * P), ALU.is_gt, ALU.mult))
                            L(dve.tensor_tensor(pos[:, 1, :], pos[:, 1, :], pos[:, 2, :], ALU.add))
                        dve.tensor_copy(pos_i[:, k, :], pos[:, 1, :])
                        dve.tensor_copy(row[:, :, k, 0].bitcast(I32), cst("token"))
                        L(dve.tensor_scalar(row[:, :, k, 2].bitcast(I32), cst("token"), float(k * TILES * P), None, ALU.add))
                        L(dve.memset(row[:, :, k, 3], 0.0))
                    dve.sem_inc(rows_ready, 1)
                    L(dve.reduce_max(cnt[:, 0:1], bank[1][:, 3 * NE:4 * NE], AX))
                    L(dve.tensor_scalar(cnt[:, 1:2], cnt[:, 0:1], P + 0.5, None, ALU.is_gt))
                    L(dve.tensor_scalar(cnt[:, 2:3], cnt[:, 0:1], 2 * P + 0.5, None, ALU.is_gt))
                    L(dve.tensor_tensor(cnt[:, 1:2], cnt[:, 1:2], cnt[:, 2:3], ALU.add))
                    L(dve.tensor_scalar(pairs[0:1, 0:1], cnt[0:1, 1:2], NE / 2.0, NE / 2.0, ALU.mult, ALU.add))

                @block.gpsimd
                def _(pool):
                    pool.wait_ge(blank_ready, 1)
                    pool.dma_start(scratch["slots"].rearrange("(n p) c -> p n c", p=P), blank[:, :, :]).then_inc(blanked, 16)
                    pool.wait_ge(blanked, 16)
                    pool.wait_ge(rows_ready, 1)
                    for k in range(2):
                        for r in range(TILES):
                            rows = P if r < 2 else NS
                            pool.indirect_dma_start(out=scratch["slots"], out_offset=bass.IndirectOffsetOnAxis(ap=pos_i[0:rows, k, r:r + 1], axis=0),
                                                    in_=row[0:rows, r, k, :], in_offset=None).then_inc(slotted, 16)
                    pool.wait_ge(slotted, 16 * 2 * TILES)

        with ExitStack() as scope:
            w_g = sb(scope, "w_g", [P, KC, FF])
            w_u = sb(scope, "w_u", [P, KC, FF])
            w_d = sb(scope, "w_d", [P, 4, D])
            slot = sb(scope, "slot", [P, 2, 4])
            rows_in = sb(scope, "rows_in", [P, 2, D])
            hT = sb(scope, "hT_e", [P, 2, KC, P])
            gate = sb(scope, "gate", [P, FF])
            act_w = sb(scope, "act_w", [P, FF])
            actT = sb(scope, "actT", [P, 4, P])
            y = sb(scope, "y", [P, D])
            gu_loaded, gu_used, d_loaded, d_used = ([sem(f"e_{n}{q}") for q in range(4)] for n in ("gu_loaded", "gu_used", "d_loaded", "d_used"))
            h_turned, h_copied, gu_made, silu_ready, act_ready, a_turned, a_copied, y_made, y_copied_a, y_copied_d, y_stored = (
                sem("e_" + n) for n in ("h_turned", "h_copied", "gu_made", "silu_ready", "act_ready", "a_turned", "a_copied", "y_made",
                                        "y_copied_a", "y_copied_d", "y_stored"))
            slot_loaded = [sem(f"e_slot_loaded{v}") for v in range(2)]
            gathered = [sem(f"e_gathered{v}") for v in range(2)]

            def turns(eng, body):
                n = eng.value_load(pairs[0:1, 0:1], min_val=NE // 2, max_val=TILES * NE // 2)
                with eng.Fori(0, n) as i:
                    for u in range(2):
                        body(i * 2 + u, u, i)

            with nc.Block() as block:
                @block.sync
                def _(sp):
                    n = sp.value_load(pairs[0:1, 0:1], min_val=NE // 2, max_val=TILES * NE // 2)
                    with sp.Fori(0, n, NE // 2) as first:
                        with sp.Fori(0, NE) as e:
                            turn = first * 2 + e
                            g = A["w_exp_gate"][0, bass.ds(e, 1)].rearrange("o (p c) f -> (o p) c f", c=KC)
                            up = A["w_exp_up"][0, bass.ds(e, 1)].rearrange("o (p c) f -> (o p) c f", c=KC)
                            d = A["w_exp_down"][0, bass.ds(e, 1)].rearrange("o (p c) n -> (o p) c n", c=4)
                            for q in range(4):
                                sp.wait_ge(gu_used[q], turn)
                                cs = slice(4 * q, 4 * q + 4)
                                sp.dma_start(w_g[:, cs, :], g[:, cs, :]).then_inc(gu_loaded[q], 16)
                                sp.dma_start(w_u[:, cs, :], up[:, cs, :]).then_inc(gu_loaded[q], 16)
                            for q in range(4):
                                sp.wait_ge(d_used[q], turn)
                                sp.dma_start(w_d[:, q, :], d[:, q, :]).then_inc(d_loaded[q], 16)

                @block.gpsimd
                def _(pool):
                    def gather(turn, u, i):
                        pool.dma_start(slot[:, u, :], scratch["slots"][bass.ds(turn * P, P)]).then_inc(slot_loaded[u], 16)
                        pool.wait_ge(slot_loaded[u], i * 16 + 16)
                        pool.sem_inc(pool_passed, 1)
                        pool.indirect_dma_start(out=rows_in[:, u, :], out_offset=None, in_=scratch["hn"],
                                                in_offset=bass.IndirectOffsetOnAxis(ap=slot[:, u, 0:1].bitcast(I32), axis=0)).then_inc(gathered[u], 16)

                    gather(0, 0, 0)

                    def step(turn, u, i):
                        pool.wait_ge(y_stored, turn * 16)
                        pool.wait_ge(h_turned, turn * 4)
                        gather(turn + 1, 1 - u, i + u)
                        pool.wait_ge(y_copied_a, turn * 2 + 2)
                        pool.wait_ge(y_copied_d, turn * 2 + 2)
                        pool.sem_inc(pool_passed, 1)
                        pool.indirect_dma_start(out=scratch["moe_y"], out_offset=bass.IndirectOffsetOnAxis(ap=slot[:, u, 2:3].bitcast(I32), axis=0),
                                                in_=y[:, :], in_offset=None, bounds_check=2 * TILES * P - 1, oob_is_err=False).then_inc(y_stored, 16)
                    turns(pool, step)
                    pool.wait_ge(gathered[0], 16)

                @block.tensor
                def _(pe):
                    def turn_rows(turn, u, i):
                        pe.wait_ge(gathered[u], i * 16 + 16)
                        for q in range(4):
                            if q >= 2:
                                pe.wait_ge(h_copied, turn * 4 + q - 1)
                            for k in range(4):
                                mm = pe.transpose(bank[6 + q % 2][:, k * P:k * P + P], rows_in[:, u, 4 * q + k:D:KC], ident)
                            mm.then_inc(h_turned, 1)

                    turn_rows(0, 0, 0)

                    def step(turn, u, i):
                        pe.wait_ge(h_copied, turn * 4 + 4)
                        for q in range(4):
                            pe.wait_ge(gu_loaded[q], turn * 32 + 32)
                            for c in range(4 * q, 4 * q + 4):
                                pe.matmul(bank[4], hT[:, u, c, :], w_g[:, c, :], start=(c == 0), stop=(c == KC - 1))
                                mm = pe.matmul(bank[5], hT[:, u, c, :], w_u[:, c, :], start=(c == 0), stop=(c == KC - 1))
                            mm.then_inc(gu_used[q], 1)
                        turn_rows(turn + 1, 1 - u, i + u)
                        pe.wait_ge(act_ready, turn + 1)
                        pe.wait_ge(h_copied, turn * 4 + 7)
                        for k in range(4):
                            mm = pe.transpose(bank[6][:, k * P:k * P + P], act_w[:, k:FF:4], ident)
                        mm.then_inc(a_turned, 1)
                        pe.wait_ge(a_copied, turn + 1)
                        pe.wait_ge(y_copied_a, turn * 2)
                        pe.wait_ge(y_copied_d, turn * 2)
                        for q in range(4):
                            pe.wait_ge(d_loaded[q], turn * 16 + 16)
                            for n in range(4):
                                mm = pe.matmul(bank[n], actT[:, q, :], w_d[:, q, 512 * n:512 * n + 512], start=(q == 0), stop=(q == 3))
                            mm.then_inc(d_used[q], 1)
                    turns(pe, step)

                @block.scalar
                def _(act):
                    def step(turn, u, i):
                        act.wait_ge(gu_used[3], turn + 1)
                        act.wait_ge(act_ready, turn)
                        act.activation(gate[:, :], bank[4], ACT.Silu).then_inc(silu_ready, 1)
                        act.wait_ge(a_turned, turn + 1)
                        act.copy(actT[:, :, :], bank[6].rearrange("p (k r) -> p k r", k=4)).then_inc(a_copied, 1)
                        act.wait_ge(d_used[3], turn + 1)
                        act.wait_ge(y_stored, turn * 16)
                        for n in range(2):
                            act.copy(y[:, 512 * n:512 * n + 512], bank[n]).then_inc(y_copied_a, 1)
                    turns(act, step)

                @block.vector
                def _(dve):
                    def drain(turn, u):
                        for q in range(4):
                            dve.wait_ge(h_turned, turn * 4 + q + 1)
                            dve.tensor_tensor(hT[:, u, 4 * q:4 * q + 4, :], bank[6 + q % 2].rearrange("p (c r) -> p c r", c=4),
                                              gain_moe[:, 4 * q:4 * q + 4].unsqueeze(2).to_broadcast([P, 4, P]), ALU.mult).then_inc(h_copied, 1)

                    drain(0, 0)

                    def step(turn, u, i):
                        dve.wait_ge(silu_ready, turn + 1)
                        dve.scalar_tensor_tensor(out=act_w[:, :], in0=bank[5], scalar=slot[:, u, 1:2], in1=gate[:, :],
                                                 op0=ALU.mult, op1=ALU.mult).then_inc(act_ready, 1)
                        drain(turn + 1, 1 - u)
                        dve.wait_ge(d_used[3], turn + 1)
                        dve.wait_ge(y_stored, turn * 16)
                        for n in range(2, 4):
                            dve.tensor_copy(y[:, 512 * n:512 * n + 512], bank[n]).then_inc(y_copied_d, 1)
                    turns(dve, step)

        with ExitStack() as scope:
            y2 = sb(scope, "y2", [P, 2, TILES, D])
            gf = sb(scope, "gf", [P, D])
            junk = sb(scope, "f_junk", [P, D])
            ms = sb(scope, "f_ms", [P, TILES])
            y_loaded, summed, squared, scaled, rooted, ready, stored = (sem("f_" + n) for n in (
                "y_loaded", "summed", "squared", "scaled", "rooted", "ready", "stored"))
            with nc.Block() as block:
                @block.sync
                def _(sp):
                    n = sp.value_load(pairs[0:1, 0:1], min_val=NE // 2, max_val=TILES * NE // 2)
                    sp.wait_ge(y_stored, n * 32)
                    for r in range(TILES):
                        rows = P if r < 2 else NS
                        for k in range(2):
                            a = (k * TILES + r) * P
                            sp.dma_start(y2[0:rows, k, r, :], scratch["moe_y"][a:a + rows]).then_inc(y_loaded, 16)
                    sp.dma_start(gf[:, :], A["g_final"].partition_broadcast(P)).then_inc(y_loaded, 16)
                    for r in range(TILES):
                        sp.wait_ge(ready, r + 1)
                        dst = out["y_p"][0, r * P:(r + 1) * P] if r < 2 else out["y_s"].rearrange("b t n -> (b t) n")
                        sp.dma_start(dst, x[0:(P if r < 2 else NS), r, :]).then_inc(stored, 16)
                    sp.wait_ge(stored, 16 * TILES)
                    sp.wait_ge(window_out, 32)

                @block.vector
                def _(dve):
                    own = dve_steps.on(dve)
                    dve.wait_ge(y_loaded, 16 * (2 * TILES + 1))
                    for r in range(TILES):
                        rows = P if r < 2 else NS
                        own.link(dve.tensor_tensor(x[0:rows, r, :], x[0:rows, r, :], y2[0:rows, 0, r, :], ALU.add))
                        dve.tensor_tensor(x[0:rows, r, :], x[0:rows, r, :], y2[0:rows, 1, r, :], ALU.add).then_inc(summed, 1)
                    dve.wait_ge(squared, TILES)
                    dve.tensor_scalar(ms[:, :], ms[:, :], 1.0 / D, EPS, ALU.mult, ALU.add).then_inc(scaled, 1)
                    dve.wait_ge(rooted, 1)
                    own.link(dve.reciprocal(ms[:, :], ms[:, :]))
                    for r in range(TILES):
                        dve.scalar_tensor_tensor(out=x[:, r, :], in0=x[:, r, :], scalar=ms[:, r:r + 1], in1=gf[:, :],
                                                 op0=ALU.mult, op1=ALU.mult).then_inc(ready, 1)

                @block.scalar
                def _(act):
                    for r in range(TILES):
                        act.wait_ge(summed, r + 1)
                        if r:
                            act.wait_ge(squared, r)
                        act.activation(junk[:, :], x[:, r, :], ACT.Square, accum_out=ms[:, r:r + 1]).then_inc(squared, 1)
                    act.wait_ge(scaled, 1)
                    act.activation(ms[:, :], ms[:, :], ACT.Sqrt).then_inc(rooted, 1)

_OUTS = [("y_p", (1, SEQ, D)), ("y_s", (NB, NT, D))] \
    + [(k + "_p", (1, 1, SEQ, NG, HD)) for k in ("cmp_k", "cmp_v", "sel_k", "sel_v", "win_k", "win_v")] \
    + [(k + "_p", (1, 1, NMEM, MH, MD)) for k in ("mem_k", "mem_v")] \
    + [(k + "_s", (1, NB, NT, NG, HD)) for k in ("cmp_k", "cmp_v", "sel_k", "sel_v")] \
    + [(k + "_s", (1, NB, WIN, NG, HD)) for k in ("win_k", "win_v")] + [("sgu_v_s", (1, NB, NT, SW))]
_SCRATCH = {"gates": (NS, 48), "hn": (SEQ + NS, D), "slots": ((3 * NE + 1) * P, 4), "moe_y": (2 * TILES * P, D)}


def kernel(**inputs):
    import numpy as _np
    import concourse.bacc as _bacc
    from concourse import mybir as _mybir
    from concourse.bass_utils import run_bass_kernel_spmd as _run

    nc = _bacc.Bacc("TRN2", target_bir_lowering=False, num_devices=1)
    const, const_at = shape_constants()
    arrays, args = {}, {}
    for name, value in list(inputs.items()) + [("const", const)]:
        a = _np.ascontiguousarray(value)
        arrays[f"in_{name}"] = a
        args[name] = nc.dram_tensor(f"in_{name}", a.shape, _mybir.dt.from_np(a.dtype), kind="ExternalInput").ap()
    out = {n: nc.dram_tensor(f"out_{n}", shape, F32, kind="ExternalOutput").ap() for n, shape in _OUTS}
    scratch = {n: nc.dram_tensor(f"scratch_{n}", shape, F32, kind="Internal").ap() for n, shape in _SCRATCH.items()}
    trunk(nc, args, out, scratch, const_at)
    r = _run(nc, [arrays], core_ids=[0])
    return tuple(r.results[0][f"out_{n}"] for n, _ in _OUTS)
```

```python
from contextlib import ExitStack, contextmanager

import concourse.bass as bass
import numpy as np
from concourse import mybir

F32 = mybir.dt.float32
I32 = mybir.dt.int32
ALU = mybir.AluOpType
ACT = mybir.ActivationFunctionType
AX = mybir.AxisListType.X

D = 2048
P = 128
KC = D // P
SEQ = 256
NB = 8
NT = 8
NS = NB * NT
PAST = 1024
PAGE = 128
NPG = PAST // PAGE
NH = 16
HD = 64
NG = 4
NJ = NH // NG
KVW = NG * HD
ROT = 16
STRIDE = 16
CH = 128
NSUB = PAST // STRIDE
NCS = NSUB - 1
NSUBP = SEQ // STRIDE
NCP = NSUBP - 1
LSEL = 64
NBLK = PAST // LSEL
WIN = 512
SW = 1024
SG = 8
IN_COLS = 4656
NMEM = 256
MH = 4
MD = 128
MW = MH * MD
NE = 16
FF = 512
EPS = 1e-6
NEG = -1e30
SCALE = HD ** -0.5
MSCALE = MD ** -0.5
C_Q, C_KC, C_VC, C_KS, C_VS, C_KW, C_VW, C_G, C_U, C_V = 0, 1024, 1280, 1536, 1792, 2048, 2304, 2560, 2608, 3632
TILES = 3


def shape_constants():
    p = np.arange(P)
    rows = np.zeros((TILES, P))
    rows[0], rows[1] = p, P + p
    rows[2] = PAST + p % NT
    freqs = np.float32(500000.0) ** (-np.arange(ROT // 2, dtype=np.float32) / np.float32(ROT // 2))
    ang = rows.astype(np.float32)[:, :, None] * freqs[None, None, :].astype(np.float32)
    cos, sin = np.cos(ang), np.sin(ang)
    t = p % NT
    key = np.arange(SEQ)
    end = np.arange(16) * STRIDE + 31
    q = np.stack([p, P + p], 1)
    bt = np.arange(NS)
    parts = {
        "ident": np.eye(P),
        "causal": np.where(key[None, None, :] <= q[:, :, None], 0.0, NEG),
        "cmp_add": np.where(end[None, None, :NCP] <= q[:, :, None], 0.0, NEG),
        "cmp_mul": np.where(end[None, None, :NCP] <= q[:, :, None], 1.0, 0.0),
        "win_add": np.where(np.arange(WIN)[None, :] > t[:, None], 0.0, NEG),
        "new_add": np.where((bt[None, None, :] // NT == np.arange(NB)[None, :, None])
                            & (bt[None, None, :] % NT <= t[:, None, None]), 0.0, NEG),
        "group": np.where((p[:, None] // 32 == p[None, :] // 32) & (p[:, None] % NT == p[None, :] % NT), 1.0, 0.0),
        "block_id": np.tile(np.arange(NBLK), (P, 1)),
        "cos2": np.concatenate([cos, cos], -1).transpose(1, 0, 2),
        "sin2": np.concatenate([-sin, sin], -1).transpose(1, 0, 2),
        "tri": np.where(p[:, None] <= p[None, :], 1.0, 0.0),
        "tri_strict": np.where(p[:, None] < p[None, :], 1.0, 0.0),
        "ones": np.ones((P, P)),
        "rep": np.where(p[:, None] == bt[None, :] % NT, 1.0, 0.0),
        "same_b": np.where((p[:, None, None] // NT == np.arange(NB)[None, :, None])
                           & (p[:, None, None] % NT <= np.arange(NT)[None, None, :]), 1.0, 0.0),
        "valid": np.stack([np.ones(P), np.ones(P), (p < NS) * 1.0], 1),
        "token": np.stack([p, P + p, 2 * P + p], 1),
        "first": np.tile(4.0 - np.arange(4), (P, 1)),
        "slot0": np.tile(np.arange(NE) * float(P), (P, 1)),
    }
    at, off = {}, 0
    for k, v in parts.items():
        v = v.reshape(P, -1)
        at[k] = (off, v.shape[1])
        off += v.shape[1]
    return np.concatenate([v.reshape(P, -1) for v in parts.values()], 1).astype(np.float32), at


class Steps:

    def __init__(self, sem):
        self.sem, self.n, self.turn, self.eng = sem, 0, 0, None

    def on(self, eng):
        self.eng = eng
        return self

    def link(self, ins):
        self.n += 1
        ins.then_inc(self.sem, 1)
        self.eng.wait_ge(self.sem, self.turn + self.n)

    @contextmanager
    def loop(self, i, turns, per):
        start, self.turn = self.n, i * per
        yield
        assert self.n - start == per, self.n - start
        self.n, self.turn = start + turns * per, 0


def trunk(nc, A, out, scratch, const_at):
    top = ExitStack()
    with top:
        def sb(scope, name, shape, dt=F32):
            return scope.enter_context(nc.sbuf_tensor(name, shape, dt))

        kept_sems, phase_sems = [], []

        def sem(name, keep=False):
            handle = nc.alloc_semaphore(name=name)
            (kept_sems if keep else phase_sems).append(handle)
            return handle

        def end_of_era():
            nc.clear_and_free_semaphores(list(phase_sems))
            phase_sems.clear()
            nc.all_engine_barrier()

        bank2 = [top.enter_context(nc.psum_tensor(f"bank2_{i}", [P, 1024], F32)) for i in range(4)]
        bank = [bank2[i // 2][:, 512 * (i % 2):512 * (i % 2) + 512] for i in range(8)]
        dve_steps, act_steps, pool_steps = Steps(sem("dve_step", True)), Steps(sem("act_step", True)), Steps(sem("pool_step", True))

        pool_passed = sem("pool_passed", True)

        n_const = sum(n for _, n in const_at.values())
        const = sb(top, "const", [P, n_const])

        def cst(name, **dims):
            a, n = const_at[name]
            v = const[:, a:a + n]
            return v.rearrange(dims.pop("to"), **dims) if dims else v

        ident = cst("ident")
        gain_attn = sb(top, "gain_attn", [P, KC])
        gain_src = sb(top, "gain_src", [P, KC])
        gain_mem = sb(top, "gain_mem", [P, KC])
        gain_moe = sb(top, "gain_moe", [P, KC])
        gain_mix = sb(top, "gain_mix", [P, KC])
        mem_kT = sb(top, "mem_kT", [P, MH, NMEM])
        mem_kv = sb(top, "mem_kv", [P, 2, 2 * MW])

        window_out = sem("window_out", True)
        const_loaded = sem("const_loaded")
        with nc.Block() as block:
            @block.sync
            def _(sp):
                sp.dma_start(const[:, :], A["const"]).then_inc(const_loaded, 16)
                for dst, src in ((gain_attn, "g_attn_norm"), (gain_src, "g_mem_src"), (gain_mem, "g_mem_norm"),
                                 (gain_moe, "g_moe_norm")):
                    sp.dma_start(dst[:, :], A[src][0].rearrange("(p c) -> p c", c=KC)).then_inc(const_loaded, 16)
                sp.dma_start(gain_mix[0:64, :], A["g_nsa_out"][0].rearrange("(p c) -> p c", c=KC)).then_inc(const_loaded, 16)
                sp.dma_start(gain_mix[64:128, :], A["g_sgu_out"][0].rearrange("(p c) -> p c", c=KC)).then_inc(const_loaded, 16)
                sp.wait_ge(const_loaded, 16 * 7)

        def norm_transpose(tag, tiles, segs, stores=(), ahead=(), last=()):
            n, ns, width = len(tiles), len(segs), segs[0][1] - segs[0][0]
            squared, scaled, rooted = sem(tag + "_squared"), sem(tag + "_scaled"), sem(tag + "_rooted")
            normed, turned, drained = (sem(tag + x) for x in ("_normed", "_turned", "_drained"))
            stored = [sem(tag + f"_stored{v}") for v in range(2)] if stores else []
            with ExitStack() as scope:
                hn = sb(scope, tag + "_hn", [P, 2, D])
                junk = hn[:, 1, 0:width]
                ms = sb(scope, tag + "_ms", [P, n * ns])
                block = scope.enter_context(nc.Block())

                @block.scalar
                def _(act):
                    for i, (src, _, _, loaded) in enumerate(tiles):
                        if loaded:
                            act.wait_ge(*loaded)
                        for j, (a, b) in enumerate(segs):
                            k = i * ns + j
                            if k:
                                act.wait_ge(squared, k)
                            act.activation(junk, src[:, a:b], ACT.Square,
                                           accum_out=ms[:, k:k + 1]).then_inc(squared, 1)
                    act.wait_ge(scaled, 1)
                    act.activation(ms[:, :], ms[:, :], ACT.Sqrt).then_inc(rooted, 1)

                @block.vector
                def _(dve):
                    own = dve_steps.on(dve)
                    dve.wait_ge(squared, n * ns)
                    dve.tensor_scalar(ms[:, :], ms[:, :], 1.0 / width, EPS, ALU.mult, ALU.add).then_inc(scaled, 1)
                    dve.wait_ge(rooted, 1)
                    own.link(dve.reciprocal(ms[:, :], ms[:, :]))

                    def normalise(i):
                        if i >= 2:
                            dve.wait_ge(turned, 4 * (i - 1))
                            if stores:
                                dve.wait_ge(stored[i % 2], 16 * (i // 2))
                        for j, (a, b) in enumerate(segs):
                            k = i * ns + j
                            dve.tensor_scalar(hn[:, i % 2, a:b], tiles[i][0][:, a:b], ms[:, k:k + 1], None,
                                              ALU.mult).then_inc(normed, 1)

                    def drain(i):
                        for j in range(4):
                            dve.wait_ge(turned, 4 * i + j + 1)
                            dve.tensor_tensor(tiles[i][2][:, 4 * j:4 * j + 4, :],
                                              bank[(i % 2) * 4 + j].rearrange("p (c r) -> p c r", c=4),
                                              tiles[i][1][:, 4 * j:4 * j + 4].unsqueeze(2).to_broadcast([P, 4, P]),
                                              ALU.mult).then_inc(drained, 1)

                    for i in range(n + 1):
                        if i < n:
                            normalise(i)
                        if i >= 1:
                            drain(i - 1)

                @block.tensor
                def _(pe):
                    for i in range(n):
                        pe.wait_ge(normed, ns * (i + 1))
                        if i >= 2:
                            pe.wait_ge(drained, 4 * (i - 1))
                        for c in range(KC):
                            mm = pe.transpose(bank[(i % 2) * 4 + c // 4][:, (c % 4) * P:(c % 4) * P + P],
                                              hn[:, i % 2, c:D:KC], ident)
                            if c % 4 == 3:
                                mm.then_inc(turned, 1)

                if stores or ahead or last:
                    @block.sync
                    def _(sp):
                        for dst, src, loaded in ahead:
                            sp.dma_start(dst, src).then_inc(loaded, 16)
                        for i, (dst, rows) in enumerate(stores):
                            sp.wait_ge(normed, ns * (i + 1))
                            sp.dma_start(dst, hn[0:rows, i % 2, :]).then_inc(stored[i % 2], 16)
                        for v in range(2):
                            if stores:
                                sp.wait_ge(stored[v], 16 * ((len(stores) + 1 - v) // 2))
                        for dst, src, loaded in last:
                            sp.dma_start(dst, src).then_inc(loaded, 16)

        def transpose_jobs(tag, jobs, loads=(), after=None):
            turned = [sem(tag + f"_turned{v}") for v in range(2)]
            copied = [sem(tag + f"_copied{v}") for v in range(2)]
            loaded = sem(tag + "_loaded")
            with nc.Block() as block:
                @block.sync
                def _(sp):
                    for dst, src in loads:
                        sp.dma_start(dst, src).then_inc(loaded, 16)

                @block.tensor
                def _(pe):
                    if loads:
                        pe.wait_ge(loaded, 16 * len(loads))
                    if after:
                        pe.wait_ge(*after)
                    for n, (blocks, _) in enumerate(jobs):
                        b = n % 4
                        if n >= 4:
                            pe.wait_ge(copied[n % 2], n // 2 - 1)
                        for rows, cols, off, src in blocks:
                            mm = pe.transpose(bank[b][0:cols, off:off + rows], src, ident[0:rows, 0:rows])
                        mm.then_inc(turned[n % 2], 1)

                def copies(eng, copy, v):
                    for n, (_, pairs) in enumerate(jobs):
                        if n % 2 != v:
                            continue
                        eng.wait_ge(turned[v], n // 2 + 1)
                        for dst, view in pairs:
                            ins = copy(dst, view(bank[n % 4]))
                        ins.then_inc(copied[v], 1)

                @block.scalar
                def _(act):
                    copies(act, act.copy, 0)

                @block.vector
                def _(dve):
                    copies(dve, dve.tensor_copy, 1)

        def project(tag, hT, toks, plan, wbuf, residual=False, chunks=KC, aside=None, first=None, x_loaded=None):
            loaded = [first if first and u == 0 else sem(tag + f"_w_loaded{u}") for u in range(2)]
            ready = [sem(tag + f"_ready{u}") for u in range(2)]
            copied = [sem(tag + f"_copied{u}") for u in range(2)]
            pairs, tile_of, peeled = plan

            def tiles(eng, body):
                if pairs:
                    with eng.Fori(0, pairs) as i:
                        for u in range(2):
                            body(u, i, *tile_of(i, u))
                for n, tile in enumerate(peeled):
                    body(n % 2, pairs + n // 2, *tile)

            with nc.Block() as block:
                @block.sync
                def _(sp):
                    def load(u, i, w, width, dst):
                        sp.wait_ge(ready[u], i * toks)
                        sp.dma_start(wbuf[u][:, 0:chunks, 0:width], w).then_inc(loaded[u], 16)

                    if not first:
                        tiles(sp, load)
                        return
                    if pairs:
                        w, width, _ = tile_of(0, 1)
                        sp.dma_start(wbuf[1][:, 0:chunks, 0:width], w).then_inc(loaded[1], 16)
                        with sp.Fori(1, pairs) as i:
                            for u in range(2):
                                load(u, i, *tile_of(i, u))
                    for n, tile in enumerate(peeled):
                        if pairs or n:
                            load(n % 2, pairs + n // 2, *tile)

                @block.tensor
                def _(pe):
                    def multiply(u, i, w, width, dst):
                        pe.wait_ge(loaded[u], i * 16 + 16)
                        pe.wait_ge(copied[u], i * toks)
                        for r in range(toks):
                            for c in range(chunks):
                                mm = pe.matmul(bank[4 * u + r][:, 0:width], hT[:, c, r * P:(r + 1) * P],
                                               wbuf[u][:, c, 0:width], start=(c == 0), stop=(c == chunks - 1))
                            mm.then_inc(ready[u], 1)
                    tiles(pe, multiply)

                @block.scalar
                def _(act):
                    if residual:
                        return
                    if aside:
                        act.wait_ge(ready[0], 1)
                        aside(act)

                    def take(u, i, w, width, dst):
                        for r in range(0, toks, 2):
                            act.wait_ge(ready[u], i * toks + r + 1)
                            act.copy(dst(r), bank[4 * u + r][:, 0:width]).then_inc(copied[u], 1)
                    tiles(act, take)

                @block.vector
                def _(dve):
                    if x_loaded:
                        dve.wait_ge(*x_loaded)

                    def take(u, i, w, width, dst):
                        for r in range(0, toks) if residual else range(1, toks, 2):
                            dve.wait_ge(ready[u], i * toks + r + 1)
                            if residual:
                                dve.tensor_tensor(dst(r), bank[4 * u + r][:, 0:width], dst(r), ALU.add).then_inc(copied[u], 1)
                                continue
                            dve.tensor_copy(dst(r), bank[4 * u + r][:, 0:width]).then_inc(copied[u], 1)
                    tiles(dve, take)

        w_view = lambda name: A[name][0].rearrange("(p c) n -> p c n", c=KC)

        with ExitStack() as scope:
            hmT = sb(scope, "hmT", [P, KC, NMEM])
            wbuf = [sb(scope, f"w_mem{u}", [P, KC, 512]) for u in range(2)]
            mem_w_loaded = sem("mem_w_loaded")
            with ExitStack() as inner:
                mem_x = sb(inner, "mem_x", [P, 2, D])
                mem_loaded = sem("mem_loaded")
                with nc.Block() as block:
                    @block.sync
                    def _(sp):
                        sp.dma_start(mem_x[:, :, :], A["mem_prompt"][0].rearrange("(r p) n -> p r n", p=P)).then_inc(mem_loaded, 16)
                norm_transpose("mem_src", [(mem_x[:, r, :], gain_src, hmT[:, :, r * P:(r + 1) * P], (mem_loaded, 16))
                                           for r in range(2)], [(0, D)], ahead=[(wbuf[0][:, :, :], w_view("w_mem_k"), mem_w_loaded)])
            project("mem_kv", hmT, 2, (0, None, [
                (w_view("w_mem_k"), 512, lambda r: mem_kv[:, r, 0:512]),
                (w_view("w_mem_v"), 512, lambda r: mem_kv[:, r, 512:1024])]), wbuf, first=mem_w_loaded)

        attn = top.enter_context(ExitStack())
        Z = sb(attn, "Z", [P, TILES, IN_COLS])
        with ExitStack() as scope:
            hT = sb(scope, "hT", [P, KC, TILES * P])
            wbuf = [sb(scope, "w_in0", [P, KC, 512])]
            w_in = w_view("w_in")
            w_in_loaded = sem("w_in_loaded")
            with ExitStack() as inner:
                x0 = sb(inner, "x0", [P, TILES, D])
                x_loaded = sem("x_loaded")
                with nc.Block() as block:
                    @block.sync
                    def _(sp):
                        sp.dma_start(x0[0:NS, 2, :], A["x_sample"].rearrange("b t n -> (b t) n")).then_inc(x_loaded, 16)
                        for r in range(2):
                            sp.dma_start(x0[:, r, :], A["x_prompt"][0, r * P:(r + 1) * P, :]).then_inc(x_loaded, 16)

                    @block.vector
                    def _(dve):
                        dve.memset(x0[NS:P, 2, :], 0.0)
                norm_transpose("attn", [(x0[:, r, :], gain_attn, hT[:, :, r * P:(r + 1) * P], (x_loaded, 48))
                                        for r in range(TILES)], [(0, D)],
                               ahead=[(wbuf[0][:, :, :], w_in[:, :, 0:512], w_in_loaded)])
            wbuf.append(sb(scope, "w_in1", [P, KC, 512]))

            def shift_windows(act):
                for cache, dst in (("cache_win_k", "win_k_s"), ("cache_win_v", "win_v_s")):
                    act.dma_start(out[dst][0, :, 0:WIN - NT].rearrange("b (s t) g d -> b s (t g d)", s=NT),
                                  A[cache][0, :, NT:WIN].rearrange("b (s t) g d -> b s (t g d)", s=NT)).then_inc(window_out, 16)

            project("w_in", hT, TILES, (4, lambda i, u: (w_in[:, :, bass.ds(i * 1024 + u * 512, 512)], 512,
                                                       lambda r: Z[:, r, bass.ds(i * 1024 + u * 512, 512)]), [
                (w_in[:, :, 4096:4608], 512, lambda r: Z[:, r, 4096:4608]),
                (w_in[:, :, 4608:IN_COLS], 48, lambda r: Z[:, r, 4608:IN_COLS])]), wbuf, aside=shift_windows, first=w_in_loaded)


        qT = sb(attn, "qT", [P, 8, TILES * P])
        qrT = sb(attn, "qrT", [P, 8, TILES * P])
        kT = sb(attn, "kT", [P, 4, TILES * P])
        state_out = sem("state_out")
        with ExitStack() as scope:
            QQ = sb(scope, "QQ", [P, TILES, 1024])
            QR = sb(scope, "QR", [P, TILES, 1024])
            vgain = sb(scope, "vgain", [P, SW])
            with ExitStack() as inner:
                ta = sb(inner, "rope_a", [P, 256])
                tb = sb(inner, "rope_b", [P, 256])
                vjunk = sb(inner, "vjunk", [P, SW])
                vms = sb(inner, "vms", [P, TILES])
                q_copied, v_squared, v_scaled, v_rooted = (sem(x) for x in ("q_copied", "v_squared", "v_scaled", "v_rooted"))
                roped, gated, v_ready, vgain_loaded = (sem(x) for x in ("roped", "gated", "v_ready", "vgain_loaded"))
                block = inner.enter_context(nc.Block())

                @block.scalar
                def _(act):
                    own = act_steps.on(act)
                    for r in range(TILES):
                        for c in range(2):
                            a = C_Q + 512 * c
                            for dst in (QR, QQ):
                                act.copy(dst[:, r, 512 * c:512 * c + 512].rearrange("p (j g d) -> p g j d", j=NJ, g=2),
                                         Z[:, r, a:a + 512].rearrange("p (g j d) -> p g j d", j=NJ, g=2)).then_inc(q_copied, 1)
                    own.link(act.activation(Z[:, :, C_U:IN_COLS], Z[:, :, C_U:IN_COLS], ACT.Gelu_apprx_tanh))
                    for r in range(TILES):
                        if r:
                            act.wait_ge(v_squared, r)
                        act.activation(vjunk[:, :], Z[:, r, C_V:C_V + SW], ACT.Square,
                                       accum_out=vms[:, r:r + 1]).then_inc(v_squared, 1)
                    act.activation(Z[:, :, C_G:C_G + 48], Z[:, :, C_G:C_G + 48], ACT.Sigmoid).then_inc(gated, 1)
                    act.wait_ge(v_scaled, 1)
                    act.activation(vms[:, :], vms[:, :], ACT.Sqrt).then_inc(v_rooted, 1)

                @block.vector
                def _(dve):
                    own = dve_steps.on(dve)
                    cos2 = cst("cos2", to="p (r n) -> p r n", r=TILES)
                    sin2 = cst("sin2", to="p (r n) -> p r n", r=TILES)

                    def rope(x, r, n, like):
                        def over(v):
                            while len(v.shape) < len(x.shape):
                                v = v.unsqueeze(1)
                            return v.to_broadcast(list(x.shape[:-1]) + [v.shape[-1]])
                        a, b = like(ta[:, 0:n * ROT]), like(tb[:, 0:n * ROT])
                        dve.tensor_tensor(a, x, over(cos2[:, r, :]), ALU.mult)
                        ix = tuple([slice(None)] * (len(x.shape) - 1))
                        dve.tensor_tensor(b[ix + (slice(0, 8),)], x[ix + (slice(8, 16),)], over(sin2[:, r, 0:8]), ALU.mult)
                        own.link(dve.tensor_tensor(b[ix + (slice(8, 16),)], x[ix + (slice(0, 8),)], over(sin2[:, r, 8:16]), ALU.mult))
                        own.link(dve.tensor_tensor(x, a, b, ALU.add))

                    dve.wait_ge(q_copied, 4 * TILES)
                    for r in range(TILES):
                        rope(QR[:, r, :].rearrange("p (h d) -> p h d", d=HD)[:, :, 0:ROT], r, NH,
                             lambda v: v.rearrange("p (h d) -> p h d", d=ROT))
                        rope(Z[:, r, C_KS:C_KS + 1024].rearrange("p (k h d) -> p k h d", k=2, d=HD)[:, :, 0:NG, 0:ROT], r, 2 * NG,
                             lambda v: v.rearrange("p (k h d) -> p k h d", k=2, d=ROT))
                    dve.sem_inc(roped, 1)
                    dve.wait_ge(v_squared, TILES)
                    dve.tensor_scalar(vms[:, :], vms[:, :], 1.0 / SW, EPS, ALU.mult, ALU.add).then_inc(v_scaled, 1)
                    dve.wait_ge(v_rooted, 1)
                    own.link(dve.reciprocal(vms[:, :], vms[:, :]))
                    dve.wait_ge(vgain_loaded, 16)
                    for r in range(TILES):
                        v = Z[:, r, C_V:C_V + SW]
                        dve.scalar_tensor_tensor(out=v, in0=v, scalar=vms[:, r:r + 1], in1=vgain[:, :],
                                                 op0=ALU.mult, op1=ALU.mult).then_inc(v_ready, 1)

                @block.sync
                def _(sp):
                    stored = [0]

                    def store(dst, src):
                        stored[0] += 1
                        sp.dma_start(dst, src).then_inc(state_out, 16)

                    sp.dma_start(vgain[:, :], A["g_sgu_v"][0].partition_broadcast(P)).then_inc(vgain_loaded, 16)

                    def state(kind, col):
                        for r in range(2):
                            store(out[kind + "_p"][0, 0, r * P:(r + 1) * P].rearrange("r g d -> r (g d)"),
                                         Z[:, r, col:col + KVW])

                    def state_s(kind, col):
                        store(out[kind + "_s"][0].rearrange("b t g d -> (b t) (g d)"),
                                     Z[0:NS, 2, col:col + KVW])
                    for kind, col in (("cmp_k", C_KC), ("cmp_v", C_VC), ("sel_v", C_VS)):
                        state(kind, col)
                        state_s(kind, col)
                    state("win_v", C_VW)
                    for n, kind in enumerate(("mem_k_p", "mem_v_p")):
                        for r in range(2):
                            store(out[kind][0, 0, r * P:(r + 1) * P].rearrange("r h d -> r (h d)"),
                                         mem_kv[:, r, n * MW:(n + 1) * MW])
                    sp.wait_ge(roped, 1)
                    state("sel_k", C_KS)
                    state_s("sel_k", C_KS)
                    state("win_k", C_KW)
                    for kind, col in (("win_k_s", C_KW), ("win_v_s", C_VW)):
                        for b in range(NB):
                            store(out[kind][0, b, WIN - NT:WIN].rearrange("t g d -> t (g d)"),
                                         Z[b * NT:(b + 1) * NT, 2, col:col + KVW])
                    sp.wait_ge(gated, 1)
                    store(scratch["gates"], Z[0:NS, 2, C_G:C_G + 48])
                    sp.wait_ge(v_ready, TILES)
                    store(out["sgu_v_s"][0].rearrange("b t n -> (b t) n"), Z[0:NS, 2, C_V:C_V + SW])
                    sp.wait_ge(state_out, 16 * stored[0])


            def bank_view(n):
                return lambda b: b[:, 0:n * P].rearrange("p (c r) -> p c r", c=n)

            jobs = []
            for r in range(TILES):
                rows = slice(r * P, (r + 1) * P)
                for src, dst in ((QQ, qT), (QR, qrT)):
                    for c in range(2):
                        jobs.append(([(P, P, j * P, src[:, r, (4 * c + j) * P:(4 * c + j + 1) * P]) for j in range(NJ)],
                                     [(dst[:, 4 * c:4 * c + 4, rows], bank_view(4))]))
                jobs.append(([(P, P, n * P, Z[:, r, col:col + P]) for n, col in enumerate((C_KS, C_KS + P, C_KW, C_KW + P))],
                             [(kT[:, :, rows], bank_view(4))]))
            for r in range(2):
                jobs.append(([(P, P, h * P, mem_kv[:, r, h * MD:(h + 1) * MD]) for h in range(MH)],
                             [(mem_kT[:, :, r * P:(r + 1) * P], bank_view(4))]))
            transpose_jobs("qk", jobs)
        end_of_era()
        kcT = sb(attn, "kcT", [P, 2, NB * NCS])
        kcT_p = sb(attn, "kcT_p", [P, 2, NCP])
        vc = sb(attn, "vc", [NCS, NB, KVW])
        vc_p = sb(attn, "vc_p", [NCP, KVW])
        pages = sb(attn, "pages", [1, NB * NPG], I32)
        pages_loaded = sem("pages_loaded")
        with ExitStack() as scope:
            raw = sb(scope, "raw", [P, 2, STRIDE * KVW // 2])
            rawg = sb(scope, "rawg", [P, 2, STRIDE * KVW // 2])
            subT = sb(scope, "subT", [P, 2, 8, 512])
            w1 = sb(scope, "w1", [P, 2, KC, CH])
            w2k = sb(scope, "w2k", [P, P])
            w2v = sb(scope, "w2v", [P, HD])
            pe_rows = sb(scope, "pe_rows", [KC, 2, P])
            peT = sb(scope, "peT", [P, 2, KC])
            pe_bias = sb(scope, "pe_bias", [P, 2])
            hid = sb(scope, "hid", [P, 504])
            cw_loaded, pe_turned, pe_copied, pe_summed, pe_ready = (sem(x) for x in (
                "cw_loaded", "pe_turned", "pe_copied", "pe_summed", "pe_ready"))
            raw_loaded = sem("raw_loaded")
            regrouped = [sem(f"regrouped{v}") for v in range(2)]
            sub_turned = [[sem(f"sub_turned{e}{v}") for v in range(2)] for e in range(2)]
            sub_copied = [sem(f"sub_copied{v}") for v in range(2)]
            hid_summed, hid_ready, kv_made, kv_kept = (sem(x) for x in ("hid_summed", "hid_ready", "kv_made", "kv_kept"))

            TURNS = NB + 2

            def is_prompt(turn):
                return isinstance(turn, int) and turn >= NB

            def turns(eng, body, own=None, per=0):
                with eng.Fori(0, NB // 2 - 1) as i:
                    with own.loop(i, NB // 2 - 1, per) if own else ExitStack():
                        for u in range(2):
                            body(i * 2 + u, u, i, 9)
                for turn in range(NB - 2, TURNS):
                    body(turn, turn % 2, turn // 2, TURNS - 1 - turn)

            with nc.Block() as block:
                @block.sync
                def _(sp):
                    sp.dma_start(pages[:, :], A["page_table"].rearrange("b n -> (b n)").unsqueeze(0)).then_inc(pages_loaded, 16)
                    for u, kind in enumerate("kv"):
                        sp.dma_start(w1[:, u, :, :], A[f"w_cmp_{kind}1"][0].rearrange("(m p) h -> p m h", p=P)).then_inc(cw_loaded, 16)
                        sp.dma_start(pe_rows[:, u, :], A[f"pe_cmp_{kind}"][0].rearrange("(m l) d -> m (l d)", m=KC)).then_inc(cw_loaded, 16)
                    for n in range(2):
                        sp.dma_start(w2k[:, HD * n:HD * n + HD], A["w_cmp_k2"][0]).then_inc(cw_loaded, 16)
                    sp.dma_start(w2v[:, :], A["w_cmp_v2"][0]).then_inc(cw_loaded, 16)
                    sp.wait_ge(pages_loaded, 16)

                    ids = []

                    def load(turn, u, i, left):
                        name = ("cache_cmp_k", "cache_cmp_v")[u]
                        if u == 0 and not is_prompt(turn):
                            ids.clear()
                            for j in range(2 * NPG):
                                ids.append(sp.value_load(pages[0:1, bass.ds(i * 2 * NPG + j, 1)], min_val=0, max_val=A[name].shape[1] - 1))
                        for v in range(2):
                            sp.wait_ge(regrouped[v], turn)
                        rows = raw[:, :, :].rearrange("p v n -> p (v n)")
                        if is_prompt(turn):
                            src = out[("cmp_k_p", "cmp_v_p")[u]][0, 0].rearrange("(n s) g d -> n (s g d)", s=STRIDE)
                            for n in range(NSUBP):
                                sp.dma_start(rows[n:n + 1, :], src[n:n + 1, :]).then_inc(raw_loaded, 16)
                            return
                        for j in range(2 * NPG):
                            src = A[name][0, bass.ds(ids[j], 1)].rearrange("o (n s) g d -> (o n) (s g d)", s=STRIDE)
                            sp.dma_start(rows[8 * j:8 * j + 8, :], src).then_inc(raw_loaded, 16)
                    turns(sp, load)

                @block.tensor
                def _(pe):
                    pe.wait_ge(cw_loaded, 16 * 7)
                    for u in range(2):
                        mm = pe.transpose(bank[0][:, 16 * u:16 * u + KC], pe_rows[:, u, :], ident[0:KC, 0:KC])
                    mm.then_inc(pe_turned, 1)
                    pe.wait_ge(pe_copied, 1)
                    for u in range(2):
                        for m in range(KC):
                            mm = pe.matmul(bank[1][:, u:u + 1], w1[:, u, m, :], peT[:, u, m:m + 1],
                                           start=(m == 0), stop=(m == KC - 1))
                    mm.then_inc(pe_summed, 1)
                    pe.wait_ge(pe_ready, 1)

                    def turn_blocks(turn):
                        n = NSUBP if is_prompt(turn) else P
                        for q in range(8):
                            v = q // 4
                            if q % 4 == 0:
                                pe.wait_ge(regrouped[v], turn + 1)
                            if not isinstance(turn, int) or turn * 4 + q // 2 > 1:
                                pe.wait_ge(sub_copied[q % 2], turn * 4 + q // 2 - 1)
                            for g in range(NG):
                                a = g * 512 + (q % 4) * P
                                mm = pe.transpose(bank[q % 4][:, g * n:g * n + n], rawg[0:n, v, a:a + P], ident[0:n, 0:n])
                            mm.then_inc(sub_turned[q % 2][v], 1)

                    def step(turn, u, i, left):
                        if left > 0:
                            turn_blocks(turn + 1)
                        prompt = is_prompt(turn)
                        n = NSUBP if prompt else P
                        nk = NCP if prompt else NCS
                        groups = NG if prompt else 2 * NG
                        for v in range(2):
                            pe.wait_ge(sub_copied[v], turn * 4 + 4)
                        for q in range(8):
                            x = subT[:, u, q, 0:4 * n].rearrange("p (k n) -> p k n", k=groups)
                            for r in range(2):
                                mm = pe.matmul(bank[4][:, 0:groups * nk], w1[:, u, 8 * r + q, :], x[:, :, r:r + nk],
                                               start=(q == 0 and r == 0), stop=(q == 7 and r == 1))
                        mm.then_inc(hid_summed, 1)
                        pe.wait_ge(hid_ready, turn + 1)
                        pe.wait_ge(kv_kept, turn)
                        if u == 0:
                            mm = pe.matmul(bank[5][:, 0:groups * nk], w2k[:, :], hid[:, 0:groups * nk], start=True, stop=True)
                        else:
                            for k in range(groups):
                                mm = pe.matmul(bank[6][0:nk, HD * k:HD * k + HD], hid[:, nk * k:nk * k + nk], w2v[:, :],
                                               start=True, stop=True)
                        mm.then_inc(kv_made, 1)
                    turn_blocks(0)
                    turns(pe, step)

                def regroup(eng, copy, v, turn):
                    n = NSUBP if is_prompt(turn) else P
                    eng.wait_ge(raw_loaded, turn * 256 + 256)
                    eng.wait_ge(sub_turned[1][v], turn * 2)
                    copy(rawg[0:n, v, :].rearrange("p (g s d) -> p g s d", g=NG, d=HD),
                         raw[0:n, v, :].rearrange("p (s g d) -> p g s d", g=NG, d=HD)).then_inc(regrouped[v], 1)

                def copy_blocks(eng, copy, v, turn, u):
                    wide = 4 * (NSUBP if is_prompt(turn) else P)
                    for k in range(4):
                        q = 2 * k + v
                        eng.wait_ge(sub_turned[v][k // 2], turn * 2 + k % 2 + 1)
                        copy(subT[:, u, q, 0:wide], bank[q % 4][:, 0:wide]).then_inc(sub_copied[v], 1)

                @block.scalar
                def _(act):
                    def step(turn, u, i, left):
                        if left > 0:
                            copy_blocks(act, act.copy, 0, turn + 1, 1 - u)
                        if left > 1:
                            regroup(act, act.copy, 0, turn + 2)
                        cols = NG * NCP if is_prompt(turn) else 2 * NG * NCS
                        act.wait_ge(hid_summed, turn + 1)
                        act.wait_ge(kv_made, turn)
                        act.activation(hid[:, 0:cols], bank[4][:, 0:cols], ACT.Silu, bias=pe_bias[:, u:u + 1]).then_inc(hid_ready, 1)
                    act.wait_ge(pe_ready, 1)
                    regroup(act, act.copy, 0, 0)
                    copy_blocks(act, act.copy, 0, 0, 0)
                    regroup(act, act.copy, 0, 1)
                    turns(act, step)

                @block.vector
                def _(dve):
                    dve.wait_ge(pe_turned, 1)
                    dve.tensor_copy(peT[:, :, :], bank[0][:, 0:32].rearrange("p (u m) -> p u m", u=2)).then_inc(pe_copied, 1)
                    dve.wait_ge(pe_summed, 1)
                    dve.tensor_copy(pe_bias[:, :], bank[1][:, 0:2]).then_inc(pe_ready, 1)

                    def step(turn, u, i, left):
                        if left > 0:
                            copy_blocks(dve, dve.tensor_copy, 1, turn + 1, 1 - u)
                        if left > 1:
                            regroup(dve, dve.tensor_copy, 1, turn + 2)
                        prompt = is_prompt(turn)
                        dve.wait_ge(kv_made, turn + 1)
                        if u == 0:
                            n = NCP if prompt else 2 * NCS
                            for h in range(2):
                                rows = slice(64 * h, 64 * h + 64)
                                src = bank[5][rows, 0:NG * n].rearrange("p (c g n) -> p c g n", c=2, g=2)[:, :, h, :]
                                dst = kcT_p[rows, :, :] if prompt else kcT[rows, :, bass.ds(i * n, n)]
                                ins = dve.tensor_copy(dst, src)
                        elif prompt:
                            ins = dve.tensor_copy(vc_p[:, :], bank[6][0:NCP, 0:KVW])
                        else:
                            ins = dve.tensor_copy(vc[:, bass.ds(i * 2, 2), :].rearrange("p b (g d) -> p g b d", g=NG),
                                                  bank[6][0:NCS, :].rearrange("p (g b d) -> p g b d", g=NG, b=2))
                        ins.then_inc(kv_kept, 1)
                    regroup(dve, dve.tensor_copy, 1, 0)
                    copy_blocks(dve, dve.tensor_copy, 1, 0, 0)
                    regroup(dve, dve.tensor_copy, 1, 1)
                    turns(dve, step)

        end_of_era()
        gates_ht = sb(attn, "gates_ht", [P, NB, 3])
        qr_bd = sb(attn, "qr_bd", [P, 2, NB, P])
        cmp_pT = sb(attn, "cmp_pT", [NCS, NB, P])
        drop_add = sb(attn, "drop_add", [P, NB, NBLK])
        oT_s = sb(attn, "oT_s", [P, 8, NS])
        with ExitStack() as scope:
            q_bd = sb(scope, "q_bd", [P, 2, NB, P])
            sc = sb(scope, "cmp_s", [P, NB, NCS])
            pc = sb(scope, "cmp_p", [P, NB, NCS])
            pg = sb(scope, "cmp_pg", [P, NB, NCS])
            st = sb(scope, "cmp_stat", [P, 4, NB])
            ps = sb(scope, "cmp_ps", [P, 3, NB, NBLK - 2])
            gates_loaded, bd_ready, cmp_scored, cmp_centred, cmp_exp, cmp_prob, cmp_grouped, cmp_turned, cmp_gated = (
                sem("c_" + x) for x in ("gates_loaded", "bd_ready", "scored", "centred", "exp", "prob", "grouped", "turned", "gated"))
            with nc.Block() as block:
                @block.sync
                def _(sp):
                    for h in range(NH):
                        sp.dma_start(gates_ht[h * NT:(h + 1) * NT, :, :],
                                     scratch["gates"][:, 3 * h:3 * h + 3].rearrange("(b t) c -> t b c", b=NB)).then_inc(gates_loaded, 16)

                @block.vector
                def _(dve):
                    own = dve_steps.on(dve)
                    dve.memset(q_bd[:, :, :, :], 0.0)
                    own.link(dve.memset(qr_bd[:, :, :, :], 0.0))
                    for src, dst in ((qT, q_bd), (qrT, qr_bd)):
                        for c in range(2):
                            for h in range(2):
                                rows = slice(64 * h, 64 * h + 64)
                                a = (2 * c + h) * 32
                                dve.tensor_copy(dst[rows, c, :, a:a + 32].rearrange("p b (j t) -> p j b t", j=NJ),
                                                src[rows, 4 * c:4 * c + 4, 256:256 + NS].rearrange("p j (b t) -> p j b t", b=NB)).then_inc(bd_ready, 1)
                    dve.wait_ge(cmp_scored, 1)
                    own.link(dve.tensor_scalar(sc[:, :, :], bank[0][:, 0:NB * NCS].rearrange("p (b n) -> p b n", b=NB), SCALE, None, ALU.mult))
                    own.link(dve.reduce_max(st[:, 0, :], sc[:, :, :], AX))
                    dve.tensor_tensor(sc[:, :, :], sc[:, :, :], st[:, 0, :].unsqueeze(2).to_broadcast([P, NB, NCS]), ALU.subtract).then_inc(cmp_centred, 1)
                    dve.wait_ge(cmp_exp, 1)
                    own.link(dve.reduce_sum(st[:, 1, :], pc[:, :, :], AX))
                    own.link(dve.reciprocal(st[:, 1, :], st[:, 1, :]))
                    dve.tensor_tensor(pc[:, :, :], pc[:, :, :], st[:, 1, :].unsqueeze(2).to_broadcast([P, NB, NCS]), ALU.mult).then_inc(cmp_prob, 1)
                    dve.wait_ge(cmp_grouped, 1)
                    own.link(dve.tensor_copy(pg[:, :, :], bank[1][:, 0:NB * NCS].rearrange("p (b n) -> p b n", b=NB)))
                    inner = pg[:, :, 4:4 * (NBLK - 1)].rearrange("p b (k r) -> p b k r", r=4)
                    own.link(dve.tensor_tensor(ps[:, 0], inner[:, :, :, 0], inner[:, :, :, 1], ALU.add))
                    own.link(dve.tensor_tensor(ps[:, 1], ps[:, 0], inner[:, :, :, 2], ALU.add))
                    own.link(dve.tensor_reduce(st[:, 2, :], ps[:, 1], AX, ALU.min))
                    own.link(dve.tensor_tensor(ps[:, 2], ps[:, 1], st[:, 2, :].unsqueeze(2).to_broadcast([P, NB, NBLK - 2]), ALU.is_equal))
                    own.link(dve.tensor_tensor(ps[:, 0], ps[:, 2], cst("block_id")[:, 1:NBLK - 1].unsqueeze(1).to_broadcast([P, NB, NBLK - 2]), ALU.mult))
                    own.link(dve.reduce_max(st[:, 3, :], ps[:, 0], AX))
                    own.link(dve.tensor_tensor(drop_add[:, :, :], cst("block_id").unsqueeze(1).to_broadcast([P, NB, NBLK]),
                                               st[:, 3, :].unsqueeze(2).to_broadcast([P, NB, NBLK]), ALU.is_equal))
                    own.link(dve.tensor_scalar(drop_add[:, :, :], drop_add[:, :, :], NEG, None, ALU.mult))
                    dve.wait_ge(gates_loaded, 16 * NH)
                    dve.tensor_tensor(sc[:, :, :], pc[:, :, :], gates_ht[:, :, 0:1].to_broadcast([P, NB, NCS]), ALU.mult).then_inc(cmp_gated, 1)
                    dve.wait_ge(cmp_turned, 1)
                    for n in range(2):
                        dve.tensor_copy(cmp_pT[:, 4 * n:4 * n + 4, :], bank[2 + n][0:NCS, :].rearrange("p (b r) -> p b r", b=4))

                @block.scalar
                def _(act):
                    act.wait_ge(cmp_centred, 1)
                    act.activation(pc[:, :, :], sc[:, :, :], ACT.Exp).then_inc(cmp_exp, 1)

                @block.tensor
                def _(pe):
                    pe.wait_ge(bd_ready, 8)
                    for b in range(NB):
                        for c in range(2):
                            mm = pe.matmul(bank[0][:, NCS * b:NCS * b + NCS], q_bd[:, c, b, :], kcT[:, c, NCS * b:NCS * b + NCS],
                                           start=(c == 0), stop=(c == 1))
                    mm.then_inc(cmp_scored, 1)
                    pe.wait_ge(cmp_prob, 1)
                    pe.matmul(bank[1][:, 0:NB * NCS], cst("group"), pc[:, :, :].rearrange("p b n -> p (b n)"),
                              start=True, stop=True).then_inc(cmp_grouped, 1)
                    pe.wait_ge(cmp_gated, 1)
                    for b in range(NB):
                        mm = pe.transpose(bank[2 + b // 4][0:NCS, (b % 4) * P:(b % 4) * P + P], sc[:, b, :], ident)
                    mm.then_inc(cmp_turned, 1)

        with ExitStack() as scope:
            k_in = sb(scope, "k_in", [P, 12, KVW])
            v_in = sb(scope, "v_in", [P, 2, 12, KVW])
            keyT = sb(scope, "keyT", [P, 2, 12 * P])
            q_now = sb(scope, "q_now", [P, 2, P])
            vc_now = sb(scope, "vc_now", [NCS, KVW])
            s = sb(scope, "s", [P, 2, PAST + NS + WIN + NS])
            S_W = PAST + NS
            s_neg = sb(scope, "s_neg", [P, 2])
            s_sum = sb(scope, "s_sum", [P, 2])
            pT = sb(scope, "pT", [P, 15, P])
            k_loaded, q_ready, key_scored, s_taken, max_ready, exp_ready, p_ready, p_turned, p_copied, o_kept, vc_ready, cp_ready = (
                sem("s_" + x) for x in ("k_loaded", "q_ready", "key_scored", "s_taken", "max_ready", "exp_ready", "p_ready",
                                        "p_turned", "p_copied", "o_kept", "vc_ready", "cp_ready"))
            o_made = [sem(f"s_o_made{v}") for v in range(2)]
            v_loaded = [sem(f"s_v_loaded{v}") for v in range(2)]
            k_turned = [sem(f"s_k_turned{v}") for v in range(2)]
            k_copied = [sem(f"s_k_copied{v}") for v in range(2)]

            def samples(eng, body, own=None, per=0):
                with eng.Fori(0, NB // 2 - 1) as i:
                    with own.loop(i, NB // 2 - 1, per) if own else ExitStack():
                        for u in range(2):
                            body(i * 2 + u, u, i, 2)
                for b in range(NB - 2, NB):
                    body(b, b % 2, b // 2, NB - 1 - b)

            with nc.Block() as block:
                @block.sync
                def _(sp):
                    def load(b, u, i, left):
                        ids = [sp.value_load(pages[0:1, bass.ds(b * NPG + j, 1)], min_val=0, max_val=A["cache_sel_k"].shape[1] - 1)
                               for j in range(NPG)]
                        for kind in "kv":
                            if kind == "k":
                                sp.wait_ge(k_turned[1], b * 3)
                                to, done = k_in[:, :, :], k_loaded
                            else:
                                sp.wait_ge(o_made[u], i)
                                to, done = v_in[:, u, :, :], v_loaded[u]
                            for j in range(NPG):
                                sp.dma_start(to[:, j, :], A["cache_sel_" + kind][0, bass.ds(ids[j], 1)].rearrange("o p g d -> (o p) (g d)")).then_inc(done, 16)
                            sp.dma_start(to[:, NPG:12, :], A["cache_win_" + kind][0, bass.ds(b, 1)].rearrange("o (n p) g d -> p (o n) (g d)", p=P)).then_inc(done, 16)
                    samples(sp, load)

                KBLOCKS = [(c, m) for m in range(3) for c in range(2)]
                PBLOCKS = [[(n, n * P, P) for n in range(0, 4)], [(n, n * P, P) for n in range(4, 8)],
                           [(9 + n, S_W + n * P, P) for n in range(3)] + [(8, PAST, NS)],
                           [(12, S_W + 3 * P, P), (13, S_W + WIN, NS)]]

                @block.tensor
                def _(pe):
                    def turn_keys(b):
                        pe.wait_ge(k_loaded, b * 144 + 144)
                        for n, (c, m) in enumerate(KBLOCKS):
                            if n >= 2:
                                pe.wait_ge(k_copied[n % 2], b * 3 + n // 2)
                            for k in range(4):
                                mm = pe.transpose(bank[4 + n % 2][:, k * P:k * P + P], k_in[:, 4 * m + k, c * P:c * P + P], ident)
                            mm.then_inc(k_turned[n % 2], 1)

                    def scores(b):
                        for v in range(2):
                            pe.wait_ge(k_copied[v], b * 3 + 3)
                        pe.wait_ge(q_ready, b + 1)
                        if not isinstance(b, int) or b:
                            pe.wait_ge(s_taken, b)
                            pe.wait_ge(o_kept, b - 1)
                        for c in range(2):
                            for n in range(3):
                                pe.matmul(bank[n], q_now[:, c, :], keyT[:, c, 512 * n:512 * n + 512], start=(c == 0), stop=(c == 1))
                        for n in range(2):
                            for c in range(2):
                                mm = pe.matmul(bank[3][:, NS * n:NS * n + NS], q_now[:, c, :], kT[:, 2 * n + c, 256:256 + NS],
                                               start=(c == 0), stop=(c == 1))
                        mm.then_inc(key_scored, 1)

                    turn_keys(0)
                    scores(0)
                    turn_keys(1)

                    def step(b, u, i, left):
                        if left:
                            scores(b + 1)
                        for n, blocks in enumerate(PBLOCKS):
                            if n % 2 == 0:
                                pe.wait_ge(p_ready, b * 2 + 1 + n // 2)
                            if n >= 2:
                                pe.wait_ge(p_copied, b * 4 + n - 1)
                            for k, (slot, off, width) in enumerate(blocks):
                                mm = pe.transpose(bank[6 + n % 2][0:width, k * P:k * P + P], s[:, u, off:off + width], ident)
                            mm.then_inc(p_turned, 1)
                        pe.wait_ge(p_copied, b * 4 + 4)
                        pe.wait_ge(v_loaded[u], i * 144 + 144)
                        pe.wait_ge(vc_ready, b + 1)
                        pe.wait_ge(cp_ready, b + 1)
                        if left:
                            pe.wait_ge(s_taken, b + 2)
                        for c in range(2):
                            cols = slice(c * P, c * P + P)
                            terms = [(v_in[:, u, n, cols], pT[:, n, :]) for n in range(8)] \
                                + [(Z[0:NS, 2, C_VS + c * P:C_VS + c * P + P], pT[0:NS, 8, :])] \
                                + [(v_in[:, u, 8 + n, cols], pT[:, 9 + n, :]) for n in range(4)] \
                                + [(Z[0:NS, 2, C_VW + c * P:C_VW + c * P + P], pT[0:NS, 13, :])] \
                                + [(vc_now[:, cols], pT[0:NCS, 14, :])]
                            for n, (v, p) in enumerate(terms):
                                mm = pe.matmul(bank[3][:, 256 + 64 * c:320 + 64 * c], v, p[:, 64 * c:64 * c + 64],
                                               start=(n == 0), stop=(n == len(terms) - 1))
                        mm.then_inc(o_made[u], 1)
                        if left > 1:
                            turn_keys(b + 2)
                    samples(pe, step)

                def copy_keys(eng, copy, v, b):
                    for n, (c, m) in enumerate(KBLOCKS):
                        if n % 2 == v:
                            eng.wait_ge(k_turned[v], b * 3 + n // 2 + 1)
                            copy(keyT[:, c, 512 * m:512 * m + 512], bank[4 + v]).then_inc(k_copied[v], 1)

                BRANCHES = ((0, S_W), (S_W, S_W + WIN + NS))

                @block.scalar
                def _(act):
                    def exps(b, u):
                        act.wait_ge(max_ready, b + 1)
                        for n, (a, z) in enumerate(BRANCHES):
                            act.activation(s[:, u, a:z], s[:, u, a:z], ACT.Exp, bias=s_neg[:, n:n + 1],
                                           accum_out=s_sum[:, n:n + 1]).then_inc(exp_ready, 1)

                    def values(b):
                        act.copy(vc_now[:, :], vc[:, bass.ds(b, 1), :].rearrange("p o n -> p (o n)")).then_inc(vc_ready, 1)

                    copy_keys(act, act.copy, 0, 0)
                    values(0)
                    copy_keys(act, act.copy, 0, 1)
                    exps(0, 0)

                    def step(b, u, i, left):
                        for n, blocks in enumerate(PBLOCKS):
                            act.wait_ge(p_turned, b * 4 + n + 1)
                            full = [k for k, x in enumerate(blocks) if x[2] == P]
                            part = [k for k, x in enumerate(blocks) if x[2] < P]
                            for k in part:
                                act.copy(pT[0:NS, blocks[k][0], :], bank[6 + n % 2][0:NS, k * P:k * P + P])
                            a, z, slot = full[0], full[-1] + 1, blocks[full[0]][0]
                            act.copy(pT[:, slot:slot + z - a, :], bank[6 + n % 2][:, a * P:z * P].rearrange("p (k r) -> p k r", r=P)).then_inc(p_copied, 1)
                        if left:
                            exps(b + 1, 1 - u)
                            act.wait_ge(o_made[u], i + 1)
                            values(b + 1)
                        if left > 1:
                            copy_keys(act, act.copy, 0, b + 2)
                    samples(act, step)

                @block.vector
                def _(dve):
                    own = dve_steps.on(dve)
                    one = lambda v: v.rearrange("p o n -> p (o n)")

                    def queries(b):
                        dve.tensor_copy(q_now[:, :, :], qr_bd[:, :, bass.ds(b, 1), :].rearrange("p c o r -> p c (o r)")).then_inc(q_ready, 1)

                    def take(b, u):
                        dve.wait_ge(key_scored, b + 1)
                        drop = one(drop_add[:, bass.ds(b, 1), :])
                        new = one(cst("new_add", to="p (b n) -> p b n", b=NB)[:, bass.ds(b, 1), :])
                        for a, width, src, mask in (
                                (PAST, NS, bank[3][:, 0:NS], new),
                                (S_W + WIN, NS, bank[3][:, NS:2 * NS], new),
                                (0, PAST, bank2[0][:, :].rearrange("p (k l) -> p k l", l=LSEL), drop.unsqueeze(2).to_broadcast([P, NBLK, LSEL])),
                                (S_W, WIN, bank[2], cst("win_add"))):
                            dst = s[:, u, a:a + width]
                            if a == 0:
                                dst = dst.rearrange("p (k l) -> p k l", l=LSEL)
                            ins = dve.scalar_tensor_tensor(out=dst, in0=src, scalar=SCALE, in1=mask, op0=ALU.mult, op1=ALU.add)
                        ins.then_inc(s_taken, 1)
                        dve.wait_ge(s_taken, b + 1)
                        for n, (a, z) in enumerate(BRANCHES):
                            ins = dve.reduce_max(s_neg[:, n:n + 1], s[:, u, a:z], AX, negate=True)
                        ins.then_inc(max_ready, 1)

                    def normalise(b, u):
                        dve.wait_ge(exp_ready, b * 2 + 2)
                        own.link(dve.reciprocal(s_sum[:, :], s_sum[:, :]))
                        own.link(dve.tensor_tensor(s_sum[:, :], s_sum[:, :], one(gates_ht[:, bass.ds(b, 1), 1:3]), ALU.mult))
                        for n, (a, z) in enumerate(BRANCHES):
                            dve.tensor_scalar(s[:, u, a:z], s[:, u, a:z], s_sum[:, n:n + 1], None, ALU.mult).then_inc(p_ready, 1)

                    def compressed(b):
                        dve.tensor_copy(pT[0:NCS, 14, :], one(cmp_pT[:, bass.ds(b, 1), :])).then_inc(cp_ready, 1)

                    queries(0)
                    compressed(0)
                    copy_keys(dve, dve.tensor_copy, 1, 0)
                    take(0, 0)
                    queries(1)
                    copy_keys(dve, dve.tensor_copy, 1, 1)
                    normalise(0, 0)

                    def step(b, u, i, left):
                        if left:
                            take(b + 1, 1 - u)
                            if left > 1:
                                queries(b + 2)
                            normalise(b + 1, 1 - u)
                        dve.wait_ge(o_made[u], i + 1)
                        for h in range(2):
                            rows = slice(64 * h, 64 * h + 64)
                            ins = dve.tensor_copy(
                                oT_s[rows, :, bass.ds(b * NT, NT)],
                                bank[3][rows, 256:384].rearrange("p (c g n) -> p c g n", c=2, g=2)[:, :, h, :].rearrange("p c (j t) -> p c j t", t=NT))
                        ins.then_inc(o_kept, 1)
                        if left:
                            compressed(b + 1)
                        if left > 1:
                            copy_keys(dve, dve.tensor_copy, 1, b + 2)

                    samples(dve, step, own, 4)

        end_of_era()
        mix_scope = top.enter_context(ExitStack())
        mix = mix_scope.enter_context(nc.sbuf_tensor("mix", [P, TILES, D], F32, side="right"))
        with ExitStack() as scope:
            s = sb(scope, "ps", [P, 2, NJ, SEQ])
            s_c = sb(scope, "ps_c", [P, NJ, NCP])
            stat = sb(scope, "p_stat", [P, 4, 3, NJ])
            pT = sb(scope, "p_pT", [P, 20, P])
            o_part = sb(scope, "o_part", [P, 3, NJ * HD])
            scored, s_taken, max_ready, centred, exp_ready, exp_c_ready, c_ready, o_made, o_taken = (sem("p_" + x) for x in (
                "scored", "s_taken", "max_ready", "centred", "exp_ready", "exp_c_ready", "c_ready", "o_made", "o_taken"))
            turned, copied = sem("p_turned"), sem("p_copied")
            STEPS = [(r, g, kind) for r in range(2) for g in range(NG) for kind in range(2)]

            def slot(r, kind, j, kt):
                return 12 * kind + j * (r + 1) + kt

            def blocks_of(r, kind):
                todo = [(slot(r, kind, j, k), s[:, kind, j, k * P:k * P + P], P) for j in range(NJ) for k in range(r + 1)]
                if kind == 0:
                    todo += [(8 + j, s_c[:, j, :], NCP) for j in range(NJ)]
                return [todo[a:a + 4] for a in range(0, len(todo), 4)]

            BEFORE = [sum(len(blocks_of(r, kind)) for r, _, kind in STEPS[:n]) for n in range(len(STEPS) + 1)]

            with nc.Block() as block:
                @block.tensor
                def _(pe):
                    def scores(n):
                        r, g, kind = STEPS[n]
                        c, half = g // 2, slice(64 * (g % 2), 64 * (g % 2) + 64)
                        keys, rows = (r + 1) * P, slice(r * P, r * P + P)
                        if n >= 2:
                            pe.wait_ge(s_taken, n - 1)
                        if kind == 0:
                            if n >= 2:
                                pe.wait_ge(o_taken, n - 1)
                            for j in range(NJ):
                                pe.matmul(bank[4][:, NCP * j:NCP * j + NCP], qT[half, 4 * c + j, rows], kcT_p[half, c, :],
                                          start=True, stop=True)
                        for j in range(NJ):
                            mm = pe.matmul(bank2[kind][:, SEQ * j:SEQ * j + keys], qrT[half, 4 * c + j, rows],
                                           kT[half, 2 * kind + c, 0:keys], start=True, stop=True)
                        mm.then_inc(scored, 1)

                    def finish(n):
                        r, g, kind = STEPS[n]
                        pe.wait_ge(exp_ready, NJ * (n + 1))
                        if kind == 0:
                            pe.wait_ge(c_ready, n // 2 + 1)
                        for m, blocks in enumerate(blocks_of(r, kind)):
                            k = BEFORE[n] + m
                            if k >= 2:
                                pe.wait_ge(copied, k - 1)
                            for y, (_, src, width) in enumerate(blocks):
                                mm = pe.transpose(bank[6 + k % 2][0:width, y * P:y * P + P], src, ident)
                            mm.then_inc(turned, 1)
                        pe.wait_ge(copied, BEFORE[n + 1])
                        if n >= 1:
                            pe.wait_ge(o_taken, n)
                        col = (C_VS, C_VW)[kind]
                        for j in range(NJ):
                            for kt in range(r + 1):
                                mm = pe.matmul(bank[5][:, (kind * NJ + j) * HD:(kind * NJ + j) * HD + HD], pT[:, slot(r, kind, j, kt), :],
                                               Z[:, kt, col + HD * g:col + HD * g + HD], start=(kt == 0), stop=(kt == r))
                        if kind == 0:
                            for j in range(NJ):
                                mm = pe.matmul(bank[4][:, 64 + HD * j:128 + HD * j], pT[0:NCP, 8 + j, :],
                                               vc_p[:, HD * g:HD * g + HD], start=True, stop=True)
                        mm.then_inc(o_made, 1)

                    scores(0)
                    for n in range(len(STEPS)):
                        if n + 1 < len(STEPS):
                            scores(n + 1)
                        finish(n)

                @block.scalar
                def _(act):
                    def exps(n):
                        r, g, kind = STEPS[n]
                        if kind == 0:
                            act.wait_ge(centred, n // 2 + 1)
                            act.activation(s_c[:, :, :], s_c[:, :, :], ACT.Exp).then_inc(exp_c_ready, 1)
                        act.wait_ge(max_ready, n + 1)
                        for j in range(NJ):
                            act.activation(s[:, kind, j, 0:(r + 1) * P], s[:, kind, j, 0:(r + 1) * P], ACT.Exp, bias=stat[:, 0, kind, j:j + 1],
                                           accum_out=stat[:, 1, kind, j:j + 1]).then_inc(exp_ready, 1)

                    exps(0)
                    for n, (r, g, kind) in enumerate(STEPS):
                        for m, blocks in enumerate(blocks_of(r, kind)):
                            act.wait_ge(turned, BEFORE[n] + m + 1)
                            w, first = blocks[0][2], blocks[0][0]
                            act.copy(pT[0:w, first:first + len(blocks), :],
                                     bank[6 + (BEFORE[n] + m) % 2][0:w, 0:len(blocks) * P].rearrange("p (k r) -> p k r", r=P)).then_inc(copied, 1)
                        if n + 1 < len(STEPS):
                            exps(n + 1)

                @block.gpsimd
                def _(pool):
                    for n, (r, g, kind) in enumerate(STEPS):
                        if kind == 0:
                            c_mul = cst("cmp_mul", to="p (r k) -> p r k", r=2)[:, r, :].unsqueeze(1).to_broadcast([P, NJ, NCP])
                            pool.wait_ge(exp_c_ready, n // 2 + 1)
                            pool.tensor_tensor(s_c[:, :, :], s_c[:, :, :], c_mul, ALU.mult).then_inc(c_ready, 1)

                @block.vector
                def _(dve):
                    own = dve_steps.on(dve)

                    def take(n):
                        r, g, kind = STEPS[n]
                        keys = (r + 1) * P
                        causal = cst("causal", to="p (r k) -> p r k", r=2)[:, r, 0:keys].unsqueeze(1).to_broadcast([P, NJ, keys])
                        dve.wait_ge(scored, n + 1)
                        if kind == 0:
                            c_add = cst("cmp_add", to="p (r k) -> p r k", r=2)[:, r, :].unsqueeze(1).to_broadcast([P, NJ, NCP])
                            dve.scalar_tensor_tensor(out=s_c[:, :, :], in0=bank[4][:, 0:NJ * NCP].rearrange("p (j k) -> p j k", j=NJ),
                                                     scalar=SCALE, in1=c_add, op0=ALU.mult, op1=ALU.add)
                        dve.scalar_tensor_tensor(out=s[:, kind, :, 0:keys], in0=bank2[kind][:, :].rearrange("p (j k) -> p j k", j=NJ)[:, :, 0:keys],
                                                 scalar=SCALE, in1=causal, op0=ALU.mult, op1=ALU.add).then_inc(s_taken, 1)
                        dve.wait_ge(s_taken, n + 1)
                        dve.reduce_max(stat[:, 0, kind, :], s[:, kind, :, 0:keys], AX, negate=True).then_inc(max_ready, 1)
                        if kind == 0:
                            own.link(dve.reduce_max(stat[:, 0, 2, :], s_c[:, :, :], AX))
                            dve.tensor_tensor(s_c[:, :, :], s_c[:, :, :], stat[:, 0, 2, :].unsqueeze(2).to_broadcast([P, NJ, NCP]),
                                              ALU.subtract).then_inc(centred, 1)

                    def weigh(n):
                        r, g, kind = STEPS[n]
                        kinds = slice(0, 3, 2) if kind == 0 else slice(1, 2)
                        if kind == 0:
                            dve.wait_ge(c_ready, n // 2 + 1)
                        if kind == 0:
                            own.link(dve.reduce_sum(stat[:, 1, 2, :], s_c[:, :, :], AX))
                        dve.wait_ge(exp_ready, NJ * (n + 1))
                        own.link(dve.tensor_scalar(stat[:, 2, kinds, :], stat[:, 1, kinds, :], 1e-30, None, ALU.max))
                        own.link(dve.reciprocal(stat[:, 2, kinds, :], stat[:, 2, kinds, :]))
                        gate = Z[:, r, C_G + 12 * g:C_G + 12 * g + 12].rearrange("p (j c) -> p c j", c=3)
                        if kind == 0:
                            dve.tensor_tensor(stat[:, 3, 2, :], stat[:, 2, 2, :], gate[:, 0, :], ALU.mult)
                        own.link(dve.tensor_tensor(stat[:, 3, kind, :], stat[:, 2, kind, :], gate[:, 1 + kind, :], ALU.mult))
                        dve.wait_ge(o_made, n + 1)
                        parts = [(kind, bank[5][:, 256 * kind:256 * kind + 256])] + ([(2, bank[4][:, 64:320])] if kind == 0 else [])
                        for part, src in parts:
                            ins = dve.tensor_tensor(o_part[:, part, :].rearrange("p (j d) -> p j d", j=NJ), src.rearrange("p (j d) -> p j d", j=NJ),
                                                    stat[:, 3, part, :].unsqueeze(2).to_broadcast([P, NJ, HD]), ALU.mult)
                        ins.then_inc(o_taken, 1)
                        dve.wait_ge(o_taken, n + 1)
                        if kind == 0:
                            own.link(dve.tensor_tensor(o_part[:, 0, :], o_part[:, 0, :], o_part[:, 2, :], ALU.add))
                        else:
                            own.link(dve.tensor_tensor(mix[:, r, 256 * g:256 * g + 256], o_part[:, 0, :], o_part[:, 1, :], ALU.add))

                    take(0)
                    for n in range(len(STEPS)):
                        if n + 1 < len(STEPS):
                            take(n + 1)
                        weigh(n)

        with ExitStack() as scope:
            w_s = sb(scope, "w_s", [P, SG, P])
            wsT = sb(scope, "wsT", [P, SG, P])
            b_s = sb(scope, "b_s", [SG, P])
            bT = sb(scope, "bT", [P, SG])
            rep = sb(scope, "rep_s", [NS, SG * NT + SG])
            bd = sb(scope, "w_bd", [NS, SG, NB, NT])
            jobs = []
            for c in range(2):
                dst = mix[0:NS, 2, 512 * c:512 * c + 512].rearrange("p (g j d) -> p j g d", g=2, j=NJ)
                jobs.append(([(P, NS, j * P, oT_s[:, 4 * c + j, :]) for j in range(NJ)],
                             [(dst[:, j], (lambda j: lambda b: b[0:NS, j * P:j * P + P].rearrange("p (g d) -> p g d", g=2))(j)) for j in range(NJ)]))
            for m in range(2):
                jobs.append(([(P, P, k * P, w_s[:, 4 * m + k, :]) for k in range(4)],
                             [(wsT[:, 4 * m:4 * m + 4, :], bank_view(4))]))
            jobs.append(([(SG, P, 0, b_s[:, :])], [(bT[:, :], lambda b: b[:, 0:SG])]))
            transpose_jobs("sgu", jobs, loads=[(w_s[:, :, :], A["w_sgu"][0].rearrange("g t s -> t g s")), (b_s[:, :], A["b_sgu"][0])])

            masked, rep_made, bd_ready, mixed = (sem("sgu_" + x) for x in ("masked", "rep_made", "bd_ready", "mixed"))
            with nc.Block() as block:
                @block.gpsimd
                def _(pool):
                    pool.memset(mix[NS:P, 2, :], 0.0)

                @block.vector
                def _(dve):
                    own = dve_steps.on(dve)
                    dve.tensor_tensor(wsT[:, :, :], wsT[:, :, :], cst("tri").unsqueeze(1).to_broadcast([P, SG, P]), ALU.mult).then_inc(masked, 1)
                    dve.wait_ge(rep_made, 1)
                    own.link(dve.tensor_copy(rep[:, :], bank[4][0:NS, 0:SG * NT + SG]))
                    same_b = cst("same_b", to="p (b t) -> p b t", b=NB)
                    for g in range(SG):
                        dve.tensor_tensor(bd[:, g], same_b[0:NS], rep[:, NT * g:NT * g + NT].unsqueeze(1).to_broadcast([NS, NB, NT]),
                                          ALU.mult).then_inc(bd_ready, 1)
                    for r in range(TILES):
                        rows = P if r < 2 else NS
                        dve.wait_ge(mixed, r + 1)
                        for g in range(SG):
                            bias = bT[:, g:g + 1] if r < 2 else rep[:, SG * NT + g:SG * NT + g + 1]
                            b = (0, 2, 5)[r] + g // 4
                            dve.scalar_tensor_tensor(out=mix[0:rows, r, SW + P * g:SW + P * g + P], in0=bank[b][0:rows, P * (g % 4):P * (g % 4) + P],
                                                     scalar=bias, in1=Z[0:rows, r, C_U + P * g:C_U + P * g + P], op0=ALU.add, op1=ALU.mult)

                @block.tensor
                def _(pe):
                    pe.matmul(bank[4][0:NS, SG * NT:SG * NT + SG], cst("rep")[0:NT, :], bT[0:NT, :], start=True, stop=True)
                    pe.wait_ge(masked, 1)
                    for g in range(SG):
                        mm = pe.matmul(bank[4][0:NS, NT * g:NT * g + NT], cst("rep")[0:NT, :], wsT[0:NT, g, 0:NT], start=True, stop=True)
                    mm.then_inc(rep_made, 1)
                    for r in range(TILES):
                        rows = P if r < 2 else NS
                        if r == 2:
                            pe.wait_ge(bd_ready, SG)
                        for g in range(SG):
                            b = (0, 2, 5)[r] + g // 4
                            lhsT = wsT[:, g, :] if r < 2 else bd[:, g].rearrange("p b t -> p (b t)")
                            mm = pe.matmul(bank[b][0:rows, P * (g % 4):P * (g % 4) + P], lhsT,
                                           Z[0:rows, r, C_V + P * g:C_V + P * g + P], start=True, stop=True)
                        mm.then_inc(mixed, 1)

        end_of_era()
        mixT = mix_scope.enter_context(nc.sbuf_tensor("mixT", [P, KC, TILES * P], F32, side="right"))
        attn.close()
        x = sb(top, "x", [P, TILES, D])
        x_again, w_out_loaded = sem("x_again"), sem("w_out_loaded")
        w_out_scope = top.enter_context(ExitStack())
        wbuf = [sb(w_out_scope, f"w_out{u}", [P, KC, 512]) for u in range(2)]
        with nc.Block() as block:
            @block.sync
            def _(sp):
                sp.dma_start(x[0:NS, 2, :], A["x_sample"].rearrange("b t n -> (b t) n")).then_inc(x_again, 16)
                sp.dma_start(x[:, 0:2, :], A["x_prompt"][0].rearrange("(r p) n -> p r n", p=P)).then_inc(x_again, 16)
                sp.dma_start(wbuf[0][:, :, :], w_view("w_out")[:, :, 0:512]).then_inc(w_out_loaded, 16)

            @block.vector
            def _(dve):
                dve.memset(x[NS:P, 2, :], 0.0)
        norm_transpose("mix", [(mix[:, r, :], gain_mix, mixT[:, :, r * P:(r + 1) * P], None) for r in range(TILES)],
                       [(0, SW), (SW, D)])
        with ExitStack() as scope:
            w_out = w_view("w_out")
            project("w_out", mixT, TILES, (2, lambda i, u: (w_out[:, :, bass.ds(i * 1024 + u * 512, 512)], 512,
                                                          lambda r: x[:, r, bass.ds(i * 1024 + u * 512, 512)]), []), wbuf, residual=True, first=w_out_loaded, x_loaded=(x_again, 32))

        w_out_scope.close()
        mix_scope.close()
        with ExitStack() as era:
            o_mT = sb(era, "o_mT", [P, MH, TILES * P])
            with ExitStack() as scope:
                hqT = sb(scope, "hqT", [P, MH, TILES * P])
                m_v = sb(scope, "m_v", [P, NB, 2, MW])
                m_k = sb(scope, "m_k", [P, NB, 2, MW])
                m_k_loaded, m_v_loaded = sem("m_k_loaded"), sem("m_v_loaded")
                tiled = lambda name, b: A[name][0, b].rearrange("(k p) h d -> p k (h d)", p=P)
                with ExitStack() as inner:
                    hT = sb(inner, "hT_mem", [P, KC, TILES * P])
                    w_q = sb(inner, "w_q", [P, KC, MW])
                    wq_loaded, hq_made = sem("wq_loaded"), sem("hq_made")
                    norm_transpose("mem", [(x[:, r, :], gain_mem, hT[:, :, r * P:(r + 1) * P], None) for r in range(TILES)], [(0, D)],
                                   ahead=[(w_q[:, :, :], w_view("w_mem_q"), wq_loaded)]
                                   + [(m_k[:, b], tiled("cache_mem_k", b), m_k_loaded) for b in range(NB)]
                                   + [(m_v[:, b], tiled("cache_mem_v", b), m_v_loaded) for b in range(NB)])
                    with nc.Block() as block:
                        @block.tensor
                        def _(pe):
                            pe.wait_ge(wq_loaded, 16)
                            for h in range(MH):
                                for c in range(KC):
                                    mm = pe.matmul(bank[h][:, 0:TILES * P], w_q[:, c, h * MD:(h + 1) * MD], hT[:, c, :],
                                                   start=(c == 0), stop=(c == KC - 1))
                                mm.then_inc(hq_made, 1)

                        @block.vector
                        def _(dve):
                            for h in range(MH):
                                dve.wait_ge(hq_made, h + 1)
                                dve.tensor_copy(hqT[:, h, :], bank[h][:, 0:TILES * P])

                m_keyT = sb(scope, "m_keyT", [P, MH, NB, NMEM])
                jobs = []
                for b in range(NB):
                    for k in range(2):
                        jobs.append(([(P, P, h * P, m_k[:, b, k, h * MD:(h + 1) * MD]) for h in range(MH)],
                                     [(m_keyT[:, :, b, k * P:(k + 1) * P], bank_view(4))]))
                transpose_jobs("m_keys", jobs, after=(m_k_loaded, 16 * NB))
                q_bd = sb(scope, "m_q_bd", [P, NB * MH, P])
                s = sb(scope, "m_s", [P, MH, NMEM])
                stat = sb(scope, "m_stat", [P, 2, MH])
                pT = sb(scope, "m_pT", [P, 2 * MH, P])
                bd_ready, scored, max_ready, exp_ready, p_ready, o_made, o_kept = (sem("m_" + n) for n in (
                    "bd_ready", "scored", "max_ready", "exp_ready", "p_ready", "o_made", "o_kept"))
                turned = [sem(f"m_turned{v}") for v in range(2)]
                copied = [sem(f"m_copied{v}") for v in range(2)]
                PARTS = [MH, MH, 1, 1]
                BLOCKS = [[[(2 * j + k, j, k) for j in range(a, min(a + 2, n)) for k in range(2)] for a in range(0, n, 2)] for n in PARTS]
                M_BEFORE = [sum(len(x) for x in BLOCKS[:n]) for n in range(5)]
                E_BEFORE = [sum(PARTS[:n]) for n in range(5)]
                half_up = lambda n, v: (n + 1 - v) // 2
                with nc.Block() as block:
                    @block.tensor
                    def _(pe):
                        pe.wait_ge(m_v_loaded, 16 * NB)
                        for n in range(4):
                            if n < 2:
                                for h in range(MH):
                                    mm = pe.matmul(bank2[0][:, NMEM * h:NMEM * h + NMEM], hqT[:, h, n * P:(n + 1) * P], mem_kT[:, h, :],
                                                   start=True, stop=True)
                            else:
                                pe.wait_ge(bd_ready, MH)
                                for k in range(4 * MH):
                                    b, h = 4 * (n - 2) + k // MH, k % MH
                                    mm = pe.matmul(bank[0][:, 0:NMEM], q_bd[:, b * MH + h, :], m_keyT[:, h, b, :],
                                                   start=(k == 0), stop=(k == 4 * MH - 1))
                            mm.then_inc(scored, 1)
                            pe.wait_ge(p_ready, n + 1)
                            for m, blocks in enumerate(BLOCKS[n]):
                                k = M_BEFORE[n] + m
                                if k >= 2:
                                    pe.wait_ge(copied[k % 2], k // 2)
                                for y, (slot, j, kt) in enumerate(blocks):
                                    mm = pe.transpose(bank[2 + k % 2][:, y * P:y * P + P], s[:, j, kt * P:kt * P + P], ident)
                                mm.then_inc(turned[k % 2], 1)
                            for v in range(2):
                                pe.wait_ge(copied[v], half_up(M_BEFORE[n + 1], v))
                            if n:
                                pe.wait_ge(o_kept, n)
                            if n < 2:
                                for h in range(MH):
                                    for kt in range(2):
                                        mm = pe.matmul(bank[4][:, h * P:h * P + P], mem_kv[:, kt, MW + h * MD:MW + (h + 1) * MD],
                                                       pT[:, 2 * h + kt, :], start=(kt == 0), stop=(kt == 1))
                            else:
                                for k in range(4 * MH):
                                    b, h = k // MH, k % MH
                                    for kt in range(2):
                                        mm = pe.matmul(bank[4][:, 32 * h + NT * b:32 * h + NT * b + NT], m_v[:, 4 * (n - 2) + b, kt, h * MD:(h + 1) * MD],
                                                       pT[:, kt, NT * k:NT * k + NT], start=(kt == 0), stop=(kt == 1))
                            mm.then_inc(o_made, 1)

                    def copy_blocks(eng, copy, v, n):
                        for m, blocks in enumerate(BLOCKS[n]):
                            k = M_BEFORE[n] + m
                            if k % 2 == v:
                                eng.wait_ge(turned[v], k // 2 + 1)
                                copy(pT[:, blocks[0][0]:blocks[-1][0] + 1, :],
                                     bank[2 + v][:, 0:len(blocks) * P].rearrange("p (k r) -> p k r", r=P)).then_inc(copied[v], 1)

                    @block.scalar
                    def _(act):
                        for n in range(4):
                            act.wait_ge(max_ready, n + 1)
                            for j in range(PARTS[n]):
                                act.activation(s[:, j, :], s[:, j, :], ACT.Exp, bias=stat[:, 0, j:j + 1],
                                               accum_out=stat[:, 1, j:j + 1]).then_inc(exp_ready, 1)
                            copy_blocks(act, act.copy, 0, n)

                    @block.vector
                    def _(dve):
                        own = dve_steps.on(dve)
                        own.link(dve.memset(q_bd[:, :, :], 0.0))
                        for h in range(MH):
                            q = q_bd[:, :, :].rearrange("p (m b h) r -> p m b h r", m=2, h=MH)
                            for m in range(2):
                                for b in range(4):
                                    ins = dve.tensor_copy(q[:, m, b, h, 32 * b + NT * h:32 * b + NT * h + NT],
                                                          hqT[:, h, 256 + 32 * m + NT * b:256 + 32 * m + NT * b + NT])
                            ins.then_inc(bd_ready, 1)
                        for n in range(4):
                            parts = PARTS[n]
                            dve.wait_ge(scored, n + 1)
                            src = bank2[0][:, 0:parts * NMEM].rearrange("p (j k) -> p j k", j=parts)
                            own.link(dve.tensor_scalar(s[:, 0:parts, :], src, MSCALE, None, ALU.mult))
                            dve.reduce_max(stat[:, 0, 0:parts], s[:, 0:parts, :], AX, negate=True).then_inc(max_ready, 1)
                            dve.wait_ge(exp_ready, E_BEFORE[n + 1])
                            own.link(dve.reciprocal(stat[:, 1, 0:parts], stat[:, 1, 0:parts]))
                            dve.tensor_tensor(s[:, 0:parts, :], s[:, 0:parts, :], stat[:, 1, 0:parts].unsqueeze(2).to_broadcast([P, parts, NMEM]),
                                              ALU.mult).then_inc(p_ready, 1)
                            copy_blocks(dve, dve.tensor_copy, 1, n)
                            dve.wait_ge(o_made, n + 1)
                            if n < 2:
                                ins = dve.tensor_copy(o_mT[:, :, n * P:(n + 1) * P], bank[4].rearrange("p (h r) -> p h r", h=MH))
                            else:
                                a = 256 + 32 * (n - 2)
                                ins = dve.tensor_copy(o_mT[:, :, a:a + 32], bank[4][:, 0:P].rearrange("p (h r) -> p h r", h=MH))
                            ins.then_inc(o_kept, 1)
                        dve.memset(o_mT[:, :, 256 + NS:], 0.0)
            with ExitStack() as scope:
                wbuf = [sb(scope, f"w_o{u}", [P, MH, 512]) for u in range(2)]
                w_o = A["w_mem_o"][0].rearrange("(c p) n -> p c n", p=P)
                project("w_mem_o", o_mT, TILES, (2, lambda i, u: (w_o[:, :, bass.ds(i * 1024 + u * 512, 512)], 512,
                                                                lambda r: x[:, r, bass.ds(i * 1024 + u * 512, 512)]), []), wbuf,
                        residual=True, chunks=MH)

        end_of_era()
        pairs = sb(top, "pairs", [1, 1], I32)
        w_g = sb(top, "w_g", [P, KC, FF])
        w_u = sb(top, "w_u", [P, KC, FF])
        w_d = sb(top, "w_d", [P, 4, D])
        gu_loaded, gu_used, d_loaded, d_used = ([sem(f"e_{n}{q}") for q in range(4)] for n in ("gu_loaded", "gu_used", "d_loaded", "d_used"))

        def expert_loads(e):
            g = A["w_exp_gate"][0, bass.ds(e, 1)].rearrange("o (p c) f -> (o p) c f", c=KC)
            up = A["w_exp_up"][0, bass.ds(e, 1)].rearrange("o (p c) f -> (o p) c f", c=KC)
            d = A["w_exp_down"][0, bass.ds(e, 1)].rearrange("o (p c) n -> (o p) c n", c=4)
            quarters = []
            for q in range(4):
                cs = slice(4 * q, 4 * q + 4)
                quarters.append((gu_used[q], [(w_g[:, cs, :], g[:, cs, :], gu_loaded[q]), (w_u[:, cs, :], up[:, cs, :], gu_loaded[q])]))
            return quarters + [(d_used[q], [(w_d[:, q, :], d[:, q, :], d_loaded[q])]) for q in range(4)]

        with ExitStack() as scope:
            w_r = sb(scope, "w_r", [P, KC, 20])
            wr_loaded = sem("r_wr_loaded")
            hT = sb(scope, "hT_moe", [P, KC, TILES * P])
            norm_transpose("moe", [(x[:, r, :], gain_moe, hT[:, :, r * P:(r + 1) * P], None) for r in range(TILES)], [(0, D)],
                           ahead=[(w_r[:, :, 0:4], w_view("w_router_group"), wr_loaded), (w_r[:, :, 4:20], w_view("w_router_expert"), wr_loaded)],
                           last=[load for _, loads in expert_loads(0) for load in loads],
                           stores=[(scratch["hn"][r * P:r * P + (P if r < 2 else NS)], P if r < 2 else NS) for r in range(TILES)])
            lg = sb(scope, "lg", [P, TILES, 20])
            t4 = sb(scope, "t4", [P, TILES, 4, 4])
            eg = sb(scope, "eg", [P, TILES, 4])
            oh = sb(scope, "oh", [P, 3, TILES, 4])
            fl = sb(scope, "fl", [P, 2, TILES, 4])
            m = sb(scope, "m_", [P, 8, TILES])
            sel = sb(scope, "sel", [P, 3, TILES, NE])
            rank = sb(scope, "rank", [P, TILES, NE])
            pos = sb(scope, "pos", [P, 4, TILES])
            t16 = sb(scope, "t16", [P, TILES, NE])
            pos_i = sb(scope, "pos_i", [P, 2, TILES], I32)
            row = sb(scope, "row", [P, TILES, 2, 4])
            blank = sb(scope, "blank", [P, 49, 4])
            cnt = sb(scope, "cnt", [P, 4])
            logits_made, g_centred, g_exp, e_centred, e_exp, sel_ready, rank_made, rows_ready, blank_ready, blanked, slotted = (
                sem("r_" + n) for n in ("logits_made", "g_centred", "g_exp", "e_centred", "e_exp", "sel_ready", "rank_made",
                                        "rows_ready", "blank_ready", "blanked", "slotted"))
            with nc.Block() as block:
                @block.tensor
                def _(pe):
                    pe.wait_ge(wr_loaded, 32)
                    for r in range(TILES):
                        for c in range(KC):
                            mm = pe.matmul(bank[0][:, 20 * r:20 * r + 20], hT[:, c, r * P:(r + 1) * P], w_r[:, c, :],
                                           start=(c == 0), stop=(c == KC - 1))
                    mm.then_inc(logits_made, 1)
                    pe.wait_ge(sel_ready, 1)
                    for r in range(TILES):
                        for q in range(r):
                            pe.matmul(bank[1][:, NE * r:NE * r + NE], cst("ones"), sel[:, 2, q, :], start=(q == 0), stop=False)
                        pe.matmul(bank[1][:, NE * r:NE * r + NE], cst("tri_strict"), sel[:, 2, r, :], start=(r == 0), stop=True)
                    for q in range(TILES):
                        mm = pe.matmul(bank[1][:, 3 * NE:4 * NE], cst("ones"), sel[:, 2, q, :], start=(q == 0), stop=(q == TILES - 1))
                    mm.then_inc(rank_made, 1)

                @block.scalar
                def _(act):
                    act.wait_ge(g_centred, 1)
                    act.activation(eg[:, :, :], eg[:, :, :], ACT.Exp).then_inc(g_exp, 1)
                    act.wait_ge(e_centred, 1)
                    act.activation(m[:, 5, :], m[:, 4, :], ACT.Exp).then_inc(e_exp, 1)

                @block.vector
                def _(dve):
                    own = dve_steps.on(dve)
                    L = own.link
                    wide = lambda v, k: v.unsqueeze(2).to_broadcast([P, TILES, k])
                    first = cst("first").unsqueeze(1).to_broadcast([P, TILES, 4])
                    L(dve.memset(blank[:, :, :], 0.0))
                    dve.tensor_scalar(blank[:, :, 2:3].rearrange("p n o -> p (n o)").bitcast(I32),
                                      cst("token")[:, 0:1].to_broadcast([P, 49]), float(2 * TILES * P), None, ALU.add).then_inc(blank_ready, 1)
                    dve.wait_ge(logits_made, 1)
                    L(dve.tensor_copy(lg[:, :, :], bank[0][:, 0:60].rearrange("p (r n) -> p r n", r=TILES)))
                    g = lg[:, :, 0:4]

                    def first_max(values, at_max, dst):
                        L(dve.tensor_tensor(dst, values, wide(at_max, 4), ALU.is_equal))
                        L(dve.tensor_tensor(dst, dst, first, ALU.mult))
                        L(dve.reduce_max(m[:, 7, :], dst, AX))
                        L(dve.tensor_tensor(dst, dst, wide(m[:, 7, :], 4), ALU.is_equal))

                    L(dve.reduce_max(m[:, 0, :], g, AX))
                    dve.tensor_tensor(eg[:, :, :], g, wide(m[:, 0, :], 4), ALU.subtract).then_inc(g_centred, 1)
                    first_max(g, m[:, 0, :], oh[:, 0])
                    dve.wait_ge(g_exp, 1)
                    L(dve.reduce_sum(m[:, 1, :], eg[:, :, :], AX))
                    L(dve.reciprocal(m[:, 1, :], m[:, 1, :]))
                    for r in range(TILES):
                        ins = dve.tensor_tensor(t4[:, r], lg[:, r, 4:20].rearrange("p (g k) -> p k g", g=4),
                                                oh[:, 0, r, :].unsqueeze(1).to_broadcast([P, 4, 4]), ALU.mult)
                    L(ins)
                    L(dve.reduce_sum(fl[:, 0], t4[:, :, :, :], AX))
                    L(dve.reduce_max(m[:, 2, :], fl[:, 0], AX))
                    first_max(fl[:, 0], m[:, 2, :], oh[:, 1])
                    L(dve.scalar_tensor_tensor(out=fl[:, 1], in0=oh[:, 1], scalar=NEG, in1=fl[:, 0], op0=ALU.mult, op1=ALU.add))
                    L(dve.reduce_max(m[:, 3, :], fl[:, 1], AX))
                    first_max(fl[:, 1], m[:, 3, :], oh[:, 2])
                    dve.tensor_tensor(m[:, 4, :], m[:, 3, :], m[:, 2, :], ALU.subtract).then_inc(e_centred, 1)
                    for k in range(2):
                        for r in range(TILES):
                            ins = dve.tensor_tensor(sel[:, k, r].rearrange("p (g j) -> p g j", g=4), oh[:, 0, r, :].unsqueeze(2).to_broadcast([P, 4, 4]),
                                                    oh[:, 1 + k, r, :].unsqueeze(1).to_broadcast([P, 4, 4]), ALU.mult)
                    L(ins)
                    L(dve.tensor_tensor(sel[:, 2], sel[:, 0], sel[:, 1], ALU.add))
                    dve.tensor_tensor(sel[:, 2], sel[:, 2], wide(cst("valid"), NE), ALU.mult).then_inc(sel_ready, 1)
                    dve.wait_ge(e_exp, 1)
                    L(dve.tensor_scalar(m[:, 6, :], m[:, 5, :], 1.0, None, ALU.add))
                    L(dve.reciprocal(m[:, 6, :], m[:, 6, :]))
                    L(dve.tensor_tensor(row[:, :, 0, 1], m[:, 6, :], m[:, 1, :], ALU.mult))
                    L(dve.tensor_tensor(row[:, :, 1, 1], row[:, :, 0, 1], m[:, 5, :], ALU.mult))
                    dve.wait_ge(rank_made, 1)
                    L(dve.tensor_copy(rank[:, :, :], bank[1][:, 0:3 * NE].rearrange("p (r e) -> p r e", r=TILES)))
                    for k in range(2):
                        L(dve.tensor_tensor(t16[:, :, :], rank[:, :, :], sel[:, k], ALU.mult))
                        L(dve.reduce_sum(pos[:, 0, :], t16[:, :, :], AX))
                        L(dve.tensor_tensor(t16[:, :, :], cst("slot0").unsqueeze(1).to_broadcast([P, TILES, NE]), sel[:, k], ALU.mult))
                        L(dve.reduce_sum(pos[:, 1, :], t16[:, :, :], AX))
                        L(dve.tensor_tensor(pos[:, 1, :], pos[:, 1, :], pos[:, 0, :], ALU.add))
                        for n in range(1, TILES):
                            L(dve.tensor_scalar(pos[:, 2, :], pos[:, 0, :], n * P - 0.5, float((NE - 1) * P), ALU.is_gt, ALU.mult))
                            L(dve.tensor_tensor(pos[:, 1, :], pos[:, 1, :], pos[:, 2, :], ALU.add))
                        dve.tensor_copy(pos_i[:, k, :], pos[:, 1, :])
                        dve.tensor_copy(row[:, :, k, 0].bitcast(I32), cst("token"))
                        L(dve.tensor_scalar(row[:, :, k, 2].bitcast(I32), cst("token"), float(k * TILES * P), None, ALU.add))
                        L(dve.memset(row[:, :, k, 3], 0.0))
                    dve.sem_inc(rows_ready, 1)
                    L(dve.reduce_max(cnt[:, 0:1], bank[1][:, 3 * NE:4 * NE], AX))
                    L(dve.tensor_scalar(cnt[:, 1:2], cnt[:, 0:1], P + 0.5, None, ALU.is_gt))
                    L(dve.tensor_scalar(cnt[:, 2:3], cnt[:, 0:1], 2 * P + 0.5, None, ALU.is_gt))
                    L(dve.tensor_tensor(cnt[:, 1:2], cnt[:, 1:2], cnt[:, 2:3], ALU.add))
                    L(dve.tensor_scalar(pairs[0:1, 0:1], cnt[0:1, 1:2], NE / 2.0, NE / 2.0, ALU.mult, ALU.add))

                @block.gpsimd
                def _(pool):
                    pool.wait_ge(blank_ready, 1)
                    pool.dma_start(scratch["slots"].rearrange("(n p) c -> p n c", p=P), blank[:, :, :]).then_inc(blanked, 16)
                    pool.wait_ge(blanked, 16)
                    pool.wait_ge(rows_ready, 1)
                    for k in range(2):
                        for r in range(TILES):
                            rows = P if r < 2 else NS
                            pool.indirect_dma_start(out=scratch["slots"], out_offset=bass.IndirectOffsetOnAxis(ap=pos_i[0:rows, k, r:r + 1], axis=0),
                                                    in_=row[0:rows, r, k, :], in_offset=None).then_inc(slotted, 16)
                    pool.wait_ge(slotted, 16 * 2 * TILES)

        with ExitStack() as scope:
            slot = sb(scope, "slot", [P, 2, 4])
            rows_in = sb(scope, "rows_in", [P, 2, D])
            hT = sb(scope, "hT_e", [P, 2, KC, P])
            gate = sb(scope, "gate", [P, FF])
            act_w = sb(scope, "act_w", [P, FF])
            actT = sb(scope, "actT", [P, 4, P])
            y = sb(scope, "y", [P, D])
            h_turned, h_copied, gu_made, silu_ready, act_ready, a_turned, a_copied, y_made, y_copied_a, y_copied_d, y_stored = (
                sem("e_" + n) for n in ("h_turned", "h_copied", "gu_made", "silu_ready", "act_ready", "a_turned", "a_copied", "y_made",
                                        "y_copied_a", "y_copied_d", "y_stored"))
            slot_loaded = [sem(f"e_slot_loaded{v}") for v in range(2)]
            gathered = [sem(f"e_gathered{v}") for v in range(2)]

            def turns(eng, body):
                n = eng.value_load(pairs[0:1, 0:1], min_val=NE // 2, max_val=TILES * NE // 2)
                with eng.Fori(0, n) as i:
                    for u in range(2):
                        body(i * 2 + u, u, i)

            with nc.Block() as block:
                @block.sync
                def _(sp):
                    n = sp.value_load(pairs[0:1, 0:1], min_val=NE // 2, max_val=TILES * NE // 2)
                    with sp.Fori(1, n * 2) as turn:
                        for used, loads in expert_loads(turn % NE):
                            sp.wait_ge(used, turn)
                            for dst, src, loaded in loads:
                                sp.dma_start(dst, src).then_inc(loaded, 16)

                @block.gpsimd
                def _(pool):
                    def gather(turn, u, i):
                        pool.dma_start(slot[:, u, :], scratch["slots"][bass.ds(turn * P, P)]).then_inc(slot_loaded[u], 16)
                        pool.wait_ge(slot_loaded[u], i * 16 + 16)
                        pool.sem_inc(pool_passed, 1)
                        pool.indirect_dma_start(out=rows_in[:, u, :], out_offset=None, in_=scratch["hn"],
                                                in_offset=bass.IndirectOffsetOnAxis(ap=slot[:, u, 0:1].bitcast(I32), axis=0)).then_inc(gathered[u], 16)

                    gather(0, 0, 0)

                    def step(turn, u, i):
                        pool.wait_ge(y_stored, turn * 16)
                        pool.wait_ge(h_turned, turn * 4)
                        gather(turn + 1, 1 - u, i + u)
                        pool.wait_ge(y_copied_a, turn * 2 + 2)
                        pool.wait_ge(y_copied_d, turn * 2 + 2)
                        pool.sem_inc(pool_passed, 1)
                        pool.indirect_dma_start(out=scratch["moe_y"], out_offset=bass.IndirectOffsetOnAxis(ap=slot[:, u, 2:3].bitcast(I32), axis=0),
                                                in_=y[:, :], in_offset=None, bounds_check=2 * TILES * P - 1, oob_is_err=False).then_inc(y_stored, 16)
                    turns(pool, step)
                    pool.wait_ge(gathered[0], 16)

                @block.tensor
                def _(pe):
                    def turn_rows(turn, u, i):
                        pe.wait_ge(gathered[u], i * 16 + 16)
                        for q in range(4):
                            if q >= 2:
                                pe.wait_ge(h_copied, turn * 4 + q - 1)
                            for k in range(4):
                                mm = pe.transpose(bank[6 + q % 2][:, k * P:k * P + P], rows_in[:, u, 4 * q + k:D:KC], ident)
                            mm.then_inc(h_turned, 1)

                    turn_rows(0, 0, 0)

                    def step(turn, u, i):
                        pe.wait_ge(h_copied, turn * 4 + 4)
                        for q in range(4):
                            pe.wait_ge(gu_loaded[q], turn * 32 + 32)
                            for c in range(4 * q, 4 * q + 4):
                                pe.matmul(bank[4], hT[:, u, c, :], w_g[:, c, :], start=(c == 0), stop=(c == KC - 1))
                                mm = pe.matmul(bank[5], hT[:, u, c, :], w_u[:, c, :], start=(c == 0), stop=(c == KC - 1))
                            mm.then_inc(gu_used[q], 1)
                        turn_rows(turn + 1, 1 - u, i + u)
                        pe.wait_ge(act_ready, turn + 1)
                        pe.wait_ge(h_copied, turn * 4 + 7)
                        for k in range(4):
                            mm = pe.transpose(bank[6][:, k * P:k * P + P], act_w[:, k:FF:4], ident)
                        mm.then_inc(a_turned, 1)
                        pe.wait_ge(a_copied, turn + 1)
                        pe.wait_ge(y_copied_a, turn * 2)
                        pe.wait_ge(y_copied_d, turn * 2)
                        for q in range(4):
                            pe.wait_ge(d_loaded[q], turn * 16 + 16)
                            for n in range(4):
                                mm = pe.matmul(bank[n], actT[:, q, :], w_d[:, q, 512 * n:512 * n + 512], start=(q == 0), stop=(q == 3))
                            mm.then_inc(d_used[q], 1)
                    turns(pe, step)

                @block.scalar
                def _(act):
                    def step(turn, u, i):
                        act.wait_ge(gu_used[3], turn + 1)
                        act.wait_ge(act_ready, turn)
                        act.activation(gate[:, :], bank[4], ACT.Silu).then_inc(silu_ready, 1)
                        act.wait_ge(a_turned, turn + 1)
                        act.copy(actT[:, :, :], bank[6].rearrange("p (k r) -> p k r", k=4)).then_inc(a_copied, 1)
                        act.wait_ge(d_used[3], turn + 1)
                        act.wait_ge(y_stored, turn * 16)
                        for n in range(2):
                            act.copy(y[:, 512 * n:512 * n + 512], bank[n]).then_inc(y_copied_a, 1)
                    turns(act, step)

                @block.vector
                def _(dve):
                    def drain(turn, u):
                        for q in range(4):
                            dve.wait_ge(h_turned, turn * 4 + q + 1)
                            dve.tensor_tensor(hT[:, u, 4 * q:4 * q + 4, :], bank[6 + q % 2].rearrange("p (c r) -> p c r", c=4),
                                              gain_moe[:, 4 * q:4 * q + 4].unsqueeze(2).to_broadcast([P, 4, P]), ALU.mult).then_inc(h_copied, 1)

                    drain(0, 0)

                    def step(turn, u, i):
                        dve.wait_ge(silu_ready, turn + 1)
                        dve.scalar_tensor_tensor(out=act_w[:, :], in0=bank[5], scalar=slot[:, u, 1:2], in1=gate[:, :],
                                                 op0=ALU.mult, op1=ALU.mult).then_inc(act_ready, 1)
                        drain(turn + 1, 1 - u)
                        dve.wait_ge(d_used[3], turn + 1)
                        dve.wait_ge(y_stored, turn * 16)
                        for n in range(2, 4):
                            dve.tensor_copy(y[:, 512 * n:512 * n + 512], bank[n]).then_inc(y_copied_d, 1)
                    turns(dve, step)

        with ExitStack() as scope:
            y2 = sb(scope, "y2", [P, 2, TILES, D])
            gf = sb(scope, "gf", [P, D])
            junk = sb(scope, "f_junk", [P, D])
            ms = sb(scope, "f_ms", [P, TILES])
            gf_loaded, summed, squared, scaled, rooted, ready, stored = (sem("f_" + n) for n in (
                "gf_loaded", "summed", "squared", "scaled", "rooted", "ready", "stored"))
            y_loaded = [sem(f"f_y_loaded{r}") for r in range(TILES)]
            with nc.Block() as block:
                @block.sync
                def _(sp):
                    sp.dma_start(gf[:, :], A["g_final"].partition_broadcast(P)).then_inc(gf_loaded, 16)
                    n = sp.value_load(pairs[0:1, 0:1], min_val=NE // 2, max_val=TILES * NE // 2)
                    sp.wait_ge(y_stored, n * 32)
                    for r in range(TILES):
                        rows = P if r < 2 else NS
                        for k in range(2):
                            a = (k * TILES + r) * P
                            sp.dma_start(y2[0:rows, k, r, :], scratch["moe_y"][a:a + rows]).then_inc(y_loaded[r], 16)
                    for r in range(TILES):
                        sp.wait_ge(ready, r + 1)
                        dst = out["y_p"][0, r * P:(r + 1) * P] if r < 2 else out["y_s"].rearrange("b t n -> (b t) n")
                        sp.dma_start(dst, x[0:(P if r < 2 else NS), r, :]).then_inc(stored, 16)
                    sp.wait_ge(stored, 16 * TILES)
                    sp.wait_ge(window_out, 32)

                @block.vector
                def _(dve):
                    own = dve_steps.on(dve)

                    def add(r):
                        rows = P if r < 2 else NS
                        dve.wait_ge(y_loaded[r], 32)
                        own.link(dve.tensor_tensor(x[0:rows, r, :], x[0:rows, r, :], y2[0:rows, 0, r, :], ALU.add))
                        dve.tensor_tensor(x[0:rows, r, :], x[0:rows, r, :], y2[0:rows, 1, r, :], ALU.add).then_inc(summed, 1)

                    def finish(r):
                        dve.wait_ge(rooted, r + 1)
                        own.link(dve.reciprocal(ms[:, r:r + 1], ms[:, r:r + 1]))
                        if r == 0:
                            dve.wait_ge(gf_loaded, 16)
                        dve.scalar_tensor_tensor(out=x[:, r, :], in0=x[:, r, :], scalar=ms[:, r:r + 1], in1=gf[:, :],
                                                 op0=ALU.mult, op1=ALU.mult).then_inc(ready, 1)

                    for r in range(TILES + 1):
                        if r < TILES:
                            add(r)
                        if r >= 1:
                            finish(r - 1)
                        if r < TILES:
                            dve.wait_ge(squared, r + 1)
                            dve.tensor_scalar(ms[:, r:r + 1], ms[:, r:r + 1], 1.0 / D, EPS, ALU.mult, ALU.add).then_inc(scaled, 1)

                @block.scalar
                def _(act):
                    for r in range(TILES):
                        act.wait_ge(summed, r + 1)
                        if r:
                            act.wait_ge(squared, r)
                        act.activation(junk[:, :], x[:, r, :], ACT.Square, accum_out=ms[:, r:r + 1]).then_inc(squared, 1)
                        act.wait_ge(scaled, r + 1)
                        act.activation(ms[:, r:r + 1], ms[:, r:r + 1], ACT.Sqrt).then_inc(rooted, 1)

_OUTS = [("y_p", (1, SEQ, D)), ("y_s", (NB, NT, D))] \
    + [(k + "_p", (1, 1, SEQ, NG, HD)) for k in ("cmp_k", "cmp_v", "sel_k", "sel_v", "win_k", "win_v")] \
    + [(k + "_p", (1, 1, NMEM, MH, MD)) for k in ("mem_k", "mem_v")] \
    + [(k + "_s", (1, NB, NT, NG, HD)) for k in ("cmp_k", "cmp_v", "sel_k", "sel_v")] \
    + [(k + "_s", (1, NB, WIN, NG, HD)) for k in ("win_k", "win_v")] + [("sgu_v_s", (1, NB, NT, SW))]
_SCRATCH = {"gates": (NS, 48), "hn": (SEQ + NS, D), "slots": ((3 * NE + 1) * P, 4), "moe_y": (2 * TILES * P, D)}


def kernel(**inputs):
    import numpy as _np
    import concourse.bacc as _bacc
    from concourse import mybir as _mybir
    from concourse.bass_utils import run_bass_kernel_spmd as _run

    nc = _bacc.Bacc("TRN2", target_bir_lowering=False, num_devices=1)
    const, const_at = shape_constants()
    arrays, args = {}, {}
    for name, value in list(inputs.items()) + [("const", const)]:
        a = _np.ascontiguousarray(value)
        arrays[f"in_{name}"] = a
        args[name] = nc.dram_tensor(f"in_{name}", a.shape, _mybir.dt.from_np(a.dtype), kind="ExternalInput").ap()
    out = {n: nc.dram_tensor(f"out_{n}", shape, F32, kind="ExternalOutput").ap() for n, shape in _OUTS}
    scratch = {n: nc.dram_tensor(f"scratch_{n}", shape, F32, kind="Internal").ap() for n, shape in _SCRATCH.items()}
    trunk(nc, args, out, scratch, const_at)
    r = _run(nc, [arrays], core_ids=[0])
    return tuple(r.results[0][f"out_{n}"] for n, _ in _OUTS)
```
